# Optimizing a Trainium2 kernel written in Bass

```python
import math
import jax, jax.numpy as jnp
from jax import lax
import numpy as np

D_MODEL = 1024
BATCH = 1
SEQ = 256
DEPTH = 2

CHUNK = 64
N_MIXERS = 4
N_A = len(range(0, DEPTH, N_MIXERS))
N_B = len(range(1, DEPTH, N_MIXERS))
N_C = len(range(2, DEPTH, N_MIXERS))
N_D = len(range(3, DEPTH, N_MIXERS))
EPS = 1e-6
Q_BLOCK = 128

MLA_HEADS = 16
MLA_NOPE = 64
MLA_ROPE = 32
MLA_QK = MLA_NOPE + MLA_ROPE
MLA_V = 64
MLA_Q_RANK = 384
MLA_KV_RANK = 256
ROPE_BASE = 10000.0

ML_HEADS = 4
ML_QK = D_MODEL // 8
ML_V = D_MODEL // 4
GATE_CAP = 15.0

GLA_HEADS = 4
GLA_K = D_MODEL // 8
GLA_V = D_MODEL // 4
GLA_GATE_RANK = 16
GLA_TAU = 16.0

CONV_WIDTH = 31

D_FF = 4 * D_MODEL


def rms_norm(x, g):
    xf = x.astype(jnp.float32)
    y = xf * lax.rsqrt(jnp.mean(xf * xf, axis=-1, keepdims=True) + EPS)
    return (y * g.astype(jnp.float32)).astype(x.dtype)

def layer_norm(x, g, b):
    xf = x.astype(jnp.float32)
    mu = jnp.mean(xf, axis=-1, keepdims=True)
    var = jnp.mean(jnp.square(xf - mu), axis=-1, keepdims=True)
    y = (xf - mu) * lax.rsqrt(var + EPS) * g.astype(jnp.float32) + b.astype(jnp.float32)
    return y.astype(x.dtype)

def apply_rope(x, pos):
    half = x.shape[-1] // 2
    inv_freq = ROPE_BASE ** (-jnp.arange(half, dtype=jnp.float32) / half)
    ang = pos.astype(jnp.float32)[:, None] * inv_freq[None, :]
    cos = jnp.cos(ang)[:, None, :]
    sin = jnp.sin(ang)[:, None, :]
    xf = x.astype(jnp.float32)
    x1, x2 = xf[..., :half], xf[..., half:]
    return jnp.concatenate([x1 * cos - x2 * sin, x2 * cos + x1 * sin], axis=-1).astype(x.dtype)

def _to_chunks(t, heads, dh):
    b, s = t.shape[0], t.shape[1]
    return t.astype(jnp.float32).reshape(b, s // CHUNK, CHUNK, heads, dh).transpose(1, 0, 3, 2, 4)

def _from_chunks(o):
    nc, b, h, l, dv = o.shape
    return o.transpose(1, 0, 3, 2, 4).reshape(b, nc * l, h, dv)

def chunk_causal_attention(q, k, v):
    b, s, h, dq = q.shape
    nqb = s // Q_BLOCK
    scale = dq ** -0.5
    key_chunk = jnp.arange(s) // CHUNK
    qb = q.reshape(b, nqb, Q_BLOCK, h, dq).transpose(1, 0, 2, 3, 4)

    def one_block(args):
        qi, bi = args
        q_chunk = (bi * Q_BLOCK + jnp.arange(Q_BLOCK)) // CHUNK
        sc = jnp.einsum('bqhd,bkhd->bhqk', qi, k, preferred_element_type=jnp.float32) * scale
        mask = key_chunk[None, :] <= q_chunk[:, None]
        p = jax.nn.softmax(jnp.where(mask, sc, -jnp.inf), axis=-1)
        return jnp.einsum('bhqk,bkhd->bqhd', p.astype(v.dtype), v)

    o = lax.map(one_block, (qb, jnp.arange(nqb)))
    return o.transpose(1, 0, 2, 3, 4).reshape(b, s, h, v.shape[-1])

def mla_mixer(h, w_dq, q_norm, w_uq, w_dkv, kv_norm, w_ukv, q_gain, k_gain, w_o):
    b, s, _ = h.shape
    pos = jnp.arange(s)
    cq = rms_norm(h @ w_dq, q_norm)
    q = (cq @ w_uq).reshape(b, s, MLA_HEADS, MLA_QK)
    dkv = h @ w_dkv
    ckv = rms_norm(dkv[..., :MLA_KV_RANK], kv_norm)
    k_rope = jnp.broadcast_to(dkv[..., None, MLA_KV_RANK:], (b, s, MLA_HEADS, MLA_ROPE))
    kv = (ckv @ w_ukv).reshape(b, s, MLA_HEADS, MLA_NOPE + MLA_V)
    k = jnp.concatenate([kv[..., :MLA_NOPE], k_rope], axis=-1)
    v = kv[..., MLA_NOPE:]
    q = rms_norm(q, q_gain)
    k = rms_norm(k, k_gain)
    q = jnp.concatenate([q[..., :MLA_NOPE], apply_rope(q[..., MLA_NOPE:], pos)], axis=-1)
    k = jnp.concatenate([k[..., :MLA_NOPE], apply_rope(k[..., MLA_NOPE:], pos)], axis=-1)
    o = chunk_causal_attention(q, k, v)
    return o.reshape(b, s, MLA_HEADS * MLA_V) @ w_o

def mlstm_mixer(h, w_in, w_if, b_if, head_norm, w_o):
    b, s, _ = h.shape
    hq, hv = ML_HEADS * ML_QK, ML_HEADS * ML_V
    q, k, v, o_pre = jnp.split(h @ w_in, [hq, 2 * hq, 2 * hq + hv], axis=-1)
    gates = (h @ w_if + b_if).astype(jnp.float32)
    gates = GATE_CAP * jnp.tanh(gates / GATE_CAP)
    log_i = _to_chunks(gates[..., :ML_HEADS], ML_HEADS, 1)[..., 0]
    log_f = _to_chunks(jax.nn.log_sigmoid(gates[..., ML_HEADS:]), ML_HEADS, 1)[..., 0]
    q = _to_chunks(q, ML_HEADS, ML_QK)
    k = _to_chunks(k, ML_HEADS, ML_QK) * ML_QK ** -0.5
    v = _to_chunks(v, ML_HEADS, ML_V)
    causal = jnp.tril(jnp.ones((CHUNK, CHUNK), dtype=bool))

    def step(carry, xs):
        c_st, n_st, m_st = carry
        qc, kc, vc, li, lf = xs
        bcum = jnp.cumsum(lf, axis=-1)
        inter = bcum + m_st[..., None]
        dmat = bcum[..., :, None] - bcum[..., None, :] + li[..., None, :]
        dmat = jnp.where(causal, dmat, -jnp.inf)
        m_t = jnp.maximum(inter, jnp.max(dmat, axis=-1))
        w_intra = jnp.exp(dmat - m_t[..., None])
        w_inter = jnp.exp(inter - m_t)
        qk = jnp.einsum('bhtd,bhsd->bhts', qc, kc) * w_intra
        num = jnp.einsum('bhts,bhsv->bhtv', qk, vc) + w_inter[..., None] * jnp.einsum('bhtd,bhvd->bhtv', qc, c_st)
        den = jnp.sum(qk, axis=-1) + w_inter * jnp.einsum('bhtd,bhd->bht', qc, n_st)
        hc = num / jnp.maximum(jnp.abs(den), jnp.exp(-m_t))[..., None]
        b_last = bcum[..., -1]
        decay_s = b_last[..., None] - bcum + li
        m_new = jnp.maximum(b_last + m_st, jnp.max(decay_s, axis=-1))
        ws = jnp.exp(decay_s - m_new[..., None])
        wc = jnp.exp(b_last + m_st - m_new)
        c_new = wc[..., None, None] * c_st + jnp.einsum('bhs,bhsv,bhsd->bhvd', ws, vc, kc)
        n_new = wc[..., None] * n_st + jnp.einsum('bhs,bhsd->bhd', ws, kc)
        return (c_new, n_new, m_new), hc

    init = (jnp.zeros((b, ML_HEADS, ML_V, ML_QK), jnp.float32),
            jnp.zeros((b, ML_HEADS, ML_QK), jnp.float32),
            jnp.zeros((b, ML_HEADS), jnp.float32))
    _, hs = lax.scan(step, init, (q, k, v, log_i, log_f))
    hs = rms_norm(_from_chunks(hs), head_norm.reshape(ML_HEADS, ML_V)).reshape(b, s, hv)
    out = jax.nn.sigmoid(o_pre.astype(jnp.float32)) * hs
    return out.astype(h.dtype) @ w_o

def gla_mixer(h, w_in, w_a1, w_a2, b_a, head_norm, w_o):
    b, s, _ = h.shape
    hk, hv = GLA_HEADS * GLA_K, GLA_HEADS * GLA_V
    q, k, v, r = jnp.split(h @ w_in, [hk, 2 * hk, 2 * hk + hv], axis=-1)
    log_a = jax.nn.log_sigmoid(((h @ w_a1) @ w_a2 + b_a).astype(jnp.float32)) / GLA_TAU
    q = _to_chunks(q, GLA_HEADS, GLA_K) * GLA_K ** -0.5
    k = _to_chunks(k, GLA_HEADS, GLA_K)
    v = _to_chunks(v, GLA_HEADS, GLA_V)
    log_a = _to_chunks(log_a, GLA_HEADS, GLA_K)
    causal = jnp.tril(jnp.ones((CHUNK, CHUNK), dtype=bool))

    def step(state, xs):
        qc, kc, vc, la = xs
        bcum = jnp.cumsum(la, axis=-2)
        diff = jnp.where(causal[:, :, None], bcum[..., :, None, :] - bcum[..., None, :, :], -jnp.inf)
        att = jnp.einsum('bhtk,bhtsk,bhsk->bhts', qc, jnp.exp(diff), kc)
        out = jnp.einsum('bhts,bhsv->bhtv', att, vc) + jnp.einsum('bhtk,bhkv->bhtv', qc * jnp.exp(bcum), state)
        b_last = bcum[..., -1:, :]
        new_state = (jnp.exp(b_last[..., 0, :])[..., None] * state
                     + jnp.einsum('bhsk,bhsv->bhkv', kc * jnp.exp(b_last - bcum), vc))
        return new_state, out

    init = jnp.zeros((b, GLA_HEADS, GLA_K, GLA_V), jnp.float32)
    _, o = lax.scan(step, init, (q, k, v, log_a))
    o = rms_norm(_from_chunks(o), head_norm.reshape(GLA_HEADS, GLA_V)).reshape(b, s, hv)
    o = o * jax.nn.silu(r.astype(jnp.float32))
    return o.astype(h.dtype) @ w_o

def conv_mixer(h, w_pw1, b_pw1, w_dw, b_dw, ln_g, ln_b, w_pw2, b_pw2):
    a, g = jnp.split(h @ w_pw1 + b_pw1, 2, axis=-1)
    u = a * jax.nn.sigmoid(g)
    u = lax.conv_general_dilated(u, w_dw[:, None, :].astype(u.dtype), window_strides=(1,),
                                 padding=[(CONV_WIDTH - 1, 0)],
                                 dimension_numbers=('NWC', 'WIO', 'NWC'),
                                 feature_group_count=D_MODEL) + b_dw
    u = jax.nn.silu(layer_norm(u, ln_g, ln_b))
    return u @ w_pw2 + b_pw2

def sqrelu_mlp(h, w1, w2):
    return jnp.square(jax.nn.relu(h @ w1)) @ w2

def _w(key, shape, fan_in):
    return jax.random.normal(key, shape, jnp.float32) * (fan_in ** -0.5)

def _gain(key, shape):
    return 1.0 + 0.02 * jax.random.normal(key, shape, jnp.float32)

def _bias(key, shape):
    return 0.02 * jax.random.normal(key, shape, jnp.float32)

def first_inputs(seed: int = 0) -> dict:
    key = jax.random.key(seed)
    ks = list(jax.random.split(key, 40))
    D = D_MODEL
    x = jax.random.normal(ks[0], (BATCH, SEQ, D), jnp.float32)
    norm_mix = _gain(ks[1], (DEPTH, D))
    norm_ffn = _gain(ks[2], (DEPTH, D))
    mla_w_dq = _w(ks[3], (N_A, D, MLA_Q_RANK), D)
    mla_q_norm = _gain(ks[4], (N_A, MLA_Q_RANK))
    mla_w_uq = _w(ks[5], (N_A, MLA_Q_RANK, MLA_HEADS * MLA_QK), MLA_Q_RANK)
    mla_w_dkv = _w(ks[6], (N_A, D, MLA_KV_RANK + MLA_ROPE), D)
    mla_kv_norm = _gain(ks[7], (N_A, MLA_KV_RANK))
    mla_w_ukv = _w(ks[8], (N_A, MLA_KV_RANK, MLA_HEADS * (MLA_NOPE + MLA_V)), MLA_KV_RANK)
    mla_q_gain = _gain(ks[9], (N_A, MLA_QK))
    mla_k_gain = _gain(ks[10], (N_A, MLA_QK))
    mla_w_o = _w(ks[11], (N_A, MLA_HEADS * MLA_V, D), MLA_HEADS * MLA_V)
    mlstm_w_in = _w(ks[12], (N_B, D, 2 * ML_HEADS * ML_QK + 2 * ML_HEADS * ML_V), D)
    mlstm_w_if = _w(ks[13], (N_B, D, 2 * ML_HEADS), D)
    mlstm_b_if = jnp.concatenate([_bias(ks[14], (N_B, ML_HEADS)),
                                  3.0 + 0.5 * jax.random.normal(ks[15], (N_B, ML_HEADS), jnp.float32)], axis=-1)
    mlstm_head_norm = _gain(ks[16], (N_B, ML_HEADS * ML_V))
    mlstm_w_o = _w(ks[17], (N_B, ML_HEADS * ML_V, D), ML_HEADS * ML_V)
    gla_w_in = _w(ks[18], (N_C, D, 2 * GLA_HEADS * GLA_K + 2 * GLA_HEADS * GLA_V), D)
    gla_w_a1 = _w(ks[19], (N_C, D, GLA_GATE_RANK), D)
    gla_w_a2 = _w(ks[20], (N_C, GLA_GATE_RANK, GLA_HEADS * GLA_K), GLA_GATE_RANK)
    gla_b_a = _bias(ks[21], (N_C, GLA_HEADS * GLA_K))
    gla_head_norm = _gain(ks[22], (N_C, GLA_HEADS * GLA_V))
    gla_w_o = _w(ks[23], (N_C, GLA_HEADS * GLA_V, D), GLA_HEADS * GLA_V)
    conv_w_pw1 = _w(ks[24], (N_D, D, 2 * D), D)
    conv_b_pw1 = _bias(ks[25], (N_D, 2 * D))
    conv_w_dw = _w(ks[26], (N_D, CONV_WIDTH, D), CONV_WIDTH)
    conv_b_dw = _bias(ks[27], (N_D, D))
    conv_ln_g = _gain(ks[28], (N_D, D))
    conv_ln_b = _bias(ks[29], (N_D, D))
    conv_w_pw2 = _w(ks[30], (N_D, D, D), D)
    conv_b_pw2 = _bias(ks[31], (N_D, D))
    ffn_w1 = _w(ks[32], (DEPTH, D, D_FF), D)
    ffn_w2 = _w(ks[33], (DEPTH, D_FF, D), D_FF)
    return {'x': x, 'norm_mix': norm_mix, 'norm_ffn': norm_ffn,
            'mla_w_dq': mla_w_dq, 'mla_q_norm': mla_q_norm, 'mla_w_uq': mla_w_uq,
            'mla_w_dkv': mla_w_dkv, 'mla_kv_norm': mla_kv_norm, 'mla_w_ukv': mla_w_ukv,
            'mla_q_gain': mla_q_gain, 'mla_k_gain': mla_k_gain, 'mla_w_o': mla_w_o,
            'mlstm_w_in': mlstm_w_in, 'mlstm_w_if': mlstm_w_if, 'mlstm_b_if': mlstm_b_if,
            'mlstm_head_norm': mlstm_head_norm, 'mlstm_w_o': mlstm_w_o,
            'gla_w_in': gla_w_in, 'gla_w_a1': gla_w_a1, 'gla_w_a2': gla_w_a2, 'gla_b_a': gla_b_a,
            'gla_head_norm': gla_head_norm, 'gla_w_o': gla_w_o,
            'conv_w_pw1': conv_w_pw1, 'conv_b_pw1': conv_b_pw1, 'conv_w_dw': conv_w_dw,
            'conv_b_dw': conv_b_dw, 'conv_ln_g': conv_ln_g, 'conv_ln_b': conv_ln_b,
            'conv_w_pw2': conv_w_pw2, 'conv_b_pw2': conv_b_pw2,
            'ffn_w1': ffn_w1, 'ffn_w2': ffn_w2}

def first_block(x, norm_mix, norm_ffn,
              mla_w_dq, mla_q_norm, mla_w_uq, mla_w_dkv, mla_kv_norm, mla_w_ukv,
              mla_q_gain, mla_k_gain, mla_w_o,
              mlstm_w_in, mlstm_w_if, mlstm_b_if, mlstm_head_norm, mlstm_w_o,
              gla_w_in, gla_w_a1, gla_w_a2, gla_b_a, gla_head_norm, gla_w_o,
              conv_w_pw1, conv_b_pw1, conv_w_dw, conv_b_dw, conv_ln_g, conv_ln_b,
              conv_w_pw2, conv_b_pw2,
              ffn_w1, ffn_w2):
    for i in range(DEPTH):
        kind = i % N_MIXERS
        j = i // N_MIXERS
        hn = rms_norm(x, norm_mix[i])
        if kind == 0:
            y = mla_mixer(hn, mla_w_dq[j], mla_q_norm[j], mla_w_uq[j], mla_w_dkv[j], mla_kv_norm[j],
                          mla_w_ukv[j], mla_q_gain[j], mla_k_gain[j], mla_w_o[j])
        elif kind == 1:
            y = mlstm_mixer(hn, mlstm_w_in[j], mlstm_w_if[j], mlstm_b_if[j], mlstm_head_norm[j], mlstm_w_o[j])
        elif kind == 2:
            y = gla_mixer(hn, gla_w_in[j], gla_w_a1[j], gla_w_a2[j], gla_b_a[j], gla_head_norm[j], gla_w_o[j])
        else:
            y = conv_mixer(hn, conv_w_pw1[j], conv_b_pw1[j], conv_w_dw[j], conv_b_dw[j],
                           conv_ln_g[j], conv_ln_b[j], conv_w_pw2[j], conv_b_pw2[j])
        x = x + y.astype(x.dtype)
        x = x + sqrelu_mlp(rms_norm(x, norm_ffn[i]), ffn_w1[i], ffn_w2[i]).astype(x.dtype)
    return x


N_A_LAYERS = DEPTH // 2
N_B_LAYERS = DEPTH - N_A_LAYERS
D_FF_2 = 2816
CONV_WIDTH_2 = 3
N_HEADS = 16
N_KV_GROUPS = 4
HEADS_PER_GROUP = N_HEADS // N_KV_GROUPS
HEAD_DIM = D_MODEL // N_HEADS
N_BRANCH = 3
CMP_BLOCK = 32
CMP_STRIDE = 16
CMP_HIDDEN = 2 * HEAD_DIM
SLC_BLOCK = 64
N_SELECT = 16
WINDOW = 512
N_BUCKETS = 32
MAX_EXACT = N_BUCKETS // 2
MAX_DISTANCE = 4096
NEG = -1e30
BIG = 1e30


def rmsnorm(x, g):
    xf = x.astype(jnp.float32)
    y = xf * lax.rsqrt(jnp.mean(xf * xf, axis=-1, keepdims=True) + EPS)
    return (y * g.astype(jnp.float32)).astype(x.dtype)

def swiglu_ffn(x, w_in, w_out):
    gate, up = jnp.split(x @ w_in, 2, axis=-1)
    return (jax.nn.silu(gate) * up) @ w_out

def rel_bucket(rel):
    n = jnp.maximum(rel, 0)
    nf = jnp.maximum(n, 1).astype(jnp.float32)
    large = MAX_EXACT + (jnp.log(nf / MAX_EXACT) / math.log(MAX_DISTANCE / MAX_EXACT)
                         * (N_BUCKETS - MAX_EXACT)).astype(jnp.int32)
    large = jnp.minimum(large, N_BUCKETS - 1)
    return jnp.where(n < MAX_EXACT, n, large)

def short_conv_mixer(x, w_in, conv_w, w_out):
    b_gate, c_gate, v = jnp.split(x @ w_in, 3, axis=-1)
    u = c_gate * v
    y = lax.conv_general_dilated(u, conv_w[:, None, :], window_strides=(1,),
                                 padding=[(CONV_WIDTH_2 - 1, 0)],
                                 dimension_numbers=('NWC', 'WIO', 'NWC'),
                                 feature_group_count=D_MODEL)
    return (b_gate * y) @ w_out

def compress(raw, pe, w1, w2):
    bsz, s = raw.shape[0], raw.shape[1]
    nc = (s - CMP_BLOCK) // CMP_STRIDE + 1
    idx = jnp.arange(nc)[:, None] * CMP_STRIDE + jnp.arange(CMP_BLOCK)[None, :]
    blk = raw[:, idx] + pe[None, None, :, None, :]
    blk = blk.transpose(0, 3, 1, 2, 4).reshape(bsz, N_KV_GROUPS, nc, CMP_BLOCK * HEAD_DIM)
    return jax.nn.gelu(blk @ w1) @ w2

def shared_kv(h, kv_norm, w_kv, k_norm, pe_k, pe_v, w1_k, w2_k, w1_v, w2_v):
    bsz, s, _ = h.shape
    kv = (rmsnorm(h, kv_norm) @ w_kv).reshape(bsz, s, N_BRANCH, 2, N_KV_GROUPS, HEAD_DIM)
    k_c = rmsnorm(compress(kv[:, :, 0, 0], pe_k, w1_k, w2_k), k_norm[0])
    v_c = compress(kv[:, :, 0, 1], pe_v, w1_v, w2_v)
    ns = s // SLC_BLOCK
    k_s = rmsnorm(kv[:, :, 1, 0], k_norm[1]).transpose(0, 2, 1, 3).reshape(bsz, N_KV_GROUPS, ns, SLC_BLOCK, HEAD_DIM)
    v_s = kv[:, :, 1, 1].transpose(0, 2, 1, 3).reshape(bsz, N_KV_GROUPS, ns, SLC_BLOCK, HEAD_DIM)
    pad = ((0, 0), (0, 0), (WINDOW, 0), (0, 0))
    k_w = jnp.pad(rmsnorm(kv[:, :, 2, 0], k_norm[2]).transpose(0, 2, 1, 3), pad)
    v_w = jnp.pad(kv[:, :, 2, 1].transpose(0, 2, 1, 3), pad)
    return k_c, v_c, k_s, v_s, k_w, v_w

def masked_softmax(s, mask):
    return jax.nn.softmax(jnp.where(mask, s.astype(jnp.float32), NEG), axis=-1)

def nsa_mixer(x, w_q, q_norm, w_o, rel_bias, kv):
    k_c, v_c, k_s, v_s, k_w, v_w = kv
    bsz, s, _ = x.shape
    G, HG, dh = N_KV_GROUPS, HEADS_PER_GROUP, HEAD_DIM
    proj = x @ w_q
    q = rmsnorm(proj[..., :N_HEADS * dh].reshape(bsz, s, G, HG, dh), q_norm)
    q = q.transpose(0, 2, 3, 1, 4)
    gates = jax.nn.sigmoid(proj[..., N_HEADS * dh:].astype(jnp.float32))
    gates = gates.reshape(bsz, s, G, HG, N_BRANCH).transpose(0, 2, 3, 1, 4).astype(x.dtype)
    nc, ns = k_c.shape[2], k_s.shape[2]
    n_sel = min(N_SELECT, ns)
    scale = HEAD_DIM ** -0.5
    c_start = jnp.arange(nc) * CMP_STRIDE
    c_end = c_start + CMP_BLOCK - 1
    s_start = jnp.arange(ns) * SLC_BLOCK
    overlap = (jnp.clip(jnp.minimum(c_start[:, None] + CMP_BLOCK, s_start[None, :] + SLC_BLOCK)
                        - jnp.maximum(c_start[:, None], s_start[None, :]), 0) / CMP_STRIDE).astype(jnp.float32)
    bias_grp = rel_bias.reshape(N_BUCKETS, G, HG).transpose(1, 0, 2)
    bi = jnp.arange(bsz)[:, None, None, None]
    gi = jnp.arange(G)[None, :, None, None]
    blk_ids = jnp.arange(ns)

    def head_bias(rel):
        return rel_bias[rel_bucket(rel)].reshape(rel.shape + (G, HG)).transpose(2, 3, 0, 1)

    def block(qb):
        q0 = qb * Q_BLOCK
        qblk = lax.dynamic_slice_in_dim(q, q0, Q_BLOCK, axis=3)
        gblk = lax.dynamic_slice_in_dim(gates, q0, Q_BLOCK, axis=3)
        t = q0 + jnp.arange(Q_BLOCK)
        rel_c = t[:, None] - c_end[None, :]
        s_c = jnp.einsum('bghqd,bgnd->bghqn', qblk, k_c) * scale + head_bias(rel_c)
        p_c = masked_softmax(s_c, rel_c >= 0)
        p_c = jnp.where((t >= CMP_BLOCK - 1)[:, None], p_c, 0.0)
        o_c = jnp.einsum('bghqn,bgnd->bghqd', p_c.astype(v_c.dtype), v_c)
        imp = jnp.einsum('bghqn,nj->bgqj', p_c, overlap)
        blk_t = t // SLC_BLOCK
        valid = blk_ids[None, :] <= blk_t[:, None]
        forced = ((blk_ids[None, :] == 0) | (blk_ids[None, :] == blk_t[:, None])
                  | (blk_ids[None, :] == blk_t[:, None] - 1))
        score = jnp.where(valid, jnp.where(forced, BIG, imp), NEG)
        _, idx = lax.top_k(score, n_sel)
        k_sel = k_s[bi, gi, idx].reshape(bsz, G, Q_BLOCK, n_sel * SLC_BLOCK, dh)
        v_sel = v_s[bi, gi, idx].reshape(bsz, G, Q_BLOCK, n_sel * SLC_BLOCK, dh)
        pos = (idx[..., None] * SLC_BLOCK + jnp.arange(SLC_BLOCK)).reshape(bsz, G, Q_BLOCK, n_sel * SLC_BLOCK)
        rel_s = t[None, None, :, None] - pos
        bias_s = bias_grp[gi, rel_bucket(rel_s)].transpose(0, 1, 4, 2, 3)
        s_s = jnp.einsum('bghqd,bgqkd->bghqk', qblk, k_sel) * scale + bias_s
        p_s = masked_softmax(s_s, (rel_s >= 0)[:, :, None])
        o_s = jnp.einsum('bghqk,bgqkd->bghqd', p_s.astype(v_sel.dtype), v_sel)
        k_wb = lax.dynamic_slice_in_dim(k_w, q0, Q_BLOCK + WINDOW, axis=2)
        v_wb = lax.dynamic_slice_in_dim(v_w, q0, Q_BLOCK + WINDOW, axis=2)
        s_pos = q0 - WINDOW + jnp.arange(Q_BLOCK + WINDOW)
        rel_w = t[:, None] - s_pos[None, :]
        mask_w = (rel_w >= 0) & (rel_w < WINDOW) & (s_pos >= 0)[None, :]
        s_w = jnp.einsum('bghqd,bgkd->bghqk', qblk, k_wb) * scale + head_bias(rel_w)
        p_w = masked_softmax(s_w, mask_w)
        o_w = jnp.einsum('bghqk,bgkd->bghqd', p_w.astype(v_wb.dtype), v_wb)
        return gblk[..., 0:1] * o_c + gblk[..., 1:2] * o_s + gblk[..., 2:3] * o_w

    out = lax.map(block, jnp.arange(s // Q_BLOCK))
    out = out.transpose(1, 0, 4, 2, 3, 5).reshape(bsz, s, N_HEADS * dh)
    return out @ w_o

def second_inputs(seed: int = 0) -> dict:
    key = jax.random.key(seed)
    ks = jax.random.split(key, 32)

    def w(k, shape, fan_in):
        return jax.random.normal(k, shape, jnp.float32) * (fan_in ** -0.5)

    def gain(k, shape):
        return 1.0 + 0.02 * jax.random.normal(k, shape, jnp.float32)

    q_cols = N_HEADS * HEAD_DIM + N_BRANCH * N_HEADS
    kv_cols = N_BRANCH * 2 * N_KV_GROUPS * HEAD_DIM
    return {
        'x': jax.random.normal(ks[0], (BATCH, SEQ, D_MODEL), jnp.float32),
        'ffn1_norm': gain(ks[1], (DEPTH, D_MODEL)),
        'ffn1_w_in': w(ks[2], (DEPTH, D_MODEL, 2 * D_FF_2), D_MODEL),
        'ffn1_w_out': w(ks[3], (DEPTH, D_FF_2, D_MODEL), D_FF_2),
        'mix_norm': gain(ks[4], (DEPTH, D_MODEL)),
        'ffn2_norm': gain(ks[5], (DEPTH, D_MODEL)),
        'ffn2_w_in': w(ks[6], (DEPTH, D_MODEL, 2 * D_FF_2), D_MODEL),
        'ffn2_w_out': w(ks[7], (DEPTH, D_FF_2, D_MODEL), D_FF_2),
        'conv_w_in': w(ks[8], (N_A_LAYERS, D_MODEL, 3 * D_MODEL), D_MODEL),
        'conv_w': w(ks[9], (N_A_LAYERS, CONV_WIDTH_2, D_MODEL), CONV_WIDTH_2),
        'conv_w_out': w(ks[10], (N_A_LAYERS, D_MODEL, D_MODEL), D_MODEL),
        'attn_w_q': w(ks[11], (N_B_LAYERS, D_MODEL, q_cols), D_MODEL),
        'attn_q_norm': gain(ks[12], (N_B_LAYERS, HEAD_DIM)),
        'attn_w_o': w(ks[13], (N_B_LAYERS, N_HEADS * HEAD_DIM, D_MODEL), N_HEADS * HEAD_DIM),
        'kv_norm': gain(ks[14], (D_MODEL,)),
        'w_kv': w(ks[15], (D_MODEL, kv_cols), D_MODEL),
        'k_norm': gain(ks[16], (N_BRANCH, HEAD_DIM)),
        'cmp_pe_k': 0.1 * jax.random.normal(ks[17], (CMP_BLOCK, HEAD_DIM), jnp.float32),
        'cmp_pe_v': 0.1 * jax.random.normal(ks[18], (CMP_BLOCK, HEAD_DIM), jnp.float32),
        'cmp_w1_k': w(ks[19], (CMP_BLOCK * HEAD_DIM, CMP_HIDDEN), CMP_BLOCK * HEAD_DIM),
        'cmp_w2_k': w(ks[20], (CMP_HIDDEN, HEAD_DIM), CMP_HIDDEN),
        'cmp_w1_v': w(ks[21], (CMP_BLOCK * HEAD_DIM, CMP_HIDDEN), CMP_BLOCK * HEAD_DIM),
        'cmp_w2_v': w(ks[22], (CMP_HIDDEN, HEAD_DIM), CMP_HIDDEN),
        'rel_bias': 0.5 * jax.random.normal(ks[23], (N_BUCKETS, N_HEADS), jnp.float32),
    }

def second_block(x, ffn1_norm, ffn1_w_in, ffn1_w_out, mix_norm, ffn2_norm, ffn2_w_in, ffn2_w_out,
              conv_w_in, conv_w, conv_w_out, attn_w_q, attn_q_norm, attn_w_o,
              kv_norm, w_kv, k_norm, cmp_pe_k, cmp_pe_v, cmp_w1_k, cmp_w2_k, cmp_w1_v, cmp_w2_v,
              rel_bias):
    h = x
    kv = None
    for i in range(DEPTH):
        if i == N_A_LAYERS:
            kv = shared_kv(h, kv_norm, w_kv, k_norm, cmp_pe_k, cmp_pe_v,
                           cmp_w1_k, cmp_w2_k, cmp_w1_v, cmp_w2_v)
        h = h + 0.5 * swiglu_ffn(rmsnorm(h, ffn1_norm[i]), ffn1_w_in[i], ffn1_w_out[i])
        hn = rmsnorm(h, mix_norm[i])
        if i < N_A_LAYERS:
            h = h + short_conv_mixer(hn, conv_w_in[i], conv_w[i], conv_w_out[i])
        else:
            j = i - N_A_LAYERS
            h = h + nsa_mixer(hn, attn_w_q[j], attn_q_norm[j], attn_w_o[j], rel_bias, kv)
        h = h + 0.5 * swiglu_ffn(rmsnorm(h, ffn2_norm[i]), ffn2_w_in[i], ffn2_w_out[i])
    return h


def setup_inputs(seed=0):
    out = dict(first_inputs(seed))
    for name, value in second_inputs(seed + 1).items():
        if name != "x":
            out[name + "_2"] = value
    return out


def reference(
    x, norm_mix, norm_ffn, mla_w_dq, mla_q_norm, mla_w_uq, mla_w_dkv, mla_kv_norm, mla_w_ukv,
    mla_q_gain, mla_k_gain, mla_w_o, mlstm_w_in, mlstm_w_if, mlstm_b_if, mlstm_head_norm,
    mlstm_w_o, gla_w_in, gla_w_a1, gla_w_a2, gla_b_a, gla_head_norm, gla_w_o, conv_w_pw1,
    conv_b_pw1, conv_w_dw, conv_b_dw, conv_ln_g, conv_ln_b, conv_w_pw2, conv_b_pw2, ffn_w1,
    ffn_w2, ffn1_norm_2, ffn1_w_in_2, ffn1_w_out_2, mix_norm_2, ffn2_norm_2, ffn2_w_in_2,
    ffn2_w_out_2, conv_w_in_2, conv_w_2, conv_w_out_2, attn_w_q_2, attn_q_norm_2, attn_w_o_2,
    kv_norm_2, w_kv_2, k_norm_2, cmp_pe_k_2, cmp_pe_v_2, cmp_w1_k_2, cmp_w2_k_2, cmp_w1_v_2,
    cmp_w2_v_2, rel_bias_2,
):
    x = first_block(
        x, norm_mix, norm_ffn, mla_w_dq, mla_q_norm, mla_w_uq, mla_w_dkv, mla_kv_norm,
        mla_w_ukv, mla_q_gain, mla_k_gain, mla_w_o, mlstm_w_in, mlstm_w_if, mlstm_b_if,
        mlstm_head_norm, mlstm_w_o, gla_w_in, gla_w_a1, gla_w_a2, gla_b_a, gla_head_norm,
        gla_w_o, conv_w_pw1, conv_b_pw1, conv_w_dw, conv_b_dw, conv_ln_g, conv_ln_b, conv_w_pw2,
        conv_b_pw2, ffn_w1, ffn_w2,
    )
    return second_block(
        x, ffn1_norm_2, ffn1_w_in_2, ffn1_w_out_2, mix_norm_2, ffn2_norm_2, ffn2_w_in_2,
        ffn2_w_out_2, conv_w_in_2, conv_w_2, conv_w_out_2, attn_w_q_2, attn_q_norm_2,
        attn_w_o_2, kv_norm_2, w_kv_2, k_norm_2, cmp_pe_k_2, cmp_pe_v_2, cmp_w1_k_2, cmp_w2_k_2,
        cmp_w1_v_2, cmp_w2_v_2, rel_bias_2,
    )


_drawn_inputs = setup_inputs


def setup_inputs(seed=0):
    import zlib

    import numpy as np

    out = dict(_drawn_inputs(seed))
    spreads = {}
    factors = {'norm_mix': 2.83,
     'mla_q_norm': 8.0,
     'mla_kv_norm': 8.0,
     'mla_q_gain': 8.0,
     'mla_k_gain': 8.0,
     'mlstm_head_norm': 6.938,
     'ffn1_norm_2': 8.0,
     'mix_norm_2': 3.63,
     'ffn2_norm_2': 21.486,
     'attn_q_norm_2': 27.336,
     'kv_norm_2': 26.603,
     'k_norm_2': 23.448,
     'cmp_pe_k_2': 106.845,
     'cmp_pe_v_2': 199.555,
     'rel_bias_2': 29.062}
    for name, (base, spread) in spreads.items():
        noise = np.random.default_rng([zlib.crc32(name.encode()), seed]).standard_normal(out[name].shape)
        drawn = base * np.exp(spread * noise) if base else spread * noise
        out[name] = __import__('jax').numpy.asarray(drawn.astype(out[name].dtype))
    for name, factor in factors.items():
        out[name] = (out[name] * factor).astype(out[name].dtype)
    return out
```

```python
from contextlib import ExitStack

import numpy as np

import concourse.bass as bass
from concourse import mybir

F32 = mybir.dt.float32
F32R = mybir.dt.float32r
ACT = mybir.ActivationFunctionType
ALU = mybir.AluOpType
AX_X = mybir.AxisListType.X

P = 128
S = 256
TB = S // P
D = 1024
KD = D // P
BLK = 8
TILE = BLK * P
RING = 4
BANK = 512
EPS = 1e-6
NEG = -1e30

Q_RANK, KV_RANK = 384, 256
H, NOPE, ROPE, VD = 16, 64, 32, 64
QK = NOPE + ROPE
HALF = ROPE // 2
KQ, KKV = Q_RANK // P, KV_RANK // P

MH, MQK, MV = 4, 128, 256
GATE_CAP = 15.0

FF1 = 4096 // P
FF2 = 2816 // P
FF2_TILES = -(-FF2 // BLK)
TAPS = 3

G, HG, DH = 4, 4, 64
NC, CSTRIDE, CBLOCK = 15, 16, 32
NC0 = 7
BUCKETS = 32

STAGES = [
    ("dq", 3, 3), ("dkv", 2, 2), ("kr", 1, 2), ("uq", 5, 6), ("uk", 2, 4), ("uv", 2, 4), ("wo_a", 8, 8),
    ("up_0", 32, 32), ("down_0", 32, 8),
    ("mgate", 2, 2), ("mqk", 8, 8), ("mv", 8, 4), ("mo", 8, 8), ("wo_m", 8, 8),
    ("up_1", 32, 32), ("down_1", 32, 8),
    ("glu_0", 44, 44), ("out_0", 24, 8), ("cin", 24, 24), ("cout", 8, 8), ("glu_1", 44, 44), ("out_1", 24, 8),
    ("kv", 8, 4), ("kvc", 8, 8), ("glu_2", 44, 44), ("out_2", 24, 8),
    ("ngate", 1, 2), ("nq", 8, 4), ("wo_n", 8, 8), ("glu_3", 44, 44), ("out_3", 24, 8),
]
TILE0, OUT0 = {}, {}
N_TILES = N_OUTS = 0
for _name, _tiles, _outs in STAGES:
    TILE0[_name], OUT0[_name] = N_TILES, N_OUTS
    N_TILES, N_OUTS = N_TILES + _tiles, N_OUTS + _outs

VEC = {}
N_VEC = 0
for _name, _n in [("mix_0", 8), ("ffn_0", 8), ("mix_1", 8), ("ffn_1", 8), ("pre_0", 8), ("mid_0", 8), ("post_0", 8),
                  ("kvn", 8), ("pre_1", 8), ("mid_1", 8), ("post_1", 8), ("q_norm", KQ), ("kv_norm", KKV),
                  ("head_norm", 8), ("taps", TAPS * KD), ("kc_norm", 1), ("b_i", 1), ("b_f", 1),
                  ("pe_k", 16), ("pe_v", 16)]:
    VEC[_name] = N_VEC
    N_VEC += _n
ROW = {"q_gain": 0, "k_gain": QK, "nq": 2 * QK, "ks": 2 * QK + DH, "kw": 2 * QK + 2 * DH}
N_ROW = 2 * QK + 3 * DH
COPIES = 16
N_STEPS = 31
CONST = {}
N_CONST = 0
for _name, _n in [("ident", P), ("blockdiag", P), ("causal", P), ("select", MH * P), ("onehot", 2 * S), ("cos", TB * HALF),
                  ("sin", TB * HALF), ("valid", TB), ("chunk_u", P), ("chunk_v", P)]:
    CONST[_name] = N_CONST
    N_CONST += _n


def constants():
    c = np.zeros((P, N_CONST), np.float32)

    def put(name, a):
        c[:a.shape[0], CONST[name]:CONST[name] + a.shape[1]] = a

    put("ident", np.eye(P))
    put("blockdiag", np.kron(np.eye(2), np.ones((DH, DH))))
    put("causal", np.triu(np.ones((P, P))))
    put("select", np.kron(np.eye(MH), np.ones((1, P))))
    rel = S - 1 - np.arange(2 * S)
    n = np.maximum(rel, 0)
    exact, most = BUCKETS // 2, 4096
    nf = np.maximum(n, 1).astype(np.float32)
    large = exact + (np.log(nf / np.float32(exact)) / np.float32(np.log(most / exact))
                     * np.float32(BUCKETS - exact)).astype(np.int32)
    bucket = np.where(n < exact, n, np.minimum(large, BUCKETS - 1))
    hot = np.zeros((BUCKETS + 1, 2 * S))
    hot[bucket, np.arange(2 * S)] = rel >= 0
    hot[BUCKETS] = np.where(rel < 0, NEG, 0.0)
    put("onehot", hot)
    freq = np.float32(10000.0) ** (-np.arange(HALF, dtype=np.float32) / np.float32(HALF))
    ang = (np.arange(S, dtype=np.float32)[:, None] * freq[None, :]).astype(np.float32)
    for name, f in (("cos", np.cos), ("sin", np.sin)):
        put(name, f(ang).reshape(TB, P, HALF).transpose(1, 0, 2).reshape(P, TB * HALF))
    put("valid", (np.arange(S) >= CBLOCK - 1).astype(np.float32).reshape(TB, P).T)
    put("chunk_u", (np.arange(P) < 64)[None, :].astype(np.float32))
    put("chunk_v", np.where(np.arange(P) >= 64, NEG, 0.0)[None, :])
    return c


def build(nc, x_in, tiles, vecs, rows, consts, rel_bias, w1c_k, w1c_v, w2c_k, w2c_v, y_out):
    ctx = ExitStack()
    with ctx:
        def sb(name, shape, dt=F32):
            return ctx.enter_context(nc.sbuf_tensor(name, shape, dt))

        def sem(name):
            return ctx.enter_context(nc.semaphore(name))

        raw = [sb(f"raw{s}", [P, TILE]) for s in range(RING)]
        w_hi = [sb(f"w_hi{s}", [P, TILE], F32R) for s in range(RING)]
        w_lo = [sb(f"w_lo{s}", [P, TILE], F32R) for s in range(RING)]
        x = sb("x", [P, KD * S])
        xs = sb("xs", [P, KD * 2 * S], F32R)
        half = [sb(f"half{s}", [P, S]) for s in range(4)]
        fsum = [sb(f"fsum{s}", [P, S]) for s in range(4)]
        sq = [sb(f"sq{s}", [P, S]) for s in range(4)]
        sil = [sb(f"sil{s}", [P, S]) for s in range(2)]
        vec = sb("vec", [P, N_VEC])
        row = sb("row", [P, N_ROW])
        con = sb("con", [P, N_CONST])
        ones = sb("ones", [P, P])
        zeros = sb("zeros", [P, P])
        eps = sb("eps", [P, 1])
        std = sb("std", [P, 64])
        rstd = sb("rstd", [P, 64])
        diag = sb("diag", [P, 4 * P])
        bias = sb("bias", [P, H * S])
        relb = sb("relb", [BUCKETS + 1, H])
        bias_row = sb("bias_row", [H, 2 * S])
        kT = sb("kT", [P, 4 * S])
        vtok = sb("vtok", [P, TB * 2 * G * DH])
        kcT = sb("kcT", [P, G * NC])
        vc = sb("vc", [NC, G * DH])
        with nc.sbuf_tensor("hs", [P, FF1 * 2 * S], F32R) as hs:
            pass
        arena = sb("arena", [P, FF1 * 2 * S])

        def part(at, n):
            return arena[:, at:at + n]

        psum = ctx.enter_context(nc.psum_tensor("psum", [P, 8 * BANK], F32))

        def bank(b, a=0, z=BANK, p=slice(None)):
            return psum[p, b * BANK + a:b * BANK + z]

        def const(name, a, z, p=slice(None)):
            at = CONST[name]
            return con[p, at + a:at + z]

        ident = const("ident", 0, P)
        STAT, RB = 4, 5

        tile_loaded = [sem(f"tile_loaded{s}") for s in range(RING)]
        hi_ready, lo_ready = sem("hi_ready"), sem("lo_ready")
        tile_done = sem("tile_done")
        out_read = sem("out_read")
        half_ready = sem("half_ready")
        loaded = sem("loaded")
        const_ready = sem("const_ready")
        stat_done, std_ready, diag_ready, rb_ready = sem("stat_done"), sem("std_ready"), sem("diag_ready"), sem("rb_ready")
        sq_ready = sem("sq_ready")
        xn_ready, xhi_ready, xs_ready = sem("xn_ready"), sem("xhi_ready"), sem("xs_ready")
        hid_ready, hhi_ready, hs_ready = sem("hid_ready"), sem("hhi_ready"), sem("hs_ready")
        sil_ready = sem("sil_ready")
        x_half = sem("x_half")
        dve_step = sem("dve_step")
        stored = sem("stored")
        sq_clear = sem("sq_clear")
        row_ready = sem("row_ready")
        bias_done, bias_out, bias_in = sem("bias_done"), sem("bias_out"), sem("bias_in")
        head_sq, head_sum, head_std = sem("head_sq"), sem("head_sum"), sem("head_std")
        a_st, a_turn, a_qkT, a_s, a_max, a_exp = (sem(f"a_{n}") for n in ("st", "turn", "qkT", "s", "max", "exp"))
        a_pT, a_pTs, a_pv, a_o = (sem(f"a_{n}") for n in ("pT", "pTs", "pv", "o"))
        o_turn = {n: sem(f"turn_{n}") for n in ("o_a", "o_n")}
        m_tanh, m_rows, m_floor, m_bcd, m_st, m_logw, m_exp, m_ptd = (
            sem(f"m_{n}") for n in ("tanh", "rows", "floor", "bcd", "st", "logw", "exp", "ptd"))
        m_dend, m_absd, m_num, m_hc, m_sqd, m_ss, m_stdd, m_sig, m_at, m_ac = (
            sem(f"m_{n}") for n in ("dend", "absd", "num", "hc", "sqd", "ss", "stdd", "sig", "at", "ac"))
        c_loaded, c_sqd, c_sum, c_std, c_bias, c_gelu, c_kc, c_kcsqd, c_kcss, c_kcstdd = (
            sem(f"c_{n}") for n in ("loaded", "sqd", "sum", "std", "bias", "gelu", "kc", "kcsqd", "kcss", "kcstdd"))
        c_kn, c_kt, c_kT, c_hd, c_vcd, c_end = (sem(f"c_{n}") for n in ("kn", "kt", "kT", "hd", "vcd", "end"))
        n_sig, n_sqd, n_sum, n_std_, n_st, n_turn, n_qTs, n_cs, n_clog, n_cexp, n_cT, n_cTs, n_cpv, n_co = (
            sem(f"n_{n}") for n in ("sig", "sqd", "sum", "std", "st", "turn", "qTs", "cs", "clog", "cexp", "cT", "cTs", "cpv", "co"))
        n_s, n_lr, n_max, n_exp, n_pT, n_pTd, n_pv, n_od, n_end = (
            sem(f"n_{n}") for n in ("s", "lr", "max", "exp", "pT", "pTd", "pv", "od", "end"))

        half0, hid0, sil0, n_half, n_hid, n_sil = {}, {}, {}, 0, 0, 0
        for name, _, outs in STAGES:
            half0[name], hid0[name], sil0[name] = n_half, n_hid, n_sil
            kind = name.split("_")[0]
            if kind in ("dq", "dkv", "up", "mgate", "mqk", "mo", "glu", "cin", "kvc"):
                n_half += outs
            n_hid += {"up": outs, "glu": outs // 2, "cin": outs // 3}.get(kind, 0)
            n_sil += {"glu": outs // 2}.get(kind, 0)
        RES = [n for n, _, _ in STAGES if n.split("_")[0] in ("wo", "down", "out", "cout")]
        res_no = {n: j for j, n in enumerate(RES)}

        class Steps:

            def __init__(self):
                self.base, self.n = 0, 0

            def mark(self, ins):
                ins.then_inc(dve_step, 1)
                self.n += 1
                return self.base + self.n

        def at(t, start, n):
            return t[:, start:start + n] if isinstance(start, int) else t[:, bass.ds(start, n)]

        def x_chunks():
            return [x[:, k * S:(k + 1) * S] for k in range(KD)]

        cqf = part(0, (KQ + KKV) * S)
        q_tok = part(2048, TB * H * QK)
        k_tok = part(2048 + 3072, TB * H * NOPE)
        v_tok = part(2048 + 5120, TB * H * VD)
        o_tok = part(0, TB * H * VD)
        kr_tok = part(9216, TB * ROPE)
        ss = part(9280, 4 * H + 2)
        rope_t = part(9408, 4 * TB * H * HALF)
        mscr = [part(11456 + 1024 * j, 1024) for j in range(2)]
        HEAD_SQ = [(q_tok[:, j * 768:(j + 1) * 768], 768) for j in range(2 * TB)]
        HEAD_SQ += [(k_tok[:, j * 1024:(j + 1) * 1024], 1024) for j in range(TB)] + [(kr_tok, TB * ROPE)]
        q_st = part(11456, TB * 4 * QK)
        k_st = part(11456 + 768, TB * 4 * QK)
        qkT = [part(12992 + 512 * j, 512) for j in range(2)]
        prob = [part(14016 + 384 * j, 384) for j in range(2)]
        probT = [part(14784 + 384 * j, 384) for j in range(2)]
        mx = part(15552, 16)
        nmx = part(15568, 16)
        rsum = part(15584, 16)
        rinv = part(15600, 16)

        chunk_u = sb("chunk_u", [1, P], F32R)
        chunk_v = sb("chunk_v", [1, P], F32R)
        mla_mask = (chunk_u, chunk_v)
        ASQ = part(2048, KD * S)

        conv_b = [part(KD * 512 + j * S, S) for j in range(2)]
        conv_c = [part(KD * 512 + (2 + j) * S, S) for j in range(2)]
        conv_v = [part(KD * 512 + (4 + j) * S, S) for j in range(2)]
        conv_y = [part(KD * 512 + (6 + j) * S, S) for j in range(2)]
        conv_u = [part(KD * 512 + 8 * S + j * 2 * S, S + TAPS - 1) for j in range(2)]

        m_qk = part(0, 2 * MH * S)
        m_v = part(2048, TB * MH * MV)
        m_o = part(4096, KD * S)
        m_row = [arena[0:MH, 6144 + j * S:6144 + (j + 1) * S] for j in range(6)]
        m_ti, m_tf, m_nb, m_a, m_g, m_one = m_row
        m_bc = arena[0:MH, 7680:7680 + 2 * S]
        m_acol = part(8192, TB * MH)
        m_w = [part(8320 + 384 * j, 384) for j in range(2)]
        m_pt = [part(9088 + 384 * j, 384) for j in range(2)]
        m_den = [part(9856 + S * j, S) for j in range(2)]
        m_fl = [part(10368 + S * j, S) for j in range(2)]
        m_h = [part(10880 + 512 * j, 512) for j in range(2)]
        m_sq = [part(11904 + 512 * j, 512) for j in range(2)]
        m_std = part(12928, S)
        m_r = part(13184, S)

        w1c = [part(16 * P * j, 16 * P) for j in range(2)]
        w2c = [part(4096 + P * j, P) for j in range(2)]
        c_dup = [part(4352 + G * S * j, G * S) for j in range(2)]
        kn_tok = part(6400, TB * 2 * G * DH)
        c_sq = [part(7424 + 512 * j, 512) for j in range(2)]
        c_ss = part(8448, 16)
        c_r = part(8464, 16)
        c_pe = part(8480, 2)
        c_hid = [part(8512 + 64 * j, G * NC) for j in range(2)]
        c_kcsq = part(8640, G * NC)
        c_kcstd = part(8704, G * NC)
        c_kcr = part(8768, G * NC)

        nq_tok = part(0, TB * D)
        no_tok = part(2048, TB * D)
        n_gate = part(4096, TB * 3 * H)
        n_sq = [part(4224 + D * j, D) for j in range(2)]
        n_ss = part(6272, TB * H)
        n_r = part(6304, TB * H)
        n_qs = part(6336, 2 * TB * P)
        n_qT = part(6848, 2 * S)
        n_g = part(7360, 4 * TB * 3)
        n_cl = part(7392, 4 * (NC0 + NC))
        n_cmx = part(7488, 8)
        n_crs = part(7504, 8)
        n_csc = part(7520, 8)
        n_cpT = arena[0:NC, 7552:7552 + 4 * S]
        n_o = part(8576, 2 * S)
        n_l = [part(9088 + 384 * j, 384) for j in range(2)]
        n_p = [part(9856 + 384 * j, 384) for j in range(2)]
        n_pTs = [part(10624 + 384 * j, 384) for j in range(2)]
        n_mx = part(11392, 16)
        n_nmx = part(11408, 16)
        n_rs = part(11424, 16)
        n_sc = part(11440, 16)

        cq_src = [cqf[:, k * S:(k + 1) * S] for k in range(KQ + KKV)]
        NORMS = {}
        for name, gain in [("mix_0", 0), ("cq", 0), ("ffn_0", 0), ("mix_1", 0), ("ffn_1", 0), ("pre_0", 0), ("mid_0", 0),
                           ("post_0", 0), ("kvn", 0), ("pre_1", 0), ("mid_1", 0), ("post_1", 0)]:
            if name == "cq":
                NORMS[name] = [(cq_src[:KQ], VEC["q_norm"], Q_RANK), (cq_src[KQ:], VEC["kv_norm"], KV_RANK)]
            else:
                NORMS[name] = [(x_chunks(), VEC[name], D)]
        STAT0, STD0, n_stat, n_std = {}, {}, 0, 0
        for name, groups in NORMS.items():
            if name != "pre_1":
                n_stat, n_std = n_stat + 1, n_std + len(groups)
            STAT0[name], STD0[name] = n_stat, n_std
        XS0, XN0, n_xs, n_xn = {}, {}, 0, 0
        for name in ["mix_0", "cq", "o_a", "ffn_0", "mix_1", "o_m", "ffn_1", "pre_0", "mid_0", "post_0", "kvn", "pre_1", "mid_1",
                     "o_n", "post_1"]:
            XS0[name], XN0[name] = n_xs, n_xn
            chunks_ = KQ + KKV if name == "cq" else KD
            n_xs, n_xn = n_xs + chunks_, n_xn + (chunks_ if name not in ("o_a", "o_n") else 0)
        SQ0 = {"mix_0": 0, "cq": 1} | {name: 2 + KD * j for j, name in enumerate(RES)}

        def xs_hi(k):
            return xs[:, k * 2 * S:k * 2 * S + S]

        def xs_lo(k):
            return xs[:, k * 2 * S + S:(k + 1) * 2 * S]

        bias_dram = nc.dram_tensor("bias_dram", (H, COPIES, 2 * S), F32, kind="Internal").ap()
        block = ctx.enter_context(nc.Block())

        @block.sync
        def _(sp):
            sp.dma_start(x[:, :].rearrange("p (k t) -> p k t", k=KD), x_in.rearrange("(k p) t -> p k t", p=P)).then_inc(loaded, 16)
            sp.dma_start(vec[:, :], vecs).then_inc(loaded, 16)
            sp.dma_start(con[:, :], consts).then_inc(loaded, 16)
            sp.dma_start(row[:, :], rows.partition_broadcast(P)).then_inc(loaded, 16)
            sp.dma_start(relb[0:BUCKETS, :], rel_bias).then_inc(loaded, 16)
            for s in range(RING):
                sp.dma_start(raw[s][:, :], tiles[s]).then_inc(tile_loaded[s], 16)
            with sp.Fori(1, N_TILES // RING) as i:
                for s in range(RING):
                    sp.wait_ge(lo_ready, i * RING + (s + 1 - RING))
                    sp.dma_start(raw[s][:, :], tiles[bass.ds(i * RING + s, 1)].rearrange("o p n -> p (o n)")).then_inc(tile_loaded[s], 16)
            for t in range(N_TILES // RING * RING, N_TILES):
                s = t % RING
                sp.wait_ge(lo_ready, t + 1 - RING)
                sp.dma_start(raw[s][:, :], tiles[t]).then_inc(tile_loaded[s], 16)
            for k in range(KD):
                sp.wait_ge(out_read, OUT0["out_3"] + k + 1)
                sp.dma_start(y_out[k * P:(k + 1) * P, :], x[:, k * S:(k + 1) * S]).then_inc(stored, 16)
            sp.wait_ge(stored, 16 * KD)
            sp.wait_ge(bias_out, 16)

        @block.gpsimd
        def _(pool):
            pool.memset(ones[:, :], 1.0).then_inc(const_ready, 1)
            pool.memset(zeros[:, :], 0.0).then_inc(const_ready, 1)
            pool.memset(eps[:, :], EPS).then_inc(const_ready, 1)
            pool.wait_ge(const_ready, 3)
            pool.memset(relb[BUCKETS:BUCKETS + 1, :], 1.0).then_inc(const_ready, 1)
            pool.wait_ge(const_ready, 4)

            def take_lo(s, t):
                pool.wait_ge(hi_ready, t + 1)
                pool.tensor_tensor(w_lo[s][:, :], raw[s][:, :], w_hi[s][:, :].bitcast(F32), ALU.subtract).then_inc(lo_ready, 1)

            with pool.Fori(0, N_TILES // RING) as i:
                for s in range(RING):
                    take_lo(s, i * RING + s)
            for t in range(N_TILES // RING * RING, N_TILES):
                take_lo(t % RING, t)

        @block.scalar
        def _(act):
            def split(t, q=0):
                if isinstance(q, int) and t + RING * q >= N_TILES:
                    return
                s = t % RING
                act.wait_ge(tile_loaded[s], (q + (t // RING + 1)) * 16)
                if t >= RING:
                    act.wait_ge(tile_done, q * RING + (t + 1 - RING))
                act.activation(w_hi[s][:, :], raw[s][:, :], ACT.Copy).then_inc(hi_ready, 1)

            def take_half(name, b, o, t, q=0, p=slice(None)):
                act.wait_ge(tile_done, t + 1)
                if not (isinstance(o, int) and OUT0[name] + o < 4):
                    act.wait_ge(out_read, o + (OUT0[name] - 3))
                act.activation(half[b][p, :], bank(b, S, 2 * S, p), ACT.Copy).then_inc(half_ready, 1)

            def norm(name):
                if name != "pre_1":
                    act.wait_ge(stat_done, STAT0[name])
                    for g, (src, _, size) in enumerate(NORMS[name]):
                        act.activation(std[:, TB * g:TB * (g + 1)], bank(STAT, TB * g, TB * (g + 1)), ACT.Sqrt, bias=eps[:, 0:1],
                                       scale=1.0 / size).then_inc(std_ready, 1)
                for k in range(sum(len(src) for src, _, _ in NORMS[name])):
                    act.wait_ge(xn_ready, XN0[name] + k + 1)
                    act.activation(xs_hi(k), fsum[k % 4][:, :], ACT.Copy).then_inc(xhi_ready, 1)

            def plain(name, outs, p=slice(None)):
                for o in range(outs):
                    t = TILE0[name] + o
                    take_half(name, (OUT0[name] + o) % 4, o, t, p=p)
                    split(t + RING)

            def used(name, tiles_):
                for t in range(TILE0[name], TILE0[name] + tiles_):
                    split(t + RING)

            def residual(name, per, outs=KD):
                t0, o0, s0 = TILE0[name], OUT0[name], SQ0[name]
                last = name == RES[-1]

                def four(i):
                    for u in range(4):
                        for j in range(per):
                            split(t0 + u * per + j + RING, i * per)
                        if not last:
                            act.wait_ge(out_read, i * 4 + (o0 + u + 1))
                            act.activation(sq[u][:, :], at(x, i * (4 * S) + u * S, S), ACT.Square).then_inc(sq_ready, 1)
                if last:
                    for i in range(outs // 4):
                        four(i)
                else:
                    with act.Fori(0, outs // 4) as i:
                        four(i)

            def up(name):
                t0, o0 = TILE0[name], OUT0[name]
                with act.Fori(0, FF1 // 4) as i:
                    for u in range(4):
                        take_half(name, (o0 + u) % 4, i * 4 + u, i * 4 + (t0 + u))
                        split(t0 + u + RING, i)
                        act.wait_ge(hid_ready, i * 4 + (hid0[name] + u + 1))
                        act.activation(at(hs, i * (8 * S) + u * 2 * S, S), fsum[(o0 + u) % 4][:, :], ACT.Copy).then_inc(hhi_ready, 1)

            def glu(name):
                t0, o0 = TILE0[name], OUT0[name]
                with act.Fori(0, FF2 // 2) as i:
                    for u in range(4):
                        take_half(name, (o0 + u) % 4, i * 4 + u, i * 4 + (t0 + u))
                        split(t0 + u + RING, i)
                        if u % 2 == 0:
                            act.wait_ge(out_read, i * 4 + (o0 + u + 1))
                            act.activation(sil[u // 2][:, :], fsum[(o0 + u) % 4][:, :], ACT.Silu).then_inc(sil_ready, 1)
                        else:
                            act.wait_ge(hid_ready, i * 2 + (hid0[name] + u // 2 + 1))
                            act.activation(at(hs, i * (4 * S) + (u // 2) * 2 * S, S), fsum[(o0 + u) % 4][:, :],
                                           ACT.Copy).then_inc(hhi_ready, 1)

            def conv():
                name = "cin"
                t0, o0 = TILE0[name], OUT0[name]
                with act.Fori(0, KD // 4) as i:
                    for u in range(12):
                        take_half(name, (o0 + u) % 4, i * 12 + u, i * 12 + (t0 + u))
                        split(t0 + u + RING, i * 3)
                        if u % 3 == 2:
                            m = u // 3
                            act.wait_ge(hid_ready, i * 4 + (hid0[name] + m + 1))
                            act.activation(at(hs, i * (8 * S) + m * 2 * S, S), conv_y[m % 2], ACT.Copy).then_inc(hhi_ready, 1)

            def mla():
                plain("dq", 3)
                plain("dkv", 2)
                used("kr", 1)
                act.wait_ge(out_read, OUT0["dkv"] + 2)
                act.activation(ASQ[:, 0:(KQ + KKV) * S], cqf, ACT.Square).then_inc(sq_ready, 1)
                norm("cq")
                used("uq", 5)
                used("uk", 2)
                used("uv", 2)
                act.wait_ge(out_read, OUT0["uv"] + 4)
                for n, (src, w) in enumerate(HEAD_SQ):
                    if n >= 2:
                        act.wait_ge(head_sum, n - 1)
                    act.activation(mscr[n % 2][:, 0:w], src, ACT.Square).then_inc(head_sq, 1)
                act.wait_ge(head_sum, len(HEAD_SQ) + 1)
                act.activation(std[:, 0:4 * H], ss[:, 0:4 * H], ACT.Sqrt, bias=eps[:, 0:1], scale=1.0 / QK).then_inc(head_std, 1)
                scale = QK ** -0.5
                with act.Fori(0, H // 4) as i:
                    act.wait_ge(a_pv, i * 4)

                    def turned(h):
                        act.wait_ge(a_turn, i * 4 + (h + 1))
                        act.activation(qkT[h % 2][0:QK, :], bank(h % 2, 0, 512, slice(0, QK)), ACT.Copy).then_inc(a_qkT, 1)

                    def exps(h):
                        act.wait_ge(a_max, i * 4 + (h + 1))
                        for tb, (a, z) in enumerate([(0, P), (P, 3 * P)]):
                            ins = act.activation(prob[h % 2][:, a:z], bank(2 + h % 2, a, z), ACT.Exp, scale=scale,
                                                 bias=nmx[:, 2 * h + tb:2 * h + tb + 1],
                                                 accum_out=rsum[:, 2 * h + tb:2 * h + tb + 1])
                            ins.then_inc(a_exp, 1)

                    def probs_turned(h):
                        act.wait_ge(a_pT, i * 4 + (h + 1))
                        if h >= 2:
                            act.wait_ge(a_pv, i * 4 + (h - 1))
                        act.activation(probT[h % 2], bank(4 + h % 2, 0, 384), ACT.Copy).then_inc(a_pTs, 1)

                    turned(0)
                    turned(1)
                    exps(0)
                    turned(2)
                    probs_turned(0)
                    exps(1)
                    turned(3)
                    probs_turned(1)
                    exps(2)
                    probs_turned(2)
                    exps(3)
                    probs_turned(3)
                out_hi("o_a")

            def out_hi(name):
                for k in range(KD):
                    act.wait_ge(o_turn[name], k + 1)
                    act.activation(xs_hi(k), bank(k % 4, 0, S), ACT.Copy).then_inc(xhi_ready, 1)

            def mlstm():
                plain("mgate", 2, p=slice(0, MH))
                plain("mqk", 8)
                used("mv", 8)
                plain("mo", 8)
                act.activation(m_ti, m_ti, ACT.Tanh, scale=1.0 / GATE_CAP).then_inc(m_tanh, 1)
                act.activation(m_tf, m_tf, ACT.Tanh, scale=1.0 / GATE_CAP).then_inc(m_tanh, 1)
                act.wait_ge(m_tanh, 2)
                act.activation(m_nb, m_tf, ACT.Exp, scale=-GATE_CAP).then_inc(m_tanh, 1)
                act.wait_ge(m_tanh, 3)
                act.activation(m_tf, m_nb, ACT.Ln, bias=ones[0:MH, 0:1]).then_inc(m_tanh, 1)
                act.wait_ge(out_read, OUT0["mo"] + 8)
                act.activation(m_o, m_o, ACT.Sigmoid).then_inc(m_sig, 1)
                act.wait_ge(m_rows, 1)
                act.activation(m_bc[:, S:2 * S], m_bc[:, S:2 * S], ACT.Exp).then_inc(m_floor, 1)
                for h in range(MH):
                    act.wait_ge(m_logw, h + 1)
                    act.activation(m_w[h % 2], m_w[h % 2], ACT.Exp).then_inc(m_exp, 1)
                    act.wait_ge(m_dend, h + 1)
                    act.activation(m_den[h % 2], bank(6, 0, S), ACT.Abs).then_inc(m_absd, 1)
                    act.wait_ge(m_hc, h + 1)
                    act.activation(m_sq[h % 2], m_h[h % 2], ACT.Square).then_inc(m_sqd, 1)
                    act.wait_ge(m_ss, h + 1)
                    act.activation(m_std, bank(7, 0, S), ACT.Sqrt, bias=eps[:, 0:1], scale=1.0 / MV).then_inc(m_stdd, 1)
                    for v in range(2):
                        act.wait_ge(xn_ready, XN0["o_m"] + 2 * h + v + 1)
                        act.activation(xs_hi(2 * h + v), m_h[h % 2][:, v * S:(v + 1) * S], ACT.Copy).then_inc(xhi_ready, 1)

            def nsa_kv():
                act.wait_ge(tile_done, TILE0["kv"])
                for j, w in enumerate((w1c_k, w1c_v)):
                    act.dma_start(w1c[j].rearrange("p (c n) -> p c n", n=P), w.rearrange("(c p) n -> p c n", p=P)).then_inc(c_loaded, 16)
                act.dma_start(w2c[0], w2c_k).then_inc(c_loaded, 16)
                act.dma_start(w2c[1], w2c_v).then_inc(c_loaded, 16)
                used("kv", 8)
                plain("kvc", 8)
                act.wait_ge(out_read, OUT0["kv"] + 4)
                for tb in range(TB):
                    act.activation(c_sq[tb], kn_tok[:, tb * 512:(tb + 1) * 512], ACT.Square).then_inc(c_sqd, 1)
                act.wait_ge(c_sum, 2)
                act.activation(std[:, 0:16], c_ss, ACT.Sqrt, bias=eps[:, 0:1], scale=1.0 / DH).then_inc(c_std, 1)
                act.wait_ge(c_bias, 1)
                for j in range(2):
                    act.activation(c_hid[j], bank(j, 0, G * NC), ACT.Gelu_apprx_tanh, bias=c_pe[:, j:j + 1]).then_inc(c_gelu, 1)
                act.wait_ge(c_kc, 1)
                act.activation(c_kcsq, bank(6, 0, G * NC), ACT.Square).then_inc(c_kcsqd, 1)
                act.wait_ge(c_kcss, 1)
                act.activation(c_kcstd, bank(3, 0, G * NC), ACT.Sqrt, bias=eps[:, 0:1], scale=1.0 / DH).then_inc(c_kcstdd, 1)

            def nsa():
                used("ngate", 1)
                used("nq", 8)
                act.wait_ge(out_read, OUT0["ngate"] + 2)
                act.activation(n_gate, n_gate, ACT.Sigmoid).then_inc(n_sig, 1)
                act.wait_ge(out_read, OUT0["nq"] + 4)
                for tb in range(TB):
                    act.activation(n_sq[tb], nq_tok[:, tb * D:(tb + 1) * D], ACT.Square).then_inc(n_sqd, 1)
                act.wait_ge(n_sum, 2)
                act.activation(std[:, 0:TB * H], n_ss, ACT.Sqrt, bias=eps[:, 0:1], scale=1.0 / DH).then_inc(n_std_, 1)
                with act.Fori(0, HG) as i:
                    act.wait_ge(n_turn, i + 1)
                    act.wait_ge(n_pv, i * 8)
                    act.activation(n_qT, bank(0), ACT.Copy).then_inc(n_qTs, 1)
                    act.wait_ge(n_clog, i + 1)
                    act.activation(n_cl, n_cl, ACT.Exp).then_inc(n_cexp, 1)
                    act.wait_ge(n_cT, i + 1)
                    for b in range(2):
                        act.activation(n_cpT[:, b * 512:(b + 1) * 512], bank(4 + b, 0, 512, slice(0, NC)), ACT.Copy).then_inc(n_cTs, 1)

                    def exps(u):
                        act.wait_ge(n_max, i * 8 + (u + 1))
                        for tb, (a, z) in enumerate([(0, P), (P, 3 * P)]):
                            act.activation(n_p[u % 2][:, a:z], n_l[u % 2][:, a:z], ACT.Exp,
                                           bias=n_nmx[:, 2 * u + tb:2 * u + tb + 1],
                                           accum_out=n_rs[:, 2 * u + tb:2 * u + tb + 1]).then_inc(n_exp, 1)

                    def probs_turned(u):
                        act.wait_ge(n_pT, i * 8 + (u + 1))
                        if u >= 2:
                            act.wait_ge(n_pv, i * 8 + (u - 1))
                        act.activation(n_pTs[u % 2], bank(4 + u % 2, 0, 384), ACT.Copy).then_inc(n_pTd, 1)

                    exps(0)
                    for u in range(1, 8):
                        exps(u)
                        probs_turned(u - 1)
                    probs_turned(7)
                out_hi("o_n")

            for t in range(RING):
                split(t)
            act.wait_ge(loaded, 16 * 5)
            act.wait_ge(const_ready, 4)
            act.activation(ASQ, x[:, :], ACT.Square).then_inc(sq_ready, 1)
            norm("mix_0")
            mla()
            residual("wo_a", 1)
            act.wait_ge(bias_done, 1)
            act.dma_start(bias_dram, bias_row[:, :].unsqueeze(1).broadcast_to((H, COPIES, 2 * S))).then_inc(bias_out, 16)
            norm("ffn_0")
            act.wait_ge(bias_out, 16)
            for g in range(P // COPIES):
                act.dma_start(bias[g * COPIES:(g + 1) * COPIES, :].rearrange("p (h s) -> p h s", h=H),
                              bass.AP(tensor=bias_dram.tensor, offset=P - 1 - g * COPIES,
                                      ap=[[2 * S - 1, COPIES], [COPIES * 2 * S, H], [1, S]])).then_inc(bias_in, 16)
            up("up_0")
            residual("down_0", 4)
            norm("mix_1")
            mlstm()
            residual("wo_m", 1)
            norm("ffn_1")
            up("up_1")
            residual("down_1", 4)
            norm("pre_0")
            glu("glu_0")
            residual("out_0", FF2_TILES)
            norm("mid_0")
            conv()
            residual("cout", 1)
            norm("post_0")
            glu("glu_1")
            residual("out_1", FF2_TILES)
            norm("kvn")
            nsa_kv()
            norm("pre_1")
            glu("glu_2")
            residual("out_2", FF2_TILES)
            norm("mid_1")
            nsa()
            residual("wo_n", 1)
            norm("post_1")
            glu("glu_3")
            residual("out_3", FF2_TILES)

        @block.vector
        def _(dve):
            steps = Steps()

            def then(ins):
                dve.wait_ge(dve_step, steps.mark(ins))

            def hi_of(ap):
                return ap.bitcast(F32)

            def norm(name, ready=None):
                groups = NORMS[name]
                if name != "pre_1":
                    n = TB * len(groups)
                    dve.wait_ge(std_ready, STD0[name])
                    then(dve.reciprocal(rstd[:, 0:n], std[:, 0:n]))
                    for j in range(n):
                        ins = dve.tensor_scalar(diag[:, j * P:(j + 1) * P], ident, rstd[:, j:j + 1], None, ALU.mult)
                    ins.then_inc(diag_ready, 1)
                    dve.wait_ge(rb_ready, STAT0[name])
                if ready is not None:
                    dve.wait_ge(tile_done, ready)
                chunks = [(s_, gain + j, g) for g, (src, gain, _) in enumerate(groups) for j, s_ in enumerate(src)]

                def lo(k):
                    dve.wait_ge(xhi_ready, XS0[name] + k + 1)
                    dve.tensor_tensor(xs_lo(k), fsum[k % 4][:, :], hi_of(xs_hi(k)), ALU.subtract).then_inc(xs_ready, 1)

                for k, (s_, gain, g) in enumerate(chunks):
                    dve.scalar_tensor_tensor(out=fsum[k % 4][:, :], in0=s_, scalar=vec[:, gain:gain + 1],
                                             in1=bank(RB, g * S, (g + 1) * S), op0=ALU.mult, op1=ALU.mult).then_inc(xn_ready, 1)
                    if k >= 1:
                        lo(k - 1)
                lo(len(chunks) - 1)

            def add_halves(name, b, u, dst, i=0, per=0, a=0, z=S, p=slice(None)):
                dve.wait_ge(half_ready, i * per + (half0[name] + u + 1))
                return dve.tensor_tensor(dst, bank(b, a, z, p), half[b][p, a:z], ALU.add).then_inc(out_read, 1)

            def plain(name, outs, dst):
                for o in range(outs):
                    add_halves(name, (OUT0[name] + o) % 4, o, dst(o))

            def token_major(name, outs, dst, tiles_):
                for o in range(outs):
                    d = dst(o)
                    dve.wait_ge(tile_done, TILE0[name] + tiles_(o))
                    dve.tensor_copy(d, bank((OUT0[name] + o) % 4, 0, d.shape[-1])).then_inc(out_read, 1)

            def residual(name, per, scale=1.0):
                t0, o0, no = TILE0[name], OUT0[name], RES.index(name)
                dve.memset(sq[3][:, :], 0.0).then_inc(sq_clear, 1)
                with dve.Fori(0, KD // 4) as i:
                    for u in range(4):
                        b = (o0 + u) % 4
                        xo = at(x, i * (4 * S) + u * S, S)
                        dve.wait_ge(tile_done, i * (4 * per) + (t0 + (u + 1) * per))
                        dve.scalar_tensor_tensor(out=xo, in0=bank(b, 0, S), scalar=scale, in1=xo, op0=ALU.mult, op1=ALU.add)\
                           .then_inc(x_half, 1)
                        dve.wait_ge(x_half, i * 4 + (KD * no + u + 1))
                        dve.scalar_tensor_tensor(out=xo, in0=bank(b, S, 2 * S), scalar=scale, in1=xo, op0=ALU.mult, op1=ALU.add)\
                           .then_inc(out_read, 1)

            def h_lo(name, src, chunk, count):
                dve.wait_ge(hhi_ready, count)
                dve.tensor_tensor(at(hs, chunk + S, S), src, hi_of(at(hs, chunk, S)), ALU.subtract).then_inc(hs_ready, 1)

            def up(name):
                o0, h0 = OUT0[name], hid0[name]
                with dve.Fori(0, FF1 // 4) as i:
                    for u in range(4):
                        b = (o0 + u) % 4
                        f = fsum[b][:, :]
                        add_halves(name, b, u, f, i, 4)
                        dve.wait_ge(out_read, i * 4 + (o0 + u + 1))
                        dve.scalar_tensor_tensor(out=f, in0=f, scalar=0.0, in1=f, op0=ALU.max, op1=ALU.mult).then_inc(hid_ready, 1)
                        h_lo(name, f, i * (8 * S) + u * 2 * S, i * 4 + (h0 + u + 1))

            def glu(name):
                o0, h0 = OUT0[name], hid0[name]
                with dve.Fori(0, FF2 // 2) as i:
                    for u in range(4):
                        b = (o0 + u) % 4
                        f = fsum[b][:, :]
                        add_halves(name, b, u, f, i, 4)
                        if u % 2:
                            dve.wait_ge(sil_ready, i * 2 + (sil0[name] + u // 2 + 1))
                            dve.wait_ge(out_read, i * 4 + (o0 + u + 1))
                            dve.tensor_tensor(f, f, sil[u // 2][:, :], ALU.mult).then_inc(hid_ready, 1)
                            h_lo(name, f, i * (4 * S) + (u // 2) * 2 * S, i * 2 + (h0 + u // 2 + 1))

            def conv():
                name, o0, h0 = "cin", OUT0["cin"], hid0["cin"]
                for j in range(2):
                    ins = dve.memset(conv_u[j][:, 0:TAPS - 1], 0.0)
                then(ins)
                with dve.Fori(0, KD // 4) as i:
                    steps.base, start, steps.n = i * 16 + steps.n, steps.n, 0
                    for m in range(4):
                        j = m % 2
                        for n, dst in enumerate((conv_b[j], conv_c[j], conv_v[j])):
                            u = 3 * m + n
                            add_halves(name, (o0 + u) % 4, u, dst, i, 12)
                        dve.wait_ge(out_read, i * 12 + (o0 + 3 * m + 3))
                        then(dve.tensor_tensor(conv_u[j][:, TAPS - 1:], conv_c[j], conv_v[j], ALU.mult))
                        for k in range(TAPS):
                            w = at(vec, i * 4 + (VEC["taps"] + k * KD + m), 1)
                            if k == 0:
                                then(dve.tensor_scalar(conv_y[j], conv_u[j][:, 0:S], w, None, ALU.mult))
                            else:
                                then(dve.scalar_tensor_tensor(out=conv_y[j], in0=conv_u[j][:, k:k + S], scalar=w, in1=conv_y[j],
                                                              op0=ALU.mult, op1=ALU.add))
                        dve.tensor_tensor(conv_y[j], conv_y[j], conv_b[j], ALU.mult).then_inc(hid_ready, 1)
                        h_lo(name, conv_y[j], i * (8 * S) + m * 2 * S, i * 4 + (h0 + m + 1))
                    assert steps.n == 16
                    steps.base, steps.n = 0, start + 16 * (KD // 4)

            def out_lo(name):
                for k in range(KD):
                    dve.wait_ge(xhi_ready, XS0[name] + k + 1)
                    dve.tensor_tensor(xs_lo(k), bank(k % 4, 0, S), hi_of(xs_hi(k)), ALU.subtract).then_inc(xs_ready, 1)

            def mla():
                plain("dq", 3, lambda o: cqf[:, o * S:(o + 1) * S])
                plain("dkv", 2, lambda o: cqf[:, (KQ + o) * S:(KQ + o + 1) * S])
                token_major("kr", 2, lambda o: kr_tok[:, o * ROPE:(o + 1) * ROPE], lambda o: 1)
                norm("cq", ready=TILE0["kr"] + 1)
                token_major("uq", 6, lambda o: q_tok[:, (o % 2) * H * QK + (o // 2) * 512:][:, 0:512],
                            lambda o: [2, 2, 3, 3, 5, 5][o])
                token_major("uk", 4, lambda o: k_tok[:, (o % 2) * H * NOPE + (o // 2) * 512:][:, 0:512], lambda o: 1 + o // 2)
                token_major("uv", 4, lambda o: v_tok[:, (o % 2) * H * VD + (o // 2) * 512:][:, 0:512], lambda o: 1 + o // 2)
                dve.wait_ge(out_read, OUT0["uv"] + 4)
                q3 = q_tok.rearrange("p (n d) -> p n d", d=QK)
                k3 = k_tok.rearrange("p (n d) -> p n d", d=NOPE)
                kr3 = kr_tok.rearrange("p (n d) -> p n d", d=ROPE)
                gq, gk = row[:, ROW["q_gain"]:ROW["q_gain"] + QK], row[:, ROW["k_gain"]:ROW["k_gain"] + QK]
                sizes = [(mscr[n % 2][:, 0:w], w) for n, (_, w) in enumerate(HEAD_SQ)]
                for n, (src, w) in enumerate(sizes):
                    d = [QK] * 4 + [NOPE] * 2 + [ROPE]
                    first = [0, 8, 16, 24, 32, 48, 64][n]
                    dve.wait_ge(head_sq, n + 1)
                    dve.tensor_reduce(ss[:, first:first + w // d[n]], src.rearrange("p (n d) -> p n d", d=d[n]), AX_X, ALU.add)\
                       .then_inc(head_sum, 1)
                dve.wait_ge(head_sum, len(HEAD_SQ))
                ssk = ss[:, 2 * H:4 * H].rearrange("p (t h) -> p t h", t=TB)
                ssr = ss[:, 4 * H:4 * H + TB].unsqueeze(2).to_broadcast([P, TB, H])
                dve.tensor_tensor(ssk, ssk, ssr, ALU.add).then_inc(head_sum, 1)
                then(dve.tensor_tensor(q3, q3, gq.unsqueeze(1).to_broadcast([P, TB * H, QK]), ALU.mult))
                dve.tensor_tensor(k3, k3, gk[:, 0:NOPE].unsqueeze(1).to_broadcast([P, TB * H, NOPE]), ALU.mult)
                then(dve.tensor_tensor(kr3, kr3, gk[:, NOPE:].unsqueeze(1).to_broadcast([P, TB, ROPE]), ALU.mult))
                cos = con[:, CONST["cos"]:CONST["cos"] + TB * HALF].rearrange("p (t d) -> p t d", t=TB)
                sin = con[:, CONST["sin"]:CONST["sin"] + TB * HALF].rearrange("p (t d) -> p t d", t=TB)
                q4 = q_tok.rearrange("p (t h d) -> p t h d", t=TB, h=H)
                for heads, lo_, hi_ in ((H, q4[:, :, :, NOPE:NOPE + HALF], q4[:, :, :, NOPE + HALF:QK]),
                                        (1, kr3[:, :, 0:HALF].unsqueeze(2), kr3[:, :, HALF:ROPE].unsqueeze(2))):
                    n = TB * heads * HALF
                    t = [rope_t[:, j * n:(j + 1) * n].rearrange("p (t h d) -> p t h d", t=TB, h=heads) for j in range(4)]
                    c4 = cos.unsqueeze(2).to_broadcast([P, TB, heads, HALF])
                    s4 = sin.unsqueeze(2).to_broadcast([P, TB, heads, HALF])
                    dve.tensor_tensor(t[0], lo_, c4, ALU.mult)
                    dve.tensor_tensor(t[1], hi_, s4, ALU.mult)
                    dve.tensor_tensor(t[2], hi_, c4, ALU.mult)
                    then(dve.tensor_tensor(t[3], lo_, s4, ALU.mult))
                    dve.tensor_tensor(lo_, t[0], t[1], ALU.subtract)
                    then(dve.tensor_tensor(hi_, t[2], t[3], ALU.add))
                dve.wait_ge(head_std, 1)
                then(dve.reciprocal(rstd[:, 0:4 * H], std[:, 0:4 * H]))
                rq = rstd[:, 0:2 * H].rearrange("p (t h) -> p t h", t=TB)
                rk = rstd[:, 2 * H:4 * H].rearrange("p (t h) -> p t h", t=TB)
                qs4 = q_st.rearrange("p (t h d) -> p t h d", t=TB, h=4)
                ks4 = k_st.rearrange("p (t h d) -> p t h d", t=TB, h=4)
                kt3 = k_tok.rearrange("p (t c) -> p t c", t=TB)
                qt3 = q_tok.rearrange("p (t c) -> p t c", t=TB)
                ot3 = o_tok.rearrange("p (t c) -> p t c", t=TB)
                with dve.Fori(0, H // 4) as i:
                    steps.base, start, steps.n = i * 8 + steps.n, steps.n, 0
                    for tb in range(TB):
                        r = rq[:, tb, bass.ds(i * 4, 4)].unsqueeze(2)
                        dve.tensor_tensor(qs4[:, tb], qt3[:, tb, bass.ds(i * (4 * QK), 4 * QK)].rearrange("p (h d) -> p h d", h=4),
                                          r.to_broadcast([P, 4, QK]), ALU.mult)
                        r = rk[:, tb, bass.ds(i * 4, 4)].unsqueeze(2)
                        dve.tensor_tensor(ks4[:, tb, :, 0:NOPE],
                                          kt3[:, tb, bass.ds(i * (4 * NOPE), 4 * NOPE)].rearrange("p (h d) -> p h d", h=4),
                                          r.to_broadcast([P, 4, NOPE]), ALU.mult)
                        ins = dve.tensor_tensor(ks4[:, tb, :, NOPE:QK], kr3[:, tb].unsqueeze(1).to_broadcast([P, 4, ROPE]),
                                                r.to_broadcast([P, 4, ROPE]), ALU.mult)
                    ins.then_inc(a_st, 1)

                    def maxima(h):
                        dve.wait_ge(a_s, i * 4 + (h + 1))
                        dve.tensor_reduce(mx[:, 2 * h:2 * h + 1], bank(2 + h % 2, 0, P), AX_X, ALU.max)
                        then(dve.tensor_reduce(mx[:, 2 * h + 1:2 * h + 2], bank(2 + h % 2, P, 3 * P), AX_X, ALU.max))
                        dve.tensor_scalar(nmx[:, 2 * h:2 * h + 2], mx[:, 2 * h:2 * h + 2], -(QK ** -0.5), None, ALU.mult).then_inc(a_max, 1)

                    def outputs(h):
                        dve.wait_ge(a_exp, i * 8 + 2 * (h + 1))
                        then(dve.reciprocal(rinv[:, 2 * h:2 * h + 2], rsum[:, 2 * h:2 * h + 2]))
                        dve.wait_ge(a_pv, i * 4 + (h + 1))
                        for tb in range(TB):
                            ins = dve.tensor_scalar(ot3[:, tb, bass.ds(i * (4 * VD) + h * VD, VD)], bank(6 + h % 2, tb * VD, (tb + 1) * VD),
                                                    rinv[:, 2 * h + tb:2 * h + tb + 1], None, ALU.mult)
                        ins.then_inc(a_o, 1)

                    maxima(0)
                    maxima(1)
                    maxima(2)
                    outputs(0)
                    maxima(3)
                    outputs(1)
                    outputs(2)
                    outputs(3)
                    assert steps.n == 8
                    steps.base, steps.n = 0, start + 8 * (H // 4)
                out_lo("o_a")

            def mlstm():
                for o, (dst, b) in enumerate(((m_ti, "b_i"), (m_tf, "b_f"))):
                    bk = (OUT0["mgate"] + o) % 4
                    dve.wait_ge(half_ready, half0["mgate"] + o + 1)
                    dve.scalar_tensor_tensor(out=dst, in0=bank(bk, 0, S, slice(0, MH)), scalar=vec[0:MH, VEC[b]:VEC[b] + 1],
                                             in1=half[bk][0:MH, :], op0=ALU.add, op1=ALU.add).then_inc(out_read, 1)
                plain("mqk", 8, lambda o: m_qk[:, o * S:(o + 1) * S])
                token_major("mv", 4, lambda o: m_v[:, (o % 2) * D + (o // 2) * 512:][:, 0:512], lambda o: 4 * (1 + o // 2))
                plain("mo", 8, lambda o: m_o[:, o * S:(o + 1) * S])
                then(dve.memset(m_one, 1.0))
                dve.wait_ge(m_tanh, 4)
                then(dve.tensor_tensor_scan(m_nb, m_one, m_tf, 0.0, ALU.mult, ALU.add))
                then(dve.scalar_tensor_tensor(out=m_a, in0=m_ti, scalar=GATE_CAP, in1=m_nb, op0=ALU.mult, op1=ALU.add))
                then(dve.tensor_tensor_scan(m_g, m_a, m_a, 0.0, ALU.max, ALU.max))
                dve.tensor_scalar(m_bc[:, 0:S], m_g, -1.0, None, ALU.mult)
                dve.tensor_tensor(m_bc[:, S:2 * S], m_nb, m_g, ALU.subtract).then_inc(m_rows, 1)
                dve.wait_ge(m_at, 1)
                then(dve.tensor_copy(m_acol, bank(7, 0, TB * MH)))
                causal = const("causal", 0, P)

                def exponents(h):
                    dve.wait_ge(m_bcd, h + 1)
                    dve.tensor_copy(m_fl[h % 2], bank(4, S, 2 * S))
                    dve.tensor_scalar(m_w[h % 2][:, 0:S], bank(4, 0, S), m_acol[:, h:h + 1], 0.0, ALU.add, ALU.min)
                    dve.tensor_scalar(m_w[h % 2][:, S:S + P], bank(4, P, S), m_acol[:, MH + h:MH + h + 1], 0.0, ALU.add, ALU.min)\
                       .then_inc(m_logw, 1)

                def weights(h):
                    w = m_w[h % 2]
                    dve.wait_ge(m_exp, h + 1)
                    dve.tensor_tensor(w[:, 0:P], w[:, 0:P], causal, ALU.mult)
                    then(dve.tensor_tensor(w[:, S:S + P], w[:, S:S + P], causal, ALU.mult))
                    dve.wait_ge(m_st, h + 1)
                    dve.scalar_tensor_tensor(out=m_pt[h % 2], in0=bank(5, 0, 384), scalar=MQK ** -0.5, in1=w, op0=ALU.mult, op1=ALU.mult)\
                       .then_inc(m_ptd, 1)

                exponents(0)
                for h in range(MH):
                    weights(h)
                    if h + 1 < MH:
                        exponents(h + 1)
                    hh = m_h[h % 2]
                    den = m_den[h % 2]
                    dve.wait_ge(m_absd, h + 1)
                    then(dve.tensor_tensor(den, den, m_fl[h % 2], ALU.max))
                    then(dve.reciprocal(den, den))
                    dve.wait_ge(m_num, h + 1)
                    dve.tensor_tensor(hh.rearrange("p (v t) -> p v t", v=2), bank(h % 2).rearrange("p (v t) -> p v t", v=2),
                                      den.unsqueeze(1).to_broadcast([P, 2, S]), ALU.mult).then_inc(m_hc, 1)
                    dve.wait_ge(m_stdd, h + 1)
                    then(dve.reciprocal(m_r, m_std))
                    for v in range(2):
                        g = VEC["head_norm"] + 2 * h + v
                        ins = dve.scalar_tensor_tensor(out=hh[:, v * S:(v + 1) * S], in0=hh[:, v * S:(v + 1) * S], scalar=vec[:, g:g + 1],
                                                       in1=m_r, op0=ALU.mult, op1=ALU.mult)
                    then(ins)
                    if h == 0:
                        dve.wait_ge(m_sig, 1)
                    for v in range(2):
                        dve.tensor_tensor(hh[:, v * S:(v + 1) * S], hh[:, v * S:(v + 1) * S],
                                          m_o[:, (2 * h + v) * S:(2 * h + v + 1) * S], ALU.mult).then_inc(xn_ready, 1)
                    for v in range(2):
                        k = 2 * h + v
                        dve.wait_ge(xhi_ready, XS0["o_m"] + k + 1)
                        dve.tensor_tensor(xs_lo(k), hh[:, v * S:(v + 1) * S], hi_of(xs_hi(k)), ALU.subtract).then_inc(xs_ready, 1)

            def nsa_kv():
                token_major("kv", 4, lambda o: (kn_tok if o < 2 else vtok)[:, (o % 2) * 512:(o % 2 + 1) * 512],
                            lambda o: 4 * (1 + o // 2))
                for o in range(8):
                    b = (OUT0["kvc"] + o) % 4
                    dst = c_dup[o // G][:, (o % G) * S:(o % G + 1) * S]
                    dve.wait_ge(half_ready, half0["kvc"] + o + 1)
                    dve.tensor_tensor(dst[0:DH, :], bank(b, 0, S, slice(0, DH)), half[b][0:DH, :], ALU.add)
                    dve.tensor_tensor(dst[DH:P, 0:S - 1], bank(b, 1, S, slice(DH, P)), half[b][DH:P, 1:S], ALU.add).then_inc(out_read, 1)
                for tb in range(TB):
                    dve.wait_ge(c_sqd, tb + 1)
                    dve.tensor_reduce(c_ss[:, tb * 8:(tb + 1) * 8], c_sq[tb].rearrange("p (n d) -> p n d", d=DH), AX_X, ALU.add)\
                       .then_inc(c_sum, 1)
                dve.wait_ge(c_std, 1)
                then(dve.reciprocal(c_r, std[:, 0:16]))
                kn3 = kn_tok.rearrange("p (n d) -> p n d", d=DH)
                then(dve.tensor_tensor(kn3, kn3, c_r.unsqueeze(2).to_broadcast([P, 16, DH]), ALU.mult))
                gain = row[:, ROW["ks"]:ROW["ks"] + 2 * DH].rearrange("p (b d) -> p b d", b=2).unsqueeze(2).to_broadcast([P, 2, G, DH])
                for tb in range(TB):
                    k4 = kn_tok[:, tb * 512:(tb + 1) * 512].rearrange("p (b g d) -> p b g d", b=2, g=G)
                    ins = dve.tensor_tensor(k4, k4, gain, ALU.mult)
                ins.then_inc(c_kn, 1)
                dve.wait_ge(c_kt, 1)
                for b in range(2):
                    dve.tensor_copy(kT[:, b * 512:(b + 1) * 512], bank(6 + b)).then_inc(c_kT, 1)
                dve.wait_ge(c_hd, 1)
                for j in range(2):
                    ins = dve.tensor_copy(c_pe[:, j:j + 1], bank(2, j, j + 1))
                ins.then_inc(c_bias, 1)
                dve.wait_ge(c_kcstdd, 1)
                then(dve.reciprocal(c_kcr, c_kcstd))
                g = VEC["kc_norm"]
                dve.scalar_tensor_tensor(out=kcT[:, :], in0=bank(6, 0, G * NC), scalar=vec[:, g:g + 1], in1=c_kcr,
                                         op0=ALU.mult, op1=ALU.mult).then_inc(c_end, 1)
                dve.wait_ge(c_vcd, 1)
                dve.tensor_copy(vc[:, :], bank(7, 0, G * DH, slice(0, NC))).then_inc(c_end, 1)

            def nsa():
                token_major("ngate", 2, lambda o: n_gate[:, o * 3 * H:(o + 1) * 3 * H], lambda o: 1)
                token_major("nq", 4, lambda o: nq_tok[:, (o % 2) * D + (o // 2) * 512:][:, 0:512], lambda o: 4 * (1 + o // 2))
                for tb in range(TB):
                    dve.wait_ge(n_sqd, tb + 1)
                    dve.tensor_reduce(n_ss[:, tb * H:(tb + 1) * H], n_sq[tb].rearrange("p (n d) -> p n d", d=DH), AX_X, ALU.add)\
                       .then_inc(n_sum, 1)
                q3 = nq_tok.rearrange("p (n d) -> p n d", d=DH)
                gain = row[:, ROW["nq"]:ROW["nq"] + DH].unsqueeze(1).to_broadcast([P, TB * H, DH])
                then(dve.tensor_tensor(q3, q3, gain, ALU.mult))
                dve.wait_ge(n_std_, 1)
                then(dve.reciprocal(n_r, std[:, 0:TB * H]))
                dve.wait_ge(n_sig, 1)
                dve.wait_ge(bias_in, 16 * (P // COPIES))
                scale = DH ** -0.5
                q4 = nq_tok.rearrange("p (t g c) -> p t g c", t=TB, g=2)
                o4 = no_tok.rearrange("p (t g c) -> p t g c", t=TB, g=2)
                r4 = n_r.rearrange("p (t g c) -> p t g c", t=TB, g=2)
                g4 = n_gate.rearrange("p (t g c) -> p t g c", t=TB, g=2)
                qs5 = n_qs.rearrange("p (t g e d) -> p t g e d", t=TB, g=2, e=2)
                gates = n_g.rearrange("p (t g c) -> p t g c", t=TB, g=2)
                gate_w = n_g.rearrange("p (t w b) -> p t w b", t=TB, b=3)
                b4 = bias[:, :].rearrange("p (h a b) -> p h a b", h=H, b=CSTRIDE)
                cl = [n_cl[:, 0:4 * NC0].rearrange("p (w c) -> p w c", w=4), n_cl[:, 4 * NC0:].rearrange("p (w c) -> p w c", w=4)]
                with dve.Fori(0, HG) as i:
                    steps.base, start, steps.n = i * N_STEPS + steps.n, steps.n, 0
                    for gp in range(2):
                        r = r4[:, :, gp, bass.ds(i * 2, 2)].unsqueeze(3).to_broadcast([P, TB, 2, DH])
                        q = q4[:, :, gp, bass.ds(i * P, P)].rearrange("p t (e d) -> p t e d", e=2)
                        ins = dve.tensor_tensor(qs5[:, :, gp], q, r, ALU.mult)
                    ins.then_inc(n_st, 1)
                    then(dve.tensor_copy(gates, g4[:, :, :, bass.ds(i * 6, 6)]))
                    dve.wait_ge(n_cs, i + 1)
                    for w in range(4):
                        gp, e = w // 2, w % 2
                        bk = 3 if e == 0 else 0
                        n = i * 2 + (gp * 8 + e)
                        for tb, (c, first) in enumerate(((NC0, 9), (NC, 1))):
                            bs = b4[:, bass.ds(n, 1), first:first + c, CSTRIDE - 1:CSTRIDE].rearrange("p o a b -> p (o a b)")
                            ins = dve.scalar_tensor_tensor(out=cl[tb][:, w, :], in0=bank(bk, w * 32 + tb * 8, w * 32 + tb * 8 + c), scalar=scale,
                                                           in1=bs, op0=ALU.mult, op1=ALU.add)
                    then(ins)
                    for tb in range(TB):
                        ins = dve.tensor_reduce(n_cmx[:, tb * 4:(tb + 1) * 4], cl[tb], AX_X, ALU.max)
                    then(ins)
                    for tb, c in enumerate((NC0, NC)):
                        ins = dve.tensor_tensor(cl[tb], cl[tb], n_cmx[:, tb * 4:(tb + 1) * 4].unsqueeze(2).to_broadcast([P, 4, c]), ALU.subtract)
                    ins.then_inc(n_clog, 1)
                    dve.wait_ge(n_cexp, i + 1)
                    for tb in range(TB):
                        ins = dve.tensor_reduce(n_crs[:, tb * 4:(tb + 1) * 4], cl[tb], AX_X, ALU.add)
                    then(ins)
                    then(dve.reciprocal(n_crs, n_crs))
                    then(dve.tensor_tensor(n_csc.rearrange("p (t w) -> p t w", t=TB), n_crs.rearrange("p (t w) -> p t w", t=TB),
                                           gate_w[:, :, :, 0], ALU.mult))
                    then(dve.tensor_tensor(n_csc.rearrange("p (t w) -> p t w", t=TB), n_csc.rearrange("p (t w) -> p t w", t=TB),
                                           con[:, CONST["valid"]:CONST["valid"] + TB].unsqueeze(2).to_broadcast([P, TB, 4]), ALU.mult))

                    def scores(u):
                        gp, br, e = u // 4, u // 2 % 2, u % 2
                        first = i * (2 * S) + (gp * 8 + e) * S
                        dve.wait_ge(n_s, i * 8 + (u + 1))
                        if u >= 2:
                            dve.wait_ge(n_exp, i * 16 + 2 * (u - 1))
                        log = n_l[u % 2]
                        dve.scalar_tensor_tensor(out=log[:, 0:P], in0=bank(1 + e, 0, P), scalar=scale, in1=at(bias, first + P, P),
                                                 op0=ALU.mult, op1=ALU.add)
                        dve.scalar_tensor_tensor(out=log[:, P:3 * P], in0=bank(1 + e, P, 3 * P), scalar=scale, in1=at(bias, first, S),
                                                 op0=ALU.mult, op1=ALU.add).then_inc(n_lr, 1)
                        dve.wait_ge(n_lr, i * 8 + (u + 1))
                        dve.tensor_reduce(n_mx[:, 2 * u:2 * u + 1], log[:, 0:P], AX_X, ALU.max)
                        then(dve.tensor_reduce(n_mx[:, 2 * u + 1:2 * u + 2], log[:, P:3 * P], AX_X, ALU.max))
                        dve.tensor_scalar(n_nmx[:, 2 * u:2 * u + 2], n_mx[:, 2 * u:2 * u + 2], -1.0, None, ALU.mult).then_inc(n_max, 1)

                    o8 = n_o.rearrange("p (n d) -> p n d", d=DH)

                    def compressed():
                        dve.wait_ge(n_cpv, i + 1)
                        dve.tensor_tensor(o8, bank(6).rearrange("p (n d) -> p n d", d=DH), n_csc.unsqueeze(2).to_broadcast([P, 8, DH]), ALU.mult)\
                           .then_inc(n_co, 1)

                    def outputs(u):
                        gp, br, e = u // 4, u // 2 % 2, u % 2
                        w = 2 * gp + e
                        dve.wait_ge(n_exp, i * 16 + 2 * (u + 1))
                        then(dve.reciprocal(n_sc[:, 2 * u:2 * u + 2], n_rs[:, 2 * u:2 * u + 2]))
                        then(dve.tensor_tensor(n_sc[:, 2 * u:2 * u + 2], n_sc[:, 2 * u:2 * u + 2], gate_w[:, :, w, 1 + br], ALU.mult))
                        dve.wait_ge(n_pv, i * 8 + (u + 1))
                        if u == 0:
                            dve.wait_ge(n_co, i + 1)
                        elif br == 1:
                            dve.wait_ge(n_od, i * 8 + (u - 1))
                        for tb in range(TB):
                            o = o8[:, tb * 4 + w, :]
                            ins = dve.scalar_tensor_tensor(out=o, in0=bank(6 + u % 2, tb * DH, (tb + 1) * DH),
                                                           scalar=n_sc[:, 2 * u + tb:2 * u + tb + 1], in1=o, op0=ALU.mult, op1=ALU.add)
                        ins.then_inc(n_od, 1)

                    scores(0)
                    scores(1)
                    compressed()
                    for u in range(2, 8):
                        scores(u)
                        outputs(u - 2)
                    outputs(6)
                    outputs(7)
                    dve.wait_ge(n_od, i * 8 + 8)
                    dve.tensor_copy(o4[:, :, :, bass.ds(i * P, P)], n_o.rearrange("p (t g c) -> p t g c", t=TB, g=2)).then_inc(n_end, 1)
                    assert steps.n == N_STEPS, steps.n
                    steps.base, steps.n = 0, start + N_STEPS * HG
                out_lo("o_n")

            dve.wait_ge(loaded, 16 * 5)
            dve.wait_ge(const_ready, 4)
            dve.tensor_copy(chunk_u[:, :], con[0:1, CONST["chunk_u"]:CONST["chunk_u"] + P])
            then(dve.tensor_copy(chunk_v[:, :], con[0:1, CONST["chunk_v"]:CONST["chunk_v"] + P]))
            dve.wait_ge(row_ready, 1)
            dve.tensor_copy(bias_row[:, :], bank(6, 0, 2 * S, slice(0, H))).then_inc(bias_done, 1)
            norm("mix_0")
            mla()
            residual("wo_a", 1)
            norm("ffn_0")
            up("up_0")
            residual("down_0", 4)
            norm("mix_1")
            mlstm()
            residual("wo_m", 1)
            norm("ffn_1")
            up("up_1")
            residual("down_1", 4)
            norm("pre_0")
            glu("glu_0")
            residual("out_0", FF2_TILES, 0.5)
            norm("mid_0")
            conv()
            residual("cout", 1)
            norm("post_0")
            glu("glu_1")
            residual("out_1", FF2_TILES, 0.5)
            norm("kvn")
            nsa_kv()
            norm("pre_1", ready=TILE0["kvc"] + 8)
            glu("glu_2")
            residual("out_2", FF2_TILES, 0.5)
            norm("mid_1")
            nsa()
            residual("wo_n", 1)
            norm("post_1")
            glu("glu_3")
            residual("out_3", FF2_TILES, 0.5)

        @block.tensor
        def _(pe):
            def product(out_bank, lhs, k, src, first, last, hi=0):
                s, c = lhs
                chunk = k * 2 * S
                pe.matmul(bank(out_bank), w_hi[s][:, c:c + P], src[:, chunk:chunk + 2 * S], start=first, stop=False)
                return pe.matmul(bank(out_bank, 0, S), w_lo[s][:, c:c + P], src[:, chunk:chunk + S], start=False, stop=last)

            def zero_stat(n):
                pe.matmul(bank(STAT, 0, n), zeros[:, :], ones[:, 0:n], start=True, stop=False)

            def add_stat(col, squares, last=False):
                for tb in range(TB):
                    ins = pe.matmul(bank(STAT, col + tb, col + tb + 1), squares[:, tb * P:(tb + 1) * P], ones[:, 0:1],
                                    start=False, stop=last and tb == TB - 1)
                return ins

            def norm(name):
                n = TB * len(NORMS[name])
                pe.wait_ge(diag_ready, STAT0[name])
                pe.matmul(bank(RB, 0, n * P), ones[:, :], diag[:, 0:n * P], start=True, stop=True).then_inc(rb_ready, 1)

            def feature(name, outs, xs_name, k0=0, chunks=KD):
                t0, o0 = TILE0[name], OUT0[name]

                def one(u, i=0, wait_x=False):
                    s, b = (t0 + u) % RING, (o0 + u) % 4
                    pe.wait_ge(lo_ready, i * 4 + (t0 + u + 1))
                    if not (isinstance(i, int) and o0 + u + 4 * i < 4):
                        pe.wait_ge(out_read, i * 4 + (o0 + u - 3))
                    for k in range(chunks):
                        if wait_x:
                            pe.wait_ge(xs_ready, XS0[xs_name] + k0 + k + 1)
                        ins = product(b, (s, k * P), k0 + k, xs, k == 0, k == chunks - 1)
                    ins.then_inc(tile_done, 1)

                head = min(outs, 4) if outs % 4 == 0 else outs
                for u in range(head):
                    one(u, 0, u == 0)
                if outs > 4 and outs % 4 == 0:
                    with pe.Fori(1, outs // 4) as i:
                        for u in range(4):
                            one(u, i)

            def residual(name, per, chunks, src, ready):
                t0, o0, no = TILE0[name], OUT0[name], RES.index(name)
                last = name == RES[-1]
                if not last:
                    zero_stat(TB)
                    pe.wait_ge(sq_clear, no + 1)
                with pe.Fori(0, KD // 4) as i:
                    for u in range(4):
                        b = (o0 + u) % 4
                        pe.wait_ge(out_read, i * 4 + (o0 + u - 3))
                        for j in range(per):
                            t = t0 + u * per + j
                            pe.wait_ge(lo_ready, i * (4 * per) + (t + 1))
                            n = min(BLK, chunks - j * BLK)
                            for k in range(n):
                                c = j * BLK + k
                                if u == 0:
                                    pe.wait_ge(*ready(c))
                                ins = product(b, (t % RING, k * P), c, src, c == 0, c == chunks - 1)
                            ins.then_inc(tile_done, 1)
                        if not last:
                            pe.wait_ge(sq_ready, i * 4 + (SQ0[name] + u))
                            add_stat(0, sq[(u - 1) % 4])
                if not last:
                    pe.wait_ge(sq_ready, SQ0[name] + KD)
                    add_stat(0, sq[3], True).then_inc(stat_done, 1)

            def token_major(name, groups, chunks, k0=0, xs_name=None):
                t0, o0 = TILE0[name], OUT0[name]
                for n in range(groups * chunks):
                    g, c = divmod(n, chunks)
                    s, col = (t0 + n // 2) % RING, n % 2 * 512
                    pe.wait_ge(lo_ready, t0 + n // 2 + 1)
                    if c == 0:
                        pe.wait_ge(out_read, o0 + 2 * g + 1 - 3)
                    if xs_name and g == 0:
                        pe.wait_ge(xs_ready, XS0[xs_name] + k0 + c + 1)
                    for tb in range(TB):
                        x_hi, x_lo = (xs[:, (k0 + c) * 2 * S + part_ * S + tb * P:][:, 0:P] for part_ in range(2))
                        out = bank((o0 + 2 * g + tb) % 4)
                        pe.matmul(out, x_hi, w_hi[s][:, col:col + 512], start=c == 0, stop=False)
                        pe.matmul(out, x_hi, w_lo[s][:, col:col + 512], start=False, stop=False)
                        ins = pe.matmul(out, x_lo, w_hi[s][:, col:col + 512], start=False, stop=c == chunks - 1)
                    if n % 2 == 1 or n == groups * chunks - 1:
                        ins.then_inc(tile_done, 1)

            def narrow(name, width, xs_name=None):
                t0, o0 = TILE0[name], OUT0[name]
                s = t0 % RING
                pe.wait_ge(lo_ready, t0 + 1)
                pe.wait_ge(out_read, o0 + 1 - 3)
                for tb in range(TB):
                    for k in range(KD):
                        if xs_name and tb == 0:
                            pe.wait_ge(xs_ready, XS0[xs_name] + k + 1)
                        x_hi, x_lo = (xs[:, k * 2 * S + part_ * S + tb * P:][:, 0:P] for part_ in range(2))
                        out = bank((o0 + tb) % 4, 0, width)
                        wh, wl = (w[s][:, k * P:k * P + width] for w in (w_hi, w_lo))
                        pe.matmul(out, x_hi, wh, start=k == 0, stop=False)
                        pe.matmul(out, x_hi, wl, start=False, stop=False)
                        ins = pe.matmul(out, x_lo, wh, start=False, stop=k == KD - 1)
                ins.then_inc(tile_done, 1)

            def turn_outputs(name, src, ready):
                pe.wait_ge(*ready)
                for k in range(KD):
                    if k >= 4:
                        pe.wait_ge(xs_ready, XS0[name] + k - 3)
                    for tb in range(TB):
                        ins = pe.transpose(bank(k % 4, tb * P, (tb + 1) * P), src[:, tb * D + k * P:tb * D + (k + 1) * P], ident)
                    ins.then_inc(o_turn[name], 1)

            def mla():
                feature("dq", 3, "mix_0")
                feature("dkv", 2, "mix_0")
                narrow("kr", ROPE)
                zero_stat(2 * TB)
                pe.wait_ge(sq_ready, SQ0["cq"] + 1)
                for k in range(KQ + KKV):
                    ins = add_stat(0 if k < KQ else TB, ASQ[:, k * S:(k + 1) * S], k == KQ + KKV - 1)
                ins.then_inc(stat_done, 1)
                norm("cq")
                token_major("uq", 3, KQ, 0, "cq")
                token_major("uk", 2, KKV, KQ, "cq")
                token_major("uv", 2, KKV, KQ)
                pe.wait_ge(out_read, OUT0["uv"] + 4)
                qs4 = q_st.rearrange("p (t h d) -> p t h d", t=TB, h=4)
                ks4 = k_st.rearrange("p (t h d) -> p t h d", t=TB, h=4)
                vt3 = v_tok.rearrange("p (t c) -> p t c", t=TB)
                with pe.Fori(0, H // 4) as i:
                    def turn(h):
                        for n, src in enumerate((qs4, ks4)):
                            for tb in range(TB):
                                at_ = (n * TB + tb) * P
                                ins = pe.transpose(bank(h % 2, at_, at_ + P, slice(0, QK)), src[:, tb, h, :], ident)
                        ins.then_inc(a_turn, 1)

                    def scores(h):
                        pe.wait_ge(a_qkT, i * 4 + (h + 1))
                        qk, b = qkT[h % 2][0:QK, :], 2 + h % 2
                        pe.matmul(bank(b, 0, P), qk[:, 0:P], qk[:, S:S + P], start=True, stop=False)
                        pe.matmul(bank(b, 0, P), chunk_u[:, :], chunk_v[:, :], start=False, stop=True)
                        pe.matmul(bank(b, P, 3 * P), qk[:, P:S], qk[:, S:2 * S], start=True, stop=False)
                        pe.matmul(bank(b, 2 * P, 3 * P), chunk_u[:, :], chunk_v[:, :], start=False, stop=True).then_inc(a_s, 1)

                    def turn_probs(h):
                        pe.wait_ge(a_exp, i * 8 + 2 * (h + 1))
                        for n in range(3):
                            ins = pe.transpose(bank(4 + h % 2, n * P, (n + 1) * P), prob[h % 2][:, n * P:(n + 1) * P], ident)
                        ins.then_inc(a_pT, 1)

                    def values(h):
                        pe.wait_ge(a_pTs, i * 4 + (h + 1))
                        if h < 2:
                            pe.wait_ge(a_o, i * 4)
                        else:
                            pe.wait_ge(a_o, i * 4 + (h - 1))
                        b, pT = 6 + h % 2, probT[h % 2]
                        v = [vt3[:, tb, bass.ds(i * (4 * VD) + h * VD, VD)] for tb in range(TB)]
                        pe.matmul(bank(b, 0, VD), pT[:, 0:P], v[0], start=True, stop=True)
                        pe.matmul(bank(b, VD, 2 * VD), pT[:, P:2 * P], v[0], start=True, stop=False)
                        pe.matmul(bank(b, VD, 2 * VD), pT[:, 2 * P:3 * P], v[1], start=False, stop=True).then_inc(a_pv, 1)

                    pe.wait_ge(a_st, i + 1)
                    turn(0)
                    turn(1)
                    scores(0)
                    scores(1)
                    turn_probs(0)
                    turn(2)
                    scores(2)
                    values(0)
                    turn_probs(1)
                    turn(3)
                    scores(3)
                    values(1)
                    turn_probs(2)
                    values(2)
                    turn_probs(3)
                    values(3)
                turn_outputs("o_a", o_tok, (a_o, H))

            def mlstm():
                feature("mgate", 2, "mix_1")
                feature("mqk", 8, "mix_1")
                token_major("mv", 2, KD)
                feature("mo", 8, "mix_1")
                pe.wait_ge(m_rows, 1)
                for tb in range(TB):
                    ins = pe.transpose(bank(7, tb * MH, (tb + 1) * MH), m_a[:, tb * P:(tb + 1) * P], con[0:MH, CONST["ident"]:CONST["ident"] + MH])
                ins.then_inc(m_at, 1)
                pe.wait_ge(m_floor, 1)
                pe.wait_ge(out_read, OUT0["mo"] + 8)

                def spread(h):
                    if h >= 1:
                        pe.wait_ge(m_logw, h)
                    pe.matmul(bank(4), const("select", h * P, (h + 1) * P, slice(0, MH)), m_bc, start=True, stop=True).then_inc(m_bcd, 1)

                def scores(h):
                    if h >= 1:
                        pe.wait_ge(m_ptd, h)
                    q, k = (m_qk[:, (n * MH + h) * S:(n * MH + h + 1) * S] for n in range(2))
                    pe.matmul(bank(5, 0, S), k[:, 0:P], q, start=True, stop=True)
                    pe.matmul(bank(5, S, S + P), k[:, P:S], q[:, P:S], start=True, stop=True).then_inc(m_st, 1)

                def outputs(h):
                    pt = m_pt[h % 2]
                    pe.wait_ge(m_ptd, h + 1)
                    if h >= 1:
                        pe.wait_ge(m_absd, h)
                    pe.matmul(bank(6, 0, S), ones[:, :], pt[:, 0:S], start=True, stop=False)
                    pe.matmul(bank(6, P, S), ones[:, :], pt[:, S:S + P], start=False, stop=True).then_inc(m_dend, 1)
                    if h >= 2:
                        pe.wait_ge(m_hc, h - 1)
                    for v in range(2):
                        cols = h * MV + v * P
                        pe.matmul(bank(h % 2, v * S, (v + 1) * S), m_v[:, cols:cols + P], pt[:, 0:S], start=True, stop=False)
                        ins = pe.matmul(bank(h % 2, v * S + P, (v + 1) * S), m_v[:, D + cols:D + cols + P], pt[:, S:S + P],
                                        start=False, stop=True)
                    ins.then_inc(m_num, 1)

                def head_squares(h):
                    pe.wait_ge(m_sqd, h + 1)
                    if h >= 1:
                        pe.wait_ge(m_stdd, h)
                    pe.matmul(bank(7, 0, S), ones[:, :], m_sq[h % 2][:, 0:S], start=True, stop=False)
                    pe.matmul(bank(7, 0, S), ones[:, :], m_sq[h % 2][:, S:2 * S], start=False, stop=True).then_inc(m_ss, 1)

                spread(0)
                scores(0)
                for h in range(MH):
                    if h + 1 < MH:
                        spread(h + 1)
                    outputs(h)
                    if h + 1 < MH:
                        scores(h + 1)
                    head_squares(h)

            def nsa_kv():
                token_major("kv", 2, KD, 0, "kvn")
                feature("kvc", 8, "kvn")
                pe.wait_ge(c_kn, 1)
                for b in range(4):
                    for tb in range(TB):
                        ins = pe.transpose(bank(6 + b // 2, b % 2 * S + tb * P, b % 2 * S + (tb + 1) * P),
                                           kn_tok[:, tb * 512 + b * P:tb * 512 + (b + 1) * P], ident)
                ins.then_inc(c_kt, 1)
                pe.wait_ge(c_loaded, 16 * 4)
                pe.wait_ge(out_read, OUT0["kvc"] + 8)
                for j in range(2):
                    for n in range(CBLOCK // 2):
                        w = w1c[j][:, n * P:(n + 1) * P]
                        blk = c_dup[j].rearrange("p (g s) -> p g s", g=G)[:, :, 2 * n:2 * n + CSTRIDE * (NC - 1) + 1:CSTRIDE]
                        pe.matmul(bank(j, 0, G * NC), w, blk, start=n == 0, stop=n == CBLOCK // 2 - 1)
                for j in range(2):
                    for n in range(CBLOCK // 2):
                        pe_col = VEC["pe_k" if j == 0 else "pe_v"] + n
                        ins = pe.matmul(bank(2, j, j + 1), w1c[j][:, n * P:(n + 1) * P], vec[:, pe_col:pe_col + 1],
                                        start=n == 0, stop=n == CBLOCK // 2 - 1)
                ins.then_inc(c_hd, 1)
                pe.wait_ge(c_gelu, 1)
                pe.wait_ge(c_kT, 2)
                pe.matmul(bank(6, 0, G * NC), w2c[0], c_hid[0], start=True, stop=True).then_inc(c_kc, 1)
                pe.wait_ge(c_gelu, 2)
                for g in range(G):
                    ins = pe.matmul(bank(7, g * DH, (g + 1) * DH, slice(0, NC)), c_hid[1][:, g * NC:(g + 1) * NC], w2c[1][:, 0:DH],
                                    start=True, stop=True)
                ins.then_inc(c_vcd, 1)
                pe.wait_ge(c_kcsqd, 1)
                pe.matmul(bank(3, 0, G * NC), const("blockdiag", 0, P), c_kcsq, start=True, stop=True).then_inc(c_kcss, 1)

            def nsa():
                narrow("ngate", 3 * H, "mid_1")
                token_major("nq", 2, KD)
                pe.wait_ge(out_read, OUT0["nq"] + 4)
                pe.wait_ge(c_end, 2)
                with pe.Fori(0, HG) as i:
                    def scores(u):
                        gp, br, e = u // 4, u // 2 % 2, u % 2
                        rows = slice(e * DH, (e + 1) * DH)
                        q = n_qT[rows, gp * S:(gp + 1) * S]
                        k = kT[rows, (br * 2 + gp) * S:(br * 2 + gp + 1) * S]
                        pe.wait_ge(n_lr, i * 8 + max(u - 1, 0))
                        pe.matmul(bank(1 + e, 0, P), q[:, 0:P], k[:, 0:P], start=True, stop=True)
                        pe.matmul(bank(1 + e, P, 3 * P), q[:, P:S], k, start=True, stop=True).then_inc(n_s, 1)

                    def turn_probs(u):
                        pe.wait_ge(n_exp, i * 16 + 2 * (u + 1))
                        for n in range(3):
                            ins = pe.transpose(bank(4 + u % 2, n * P, (n + 1) * P), n_p[u % 2][:, n * P:(n + 1) * P], ident)
                        ins.then_inc(n_pT, 1)

                    def values(u):
                        gp, br, e = u // 4, u // 2 % 2, u % 2
                        pe.wait_ge(n_pTd, i * 8 + (u + 1))
                        if u < 2:
                            pe.wait_ge(n_co, i + 1)
                        else:
                            pe.wait_ge(n_od, i * 8 + (u - 1))
                        b, pT = 6 + u % 2, n_pTs[u % 2]
                        v = [vtok[:, tb * 512 + br * S + (gp * 2 + e) * DH:][:, 0:DH] for tb in range(TB)]
                        pe.matmul(bank(b, 0, DH), pT[:, 0:P], v[0], start=True, stop=True)
                        pe.matmul(bank(b, DH, 2 * DH), pT[:, P:2 * P], v[0], start=True, stop=False)
                        pe.matmul(bank(b, DH, 2 * DH), pT[:, 2 * P:3 * P], v[1], start=False, stop=True).then_inc(n_pv, 1)

                    pe.wait_ge(n_st, i + 1)
                    for gp in range(2):
                        for tb in range(TB):
                            ins = pe.transpose(bank(0, gp * S + tb * P, gp * S + (tb + 1) * P),
                                               n_qs[:, (tb * 2 + gp) * P:(tb * 2 + gp + 1) * P], ident)
                    ins.then_inc(n_turn, 1)
                    pe.wait_ge(n_qTs, i + 1)
                    for w in range(4):
                        gp, e = w // 2, w % 2
                        rows = slice(e * DH, (e + 1) * DH)
                        for tb, c in enumerate((NC0, NC)):
                            first = w * 32 + tb * 8
                            ins = pe.matmul(bank(3 if e == 0 else 0, first, first + c), n_qT[rows, gp * S + tb * P:gp * S + (tb + 1) * P],
                                            kcT[rows, (2 * gp + e) * NC:(2 * gp + e) * NC + c], start=True, stop=True)
                    ins.then_inc(n_cs, 1)
                    scores(0)
                    scores(1)
                    pe.wait_ge(n_cexp, i + 1)
                    for w in range(4):
                        for tb, (a, c) in enumerate(((0, NC0), (4 * NC0, NC))):
                            first = w % 2 * S + tb * P
                            ins = pe.transpose(bank(4 + w // 2, first, first + P, slice(0, NC)), n_cl[:, a + w * c:a + w * c + NC], ident)
                    ins.then_inc(n_cT, 1)
                    pe.wait_ge(n_cTs, i * 2 + 2)
                    pe.wait_ge(n_od, i * 8)
                    for tb, c in enumerate((NC0, NC)):
                        for w in range(4):
                            g = w
                            first = tb * S + w * DH
                            ins = pe.matmul(bank(6, first, first + DH), n_cpT[0:c, w * S + tb * P:w * S + (tb + 1) * P],
                                            vc[0:c, g * DH:(g + 1) * DH], start=True, stop=True)
                    ins.then_inc(n_cpv, 1)
                    turn_probs(0)
                    for u in range(2, 8):
                        scores(u)
                        values(u - 2)
                        turn_probs(u - 1)
                    values(6)
                    turn_probs(7)
                    values(7)
                turn_outputs("o_n", no_tok, (n_end, HG))

            pe.wait_ge(loaded, 16 * 5)
            pe.wait_ge(const_ready, 4)
            pe.matmul(bank(6, 0, 2 * S, slice(0, H)), relb[:, :], const("onehot", 0, 2 * S, slice(0, BUCKETS + 1)), start=True, stop=True)\
              .then_inc(row_ready, 1)
            zero_stat(TB)
            pe.wait_ge(sq_ready, 1)
            for k in range(KD):
                ins = add_stat(0, ASQ[:, k * S:(k + 1) * S], k == KD - 1)
            ins.then_inc(stat_done, 1)
            norm("mix_0")
            mla()

            def after(event, first):
                return lambda c: (event, first + c + 1)

            residual("wo_a", 1, KD, xs, after(xs_ready, XS0["o_a"]))
            norm("ffn_0")
            feature("up_0", FF1, "ffn_0")
            residual("down_0", FF1 // BLK, FF1, hs, after(hs_ready, hid0["up_0"]))
            norm("mix_1")
            mlstm()
            residual("wo_m", 1, KD, xs, after(xs_ready, XS0["o_m"]))
            norm("ffn_1")
            feature("up_1", FF1, "ffn_1")
            residual("down_1", FF1 // BLK, FF1, hs, after(hs_ready, hid0["up_1"]))
            norm("pre_0")
            feature("glu_0", 2 * FF2, "pre_0")
            residual("out_0", FF2_TILES, FF2, hs, after(hs_ready, hid0["glu_0"]))
            norm("mid_0")
            feature("cin", 3 * KD, "mid_0")
            residual("cout", 1, KD, hs, after(hs_ready, hid0["cin"]))
            norm("post_0")
            feature("glu_1", 2 * FF2, "post_0")
            residual("out_1", FF2_TILES, FF2, hs, after(hs_ready, hid0["glu_1"]))
            norm("kvn")
            nsa_kv()
            feature("glu_2", 2 * FF2, "pre_1")
            residual("out_2", FF2_TILES, FF2, hs, after(hs_ready, hid0["glu_2"]))
            norm("mid_1")
            nsa()
            residual("wo_n", 1, KD, xs, after(xs_ready, XS0["o_n"]))
            norm("post_1")
            feature("glu_3", 2 * FF2, "post_1")
            residual("out_3", FF2_TILES, FF2, hs, after(hs_ready, hid0["glu_3"]))


def feature_tiles(w):
    k, m = w.shape[0] // P, w.shape[1] // P
    per = -(-k // BLK)
    out = np.zeros((m, P, per * BLK, P), np.float32)
    out[:, :, :k] = w.reshape(k, P, m, P).transpose(2, 1, 0, 3)
    return out.reshape(m, P, per, TILE).transpose(0, 2, 1, 3).reshape(m * per, P, TILE)


def token_tiles(w):
    k, g = w.shape[0] // P, w.shape[1] // 512
    out = np.zeros((-(-k * g // 2) * 2, P, 512), np.float32)
    out[:k * g] = w.reshape(k, P, g, 512).transpose(2, 0, 1, 3).reshape(k * g, P, 512)
    return out.reshape(-1, 2, P, 512).transpose(0, 2, 1, 3).reshape(-1, P, TILE)


def narrow_tile(w):
    out = np.zeros((P, KD, P), np.float32)
    out[:, :, :w.shape[1]] = w.reshape(KD, P, -1).transpose(1, 0, 2)
    return out.reshape(1, P, TILE)


def interleave(*ws):
    k = ws[0].shape[0]
    return np.stack([w.reshape(k, -1, P) for w in ws], axis=2).reshape(k, -1)


_OUT = ((D, S), "float32")


def kernel(**inputs):
    import concourse.bacc as bacc
    from concourse.bass_utils import run_bass_kernel_spmd

    a = {n: np.asarray(v) for n, v in inputs.items()}
    heads = np.array([(2 * gp + e) * HG + hg for gp in range(2) for hg in range(HG) for e in range(2)])
    w_ukv = a["mla_w_ukv"][0].reshape(KV_RANK, H, NOPE + VD)
    w_dkv = a["mla_w_dkv"][0]
    m_in, w_if = a["mlstm_w_in"][0], a["mlstm_w_if"][0]
    mqk = 2 * MH * MQK
    kv = a["w_kv_2"].reshape(D, 3, 2, G, DH)
    wq = a["attn_w_q_2"][0]
    glu, out, mlp1, mlp2 = {}, {}, a["ffn_w1"], a["ffn_w2"]
    for n, (which, layer) in enumerate((("ffn1", 0), ("ffn2", 0), ("ffn1", 1), ("ffn2", 1))):
        w = a[f"{which}_w_in_2"][layer]
        glu[n] = feature_tiles(interleave(w[:, :FF2 * P], w[:, FF2 * P:]))
        out[n] = feature_tiles(a[f"{which}_w_out_2"][layer])
    w_cin = a["conv_w_in_2"][0]
    stream = [
        feature_tiles(a["mla_w_dq"][0]), feature_tiles(w_dkv[:, :KV_RANK]), narrow_tile(w_dkv[:, KV_RANK:]),
        token_tiles(a["mla_w_uq"][0]), token_tiles(w_ukv[:, :, :NOPE].reshape(KV_RANK, -1)),
        token_tiles(w_ukv[:, :, NOPE:].reshape(KV_RANK, -1)), feature_tiles(a["mla_w_o"][0]),
        feature_tiles(mlp1[0]), feature_tiles(mlp2[0]),
        narrow_tile(w_if[:, :MH]), narrow_tile(w_if[:, MH:]), feature_tiles(m_in[:, :mqk]),
        token_tiles(m_in[:, mqk:mqk + MH * MV]), feature_tiles(m_in[:, mqk + MH * MV:]), feature_tiles(a["mlstm_w_o"][0]),
        feature_tiles(mlp1[1]), feature_tiles(mlp2[1]),
        glu[0], out[0], feature_tiles(interleave(w_cin[:, :D], w_cin[:, D:2 * D], w_cin[:, 2 * D:])),
        feature_tiles(a["conv_w_out_2"][0]), glu[1], out[1],
        token_tiles(kv[:, 1:, :, :, :].transpose(0, 2, 1, 3, 4).reshape(D, -1)),
        feature_tiles(np.stack([kv[:, 0], kv[:, 0]], axis=3).reshape(D, -1)), glu[2], out[2],
        narrow_tile(wq[:, H * DH:].reshape(D, H, 3)[:, heads].reshape(D, -1)),
        token_tiles(wq[:, :H * DH].reshape(D, H, DH)[:, heads].reshape(D, -1)),
        feature_tiles(a["attn_w_o_2"][0].reshape(H, DH, D)[heads].reshape(D, D)), glu[3], out[3],
    ]
    tiles = np.concatenate(stream)
    assert tiles.shape[0] == N_TILES

    vecs = np.zeros((P, N_VEC), np.float32)

    def put(name, v):
        v = v.reshape(-1, min(P, v.shape[-1])).T
        vecs[:v.shape[0], VEC[name]:VEC[name] + v.shape[1]] = v

    for name, v in (("mix_0", a["norm_mix"][0]), ("ffn_0", a["norm_ffn"][0]), ("mix_1", a["norm_mix"][1]), ("ffn_1", a["norm_ffn"][1]),
                    ("pre_0", a["ffn1_norm_2"][0]), ("mid_0", a["mix_norm_2"][0]), ("post_0", a["ffn2_norm_2"][0]),
                    ("kvn", a["kv_norm_2"]), ("pre_1", a["ffn1_norm_2"][1]), ("mid_1", a["mix_norm_2"][1]),
                    ("post_1", a["ffn2_norm_2"][1]), ("q_norm", a["mla_q_norm"][0]), ("kv_norm", a["mla_kv_norm"][0]),
                    ("head_norm", a["mlstm_head_norm"][0]), ("taps", a["conv_w_2"][0].reshape(-1)),
                    ("kc_norm", np.concatenate([a["k_norm_2"][0]] * 2)), ("b_i", a["mlstm_b_if"][0][:MH]),
                    ("b_f", a["mlstm_b_if"][0][MH:]), ("pe_k", a["cmp_pe_k_2"].reshape(-1)), ("pe_v", a["cmp_pe_v_2"].reshape(-1))):
        put(name, v)
    rows = np.concatenate([a["mla_q_gain"][0], a["mla_k_gain"][0], a["attn_q_norm_2"][0], a["k_norm_2"][1], a["k_norm_2"][2]])
    w2 = [np.concatenate([a[n]] * 2, axis=1) for n in ("cmp_w2_k_2", "cmp_w2_v_2")]
    arrays = {
        "x_in": np.ascontiguousarray(a["x"][0].T), "tiles": tiles, "vecs": vecs, "rows": rows, "consts": constants(),
        "rel_bias": np.ascontiguousarray(a["rel_bias_2"][:, heads]), "w1c_k": a["cmp_w1_k_2"], "w1c_v": a["cmp_w1_v_2"],
        "w2c_k": w2[0], "w2c_v": w2[1],
    }
    nc = bacc.Bacc("TRN2", target_bir_lowering=False, num_devices=1)
    args = [nc.dram_tensor(n, v.shape, mybir.dt.from_np(v.dtype), kind="ExternalInput").ap() for n, v in arrays.items()]
    y = nc.dram_tensor("y_out", _OUT[0], F32, kind="ExternalOutput").ap()
    build(nc, *args, y)
    r = run_bass_kernel_spmd(nc, [arrays], core_ids=[0])
    return np.ascontiguousarray(r.results[0]["y_out"].T)[None]
```

```python
from contextlib import ExitStack

import numpy as np

import concourse.bass as bass
from concourse import mybir

F32 = mybir.dt.float32
F32R = mybir.dt.float32r
ACT = mybir.ActivationFunctionType
ALU = mybir.AluOpType
AX_X = mybir.AxisListType.X

P = 128
S = 256
TB = S // P
D = 1024
KD = D // P
BLK = 8
TILE = BLK * P
RING = 4
BANK = 512
EPS = 1e-6
NEG = -1e30

Q_RANK, KV_RANK = 384, 256
H, NOPE, ROPE, VD = 16, 64, 32, 64
QK = NOPE + ROPE
HALF = ROPE // 2
KQ, KKV = Q_RANK // P, KV_RANK // P

MH, MQK, MV = 4, 128, 256
GATE_CAP = 15.0

FF1 = 4096 // P
FF2 = 2816 // P
FF2_TILES = -(-FF2 // BLK)
TAPS = 3

G, HG, DH = 4, 4, 64
NC, CSTRIDE, CBLOCK = 15, 16, 32
NC0 = 7
BUCKETS = 32

STAGES = [
    ("dq", 3, 3), ("dkv", 2, 2), ("kr", 1, 2), ("uq", 5, 6), ("uk", 2, 4), ("uv", 2, 4), ("wo_a", 8, 8),
    ("up_0", 32, 32), ("down_0", 32, 8),
    ("mgate", 2, 2), ("mqk", 8, 8), ("mv", 8, 4), ("mo", 8, 8), ("wo_m", 8, 8),
    ("up_1", 32, 32), ("down_1", 32, 8),
    ("glu_0", 44, 44), ("out_0", 24, 8), ("cin", 24, 24), ("cout", 8, 8), ("glu_1", 44, 44), ("out_1", 24, 8),
    ("kv", 8, 4), ("kvc", 8, 8), ("glu_2", 44, 44), ("out_2", 24, 8),
    ("ngate", 1, 2), ("nq", 8, 4), ("wo_n", 8, 8), ("glu_3", 44, 44), ("out_3", 24, 8),
]
TILE0, OUT0 = {}, {}
N_TILES = N_OUTS = 0
for _name, _tiles, _outs in STAGES:
    TILE0[_name], OUT0[_name] = N_TILES, N_OUTS
    N_TILES, N_OUTS = N_TILES + _tiles, N_OUTS + _outs

VEC = {}
N_VEC = 0
for _name, _n in [("mix_0", 8), ("ffn_0", 8), ("mix_1", 8), ("ffn_1", 8), ("pre_0", 8), ("mid_0", 8), ("post_0", 8),
                  ("kvn", 8), ("pre_1", 8), ("mid_1", 8), ("post_1", 8), ("q_norm", KQ), ("kv_norm", KKV),
                  ("head_norm", 8), ("taps", TAPS * KD), ("kc_norm", 1), ("nq_norm", 1), ("b_i", 1), ("b_f", 1),
                  ("pe_k", 16), ("pe_v", 16)]:
    VEC[_name] = N_VEC
    N_VEC += _n
ROW = {"q_gain": 0, "k_gain": QK, "nq": 2 * QK, "ks": 2 * QK + DH, "kw": 2 * QK + 2 * DH}
N_ROW = 2 * QK + 3 * DH
COPIES = 16
CONST = {}
N_CONST = 0
for _name, _n in [("ident", P), ("blockdiag", P), ("causal", P), ("select", MH * P), ("onehot", 2 * S), ("cos", TB * HALF),
                  ("sin", TB * HALF), ("valid", TB), ("chunk_u", P), ("chunk_v", P), ("groups", G)]:
    CONST[_name] = N_CONST
    N_CONST += _n


def constants():
    c = np.zeros((P, N_CONST), np.float32)

    def put(name, a):
        c[:a.shape[0], CONST[name]:CONST[name] + a.shape[1]] = a

    put("ident", np.eye(P))
    put("blockdiag", np.kron(np.eye(2), np.ones((DH, DH))))
    put("causal", np.triu(np.ones((P, P))))
    put("select", np.kron(np.eye(MH), np.ones((1, P))))
    rel = S - 1 - np.arange(2 * S)
    n = np.maximum(rel, 0)
    exact, most = BUCKETS // 2, 4096
    nf = np.maximum(n, 1).astype(np.float32)
    large = exact + (np.log(nf / np.float32(exact)) / np.float32(np.log(most / exact))
                     * np.float32(BUCKETS - exact)).astype(np.int32)
    bucket = np.where(n < exact, n, np.minimum(large, BUCKETS - 1))
    hot = np.zeros((BUCKETS + 1, 2 * S))
    hot[bucket, np.arange(2 * S)] = rel >= 0
    hot[BUCKETS] = np.where(rel < 0, NEG, 0.0)
    put("onehot", hot)
    freq = np.float32(10000.0) ** (-np.arange(HALF, dtype=np.float32) / np.float32(HALF))
    ang = (np.arange(S, dtype=np.float32)[:, None] * freq[None, :]).astype(np.float32)
    for name, f in (("cos", np.cos), ("sin", np.sin)):
        put(name, f(ang).reshape(TB, P, HALF).transpose(1, 0, 2).reshape(P, TB * HALF))
    put("valid", (np.arange(S) >= CBLOCK - 1).astype(np.float32).reshape(TB, P).T)
    put("groups", np.kron(np.eye(G), np.ones((NC, 1))))
    put("chunk_u", (np.arange(P) < 64)[None, :].astype(np.float32))
    put("chunk_v", np.where(np.arange(P) >= 64, NEG, 0.0)[None, :])
    return c


def build(nc, x_in, tiles, vecs, rows, consts, rel_bias, w1c_k, w1c_v, w2c_k, w2c_v, y_out):
    ctx = ExitStack()
    with ctx:
        def sb(name, shape, dt=F32):
            return ctx.enter_context(nc.sbuf_tensor(name, shape, dt))

        def sem(name):
            return ctx.enter_context(nc.semaphore(name))

        raw = [sb(f"raw{s}", [P, TILE]) for s in range(RING)]
        w_hi = [sb(f"w_hi{s}", [P, TILE], F32R) for s in range(RING)]
        w_lo = [sb(f"w_lo{s}", [P, TILE], F32R) for s in range(RING)]
        x = sb("x", [P, KD * S])
        with nc.sbuf_tensor("w1c_all", [P, 2 * 16 * P], F32) as w1c_all:
            pass
        xs = sb("xs", [P, KD * 2 * S], F32R)
        half = [sb(f"half{s}", [P, S]) for s in range(4)]
        fsum = [sb(f"fsum{s}", [P, S]) for s in range(4)]
        sq = [sb(f"sq{s}", [P, S]) for s in range(4)]
        sil = [sb(f"sil{s}", [P, S]) for s in range(2)]
        vec = sb("vec", [P, N_VEC])
        row = sb("row", [P, N_ROW])
        con = sb("con", [P, N_CONST])
        ones = sb("ones", [P, P])
        eps = sb("eps", [P, 1])
        std = sb("std", [P, 64])
        rstd = sb("rstd", [P, 64])
        ssq = sb("ssq", [P, S])
        stdb = sb("stdb", [P, S])
        rb = sb("rb", [P, S])
        with nc.sbuf_tensor("os", [P, KD * 2 * S], F32R) as os_:
            pass
        bias = sb("bias", [P, H * S])
        relb = sb("relb", [BUCKETS + 1, H])
        bias_row = sb("bias_row", [H, 2 * S])
        kT = sb("kT", [P, 4 * S])
        vtok = sb("vtok", [P, TB * 2 * G * DH])
        kcT = sb("kcT", [P, G * NC])
        vc = sb("vc", [G * NC, G * DH])
        with nc.sbuf_tensor("hs", [P, FF1 * 2 * S], F32R) as hs:
            pass
        arena = sb("arena", [P, FF1 * 2 * S])

        def part(at, n):
            return arena[:, at:at + n]

        psum = ctx.enter_context(nc.psum_tensor("psum", [P, 8 * BANK], F32))

        def bank(b, a=0, z=BANK, p=slice(None)):
            return psum[p, b * BANK + a:b * BANK + z]

        def const(name, a, z, p=slice(None)):
            at = CONST[name]
            return con[p, at + a:at + z]

        ident = const("ident", 0, P)
        STAT, RB = 4, 5

        tile_loaded = [sem(f"tile_loaded{s}") for s in range(RING)]
        hi_ready, lo_ready = sem("hi_ready"), sem("lo_ready")
        tile_done = sem("tile_done")
        out_read = sem("out_read")
        half_ready = sem("half_ready")
        x_loaded, loaded = sem("x_loaded"), sem("loaded")
        scaled = sem("scaled")
        const_ready = sem("const_ready")
        ssq_ready = sem("ssq_ready")
        stat_done, std_ready = sem("stat_done"), sem("std_ready")
        sq_ready = sem("sq_ready")
        xhi_ready, xs_ready = sem("xhi_ready"), sem("xs_ready")
        hid_ready, hhi_ready, hs_ready = sem("hid_ready"), sem("hhi_ready"), sem("hs_ready")
        sil_ready = sem("sil_ready")
        x_half = sem("x_half")
        dve_step = sem("dve_step")
        stored = sem("stored")
        row_ready = sem("row_ready")
        bias_done, bias_out, bias_in = sem("bias_done"), sem("bias_out"), sem("bias_in")
        head_sq, head_sum, head_std = sem("head_sq"), sem("head_sum"), sem("head_std")
        a_st, a_turn, a_qkT, a_s, a_max, a_exp = (sem(f"a_{n}") for n in ("st", "turn", "qkT", "s", "max", "exp"))
        a_pT, a_pTs, a_pv, a_o = (sem(f"a_{n}") for n in ("pT", "pTs", "pv", "o"))
        o_turn = {n: sem(f"turn_{n}") for n in ("o_a", "o_n")}
        m_gates, m_out = sem("m_gates"), sem("m_out")
        m_tanh, m_rows, m_floor, m_bcd, m_st, m_logw, m_exp, m_ptd = (
            sem(f"m_{n}") for n in ("tanh", "rows", "floor", "bcd", "st", "logw", "exp", "ptd"))
        m_dend, m_absd, m_num, m_hc, m_sqd, m_ss, m_stdd, m_sig, m_at, m_ac = (
            sem(f"m_{n}") for n in ("dend", "absd", "num", "hc", "sqd", "ss", "stdd", "sig", "at", "ac"))
        c_loaded, c_sqd, c_sum, c_std, c_bias, c_gelu, c_kc, c_kcsqd, c_kcss, c_kcstdd = (
            sem(f"c_{n}") for n in ("loaded", "sqd", "sum", "std", "bias", "gelu", "kc", "kcsqd", "kcss", "kcstdd"))
        c_kn, c_kt, c_kT, c_hd, c_vcd, c_end = (sem(f"c_{n}") for n in ("kn", "kt", "kT", "hd", "vcd", "end"))
        n_sig, n_sqd, n_sum, n_std_, n_turn, n_qTd, n_cs, n_clog, n_cexp, n_cT, n_cTs, n_cpv, n_co = (
            sem(f"n_{n}") for n in ("sig", "sqd", "sum", "std", "turn", "qTd", "cs", "clog", "cexp", "cT", "cTs", "cpv", "co"))
        n_zero = sem("n_zero")
        n_q, n_s, n_log, n_max, n_exp, n_pT, n_pTd, n_pv, n_od = (
            sem(f"n_{n}") for n in ("q", "s", "log", "max", "exp", "pT", "pTd", "pv", "od"))

        half0, hid0, sil0, n_half, n_hid, n_sil = {}, {}, {}, 0, 0, 0
        for name, _, outs in STAGES:
            half0[name], hid0[name], sil0[name] = n_half, n_hid, n_sil
            kind = name.split("_")[0]
            if kind in ("dq", "dkv", "up", "mgate", "mqk", "mo", "glu", "cin", "kvc"):
                n_half += outs
            n_hid += {"up": outs, "glu": outs // 2, "cin": outs // 3}.get(kind, 0)
            n_sil += {"glu": outs // 2}.get(kind, 0)
        RES = [n for n, _, _ in STAGES if n.split("_")[0] in ("wo", "down", "out", "cout")]

        class Steps:

            def __init__(self):
                self.base, self.n = 0, 0

            def mark(self, ins):
                ins.then_inc(dve_step, 1)
                self.n += 1
                return self.base + self.n

        def at(t, start, n):
            return t[:, start:start + n] if isinstance(start, int) else t[:, bass.ds(start, n)]

        def x_chunks():
            return [x[:, k * S:(k + 1) * S] for k in range(KD)]

        cqf = part(0, (KQ + KKV) * S)
        q_tok = part(2048, TB * H * QK)
        k_tok = part(2048 + 3072, TB * H * NOPE)
        v_tok = part(2048 + 5120, TB * H * VD)
        o_tok = part(0, TB * H * VD)
        kr_tok = part(9216, TB * ROPE)
        ss = part(9280, 4 * H + 2)
        rope_t = part(9408, 4 * TB * H * HALF)
        mscr = [part(11456 + 1024 * j, 1024) for j in range(2)]
        HEAD_SQ = [(q_tok[:, j * 768:(j + 1) * 768], 768) for j in range(2 * TB)]
        HEAD_SQ += [(k_tok[:, j * 1024:(j + 1) * 1024], 1024) for j in range(TB)] + [(kr_tok, TB * ROPE)]
        q_st = part(11456, TB * 4 * QK)
        k_st = part(11456 + 768, TB * 4 * QK)
        qkT = [part(12992 + 512 * j, 512) for j in range(2)]
        prob = [part(14016 + 384 * j, 384) for j in range(2)]
        probT = [part(14784 + 384 * j, 384) for j in range(2)]
        mx = part(15552, 16)
        nmx = part(15568, 16)
        rsum = part(15584, 16)
        rinv = part(15600, 16)

        chunk_u = sb("chunk_u", [1, P], F32R)
        chunk_v = sb("chunk_v", [1, P], F32R)
        mla_mask = (chunk_u, chunk_v)
        ASQ = part(2048, KD * S)

        conv_b = [part(KD * 512 + j * S, S) for j in range(2)]
        conv_c = [part(KD * 512 + (2 + j) * S, S) for j in range(2)]
        conv_v = [part(KD * 512 + (4 + j) * S, S) for j in range(2)]
        conv_y = [part(KD * 512 + (6 + j) * S, S) for j in range(2)]
        conv_u = [part(KD * 512 + 8 * S + j * 2 * S, S + TAPS - 1) for j in range(2)]

        m_qk = part(0, 2 * MH * S)
        m_v = part(2048, TB * MH * MV)
        m_o = part(4096, KD * S)
        m_row = [arena[0:MH, 6144 + j * S:6144 + (j + 1) * S] for j in range(6)]
        m_ti, m_tf, m_nb, m_a, m_g, m_one = m_row
        m_bc = arena[0:MH, 7680:7680 + 2 * S]
        m_acol = part(8192, TB * MH)
        m_w = [part(8320 + 384 * j, 384) for j in range(2)]
        m_pt = [part(9088 + 384 * j, 384) for j in range(2)]
        m_den = [part(9856 + S * j, S) for j in range(2)]
        m_fl = [part(10368 + S * j, S) for j in range(2)]
        m_h = [part(10880 + 512 * j, 512) for j in range(2)]
        m_sq = [part(11904 + 512 * j, 512) for j in range(2)]
        m_std = part(12928, S)
        m_r = part(13184, S)

        w1c = [w1c_all[:, 16 * P * j:16 * P * (j + 1)] for j in range(2)]
        c_at = FF2 * 2 * S
        w2c = [part(c_at + P * j, P) for j in range(2)]
        c_dup = [part(c_at + 256 + (G + 1) * S * j, (G + 1) * S) for j in range(2)]
        kn_tok = part(c_at + 2816, TB * 2 * G * DH)
        c_sq = [part(c_at + 3840 + 512 * j, 512) for j in range(2)]
        c_ss = part(c_at + 4864, 16)
        c_r = part(c_at + 4880, 16)
        c_pe = part(c_at + 4896, 2)
        c_hid, c_kcsq, c_kcstd, c_kcr = ([part(c_at + 3840 + 64 * j, G * NC) for j in range(2)],
                                         *(part(c_at + 3840 + 64 * j, G * NC) for j in (2, 3, 4)))

        nq_tok = part(0, TB * D)
        no_tok = part(2048, TB * D)
        n_gate = part(4096, TB * 3 * H)
        n_sq = part(4224, TB * 512)
        n_r = part(6272, TB * H)
        n_ss = part(6304, TB * H)
        n_qTa = part(6336, 2 * D)
        n_qT = [[part(14720 + S * (2 * j + e), S) for e in range(2)] for j in range(2)]
        n_l = [part(8896 + 768 * j, 768) for j in range(2)]
        n_p = [part(10432 + 768 * j, 768) for j in range(2)]
        n_pTs = [part(11968 + 768 * j, 768) for j in range(2)]
        n_mx, n_nmx, n_rs, n_sc = ([part(13504 + 16 * j + 4 * w, 4) for w in range(4)] for j in range(4))
        n_cl = [part(13568 + H * NC * tb, H * NC) for tb in range(TB)]
        n_cmx, n_crs, n_csc = (part(14048 + TB * H * j, TB * H) for j in range(3))
        n_cpT = arena[0:G * NC, 14144:14144 + 2 * S]

        NORMS = ["mix_0", "cq", "ffn_0", "mix_1", "ffn_1", "pre_0", "mid_0", "post_0", "kvn", "mid_1", "post_1"]
        NEXT = dict(zip(RES, NORMS[2:]))
        TO_ROWS = [n for n in NORMS if n not in ("cq", "mid_1")]
        TO_COLUMNS = ["mix_0", "cq", "mix_1", "kvn", "mid_1"]
        SUMS = [n for n in NORMS if n != "cq"]
        STAT0 = {n: j + 1 for j, n in enumerate(NORMS)}
        SSQ0 = {n: (KD + 1) * j for j, n in enumerate(SUMS)}
        STD0, n_std = {}, 0
        for name in NORMS:
            n_std += (name in TO_ROWS) + (name in TO_COLUMNS) + (name == "cq")
            STD0[name] = n_std
        XS0, n_xs = {}, 0
        for name in ["mix_0", "cq", "o_a", "ffn_0", "mix_1", "o_m", "ffn_1", "pre_0", "mid_0", "post_0", "kvn", "pre_1", "mid_1",
                     "o_n", "post_1"]:
            XS0[name] = n_xs
            n_xs += KQ + KKV if name == "cq" else KD
        SQ0 = {"mix_0": 0, "cq": KD} | {name: KD + 1 + KD * j for j, name in enumerate(RES)}

        def hi_part(t, k):
            return t[:, k * 2 * S:k * 2 * S + S]

        def lo_part(t, k):
            return t[:, k * 2 * S + S:(k + 1) * 2 * S]

        bias_dram = nc.dram_tensor("bias_dram", (H, COPIES, 2 * S), F32, kind="Internal").ap()
        block = ctx.enter_context(nc.Block())

        @block.sync
        def _(sp):
            sp.dma_start(x[:, :].rearrange("p (k t) -> p k t", k=KD), x_in.rearrange("(k p) t -> p k t", p=P)).then_inc(x_loaded, 16)
            sp.dma_start(vec[:, :], vecs).then_inc(x_loaded, 16)
            for s in range(RING):
                sp.dma_start(raw[s][:, :], tiles[s]).then_inc(tile_loaded[s], 16)
            sp.dma_start(con[:, :], consts).then_inc(loaded, 16)
            sp.dma_start(row[:, :], rows.partition_broadcast(P)).then_inc(loaded, 16)
            sp.dma_start(relb[0:BUCKETS, :], rel_bias).then_inc(loaded, 16)
            with sp.Fori(1, N_TILES // RING) as i:
                for s in range(RING):
                    sp.wait_ge(lo_ready, i * RING + (s + 1 - RING))
                    sp.dma_start(raw[s][:, :], tiles[bass.ds(i * RING + s, 1)].rearrange("o p n -> p (o n)")).then_inc(tile_loaded[s], 16)
            for t in range(N_TILES // RING * RING, N_TILES):
                s = t % RING
                sp.wait_ge(lo_ready, t + 1 - RING)
                sp.dma_start(raw[s][:, :], tiles[t]).then_inc(tile_loaded[s], 16)
            for k in range(KD):
                sp.wait_ge(out_read, OUT0["out_3"] + k + 1)
                sp.dma_start(y_out[k * P:(k + 1) * P, :], x[:, k * S:(k + 1) * S]).then_inc(stored, 16)
            sp.wait_ge(stored, 16 * KD)
            sp.wait_ge(bias_out, 16)

        @block.gpsimd
        def _(pool):
            pool.memset(ones[:, :], 1.0).then_inc(const_ready, 1)
            pool.memset(eps[:, :], EPS).then_inc(const_ready, 1)
            pool.wait_ge(const_ready, 2)
            pool.memset(relb[BUCKETS:BUCKETS + 1, :], 1.0).then_inc(const_ready, 1)
            pool.wait_ge(const_ready, 3)

            def take_lo(s, t):
                pool.wait_ge(hi_ready, t + 1)
                pool.tensor_tensor(w_lo[s][:, :], raw[s][:, :], w_hi[s][:, :].bitcast(F32), ALU.subtract).then_inc(lo_ready, 1)

            with pool.Fori(0, N_TILES // RING) as i:
                for s in range(RING):
                    take_lo(s, i * RING + s)
            for t in range(N_TILES // RING * RING, N_TILES):
                take_lo(t % RING, t)

        @block.scalar
        def _(act):
            def split(t, q=0):
                if isinstance(q, int) and t + RING * q >= N_TILES:
                    return
                s = t % RING
                act.wait_ge(tile_loaded[s], (q + (t // RING + 1)) * 16)
                if t >= RING:
                    act.wait_ge(tile_done, q * RING + (t + 1 - RING))
                act.activation(w_hi[s][:, :], raw[s][:, :], ACT.Copy).then_inc(hi_ready, 1)

            def take_half(name, b, o, t, q=0, p=slice(None)):
                act.wait_ge(tile_done, t + 1)
                if not (isinstance(o, int) and OUT0[name] + o < 4):
                    act.wait_ge(out_read, o + (OUT0[name] - 3))
                act.activation(half[b][p, :], bank(b, S, 2 * S, p), ACT.Copy).then_inc(half_ready, 1)

            def root(name):
                act.wait_ge(stat_done, STAT0[name])
                if name in TO_ROWS:
                    act.activation(stdb[:, :], bank(RB, 0, S), ACT.Sqrt, bias=eps[:, 0:1], scale=1.0 / D).then_inc(std_ready, 1)
                if name in TO_COLUMNS:
                    for col, size in [(4, Q_RANK), (6, KV_RANK)] if name == "cq" else [(0, D)]:
                        act.activation(std[:, col:col + TB], bank(STAT, col, col + TB), ACT.Sqrt, bias=eps[:, 0:1],
                                       scale=1.0 / size).then_inc(std_ready, 1)

            def split_x(dst, src, gain):
                act.activation(dst, src, ACT.Copy, scale=gain).then_inc(xhi_ready, 1)

            def plain(name, outs, p=slice(None)):
                for o in range(outs):
                    t = TILE0[name] + o
                    take_half(name, (OUT0[name] + o) % 4, o, t, p=p)
                    split(t + RING)

            def used(name, tiles_):
                for t in range(TILE0[name], TILE0[name] + tiles_):
                    split(t + RING)

            def residual(name, per, outs=KD):
                t0, o0 = TILE0[name], OUT0[name]
                last = name == RES[-1]
                gain = 0 if last else VEC[NEXT[name]]

                def four(i):
                    for u in range(4):
                        for j in range(per):
                            split(t0 + u * per + j + RING, i * per)
                        if not last:
                            act.wait_ge(out_read, i * 4 + (o0 + u + 1))
                            split_x(at(xs, i * (8 * S) + u * 2 * S, S), at(x, i * (4 * S) + u * S, S), at(vec, i * 4 + (gain + u), 1))
                            act.activation(sq[u][:, :], at(x, i * (4 * S) + u * S, S), ACT.Square).then_inc(sq_ready, 1)
                if last:
                    for i in range(outs // 4):
                        four(i)
                else:
                    with act.Fori(0, outs // 4) as i:
                        four(i)

            def up(name):
                t0, o0 = TILE0[name], OUT0[name]
                with act.Fori(0, FF1 // 4) as i:
                    for u in range(4):
                        take_half(name, (o0 + u) % 4, i * 4 + u, i * 4 + (t0 + u))
                        split(t0 + u + RING, i)
                        act.wait_ge(hid_ready, i * 4 + (hid0[name] + u + 1))
                        act.activation(at(hs, i * (8 * S) + u * 2 * S, S), fsum[(o0 + u) % 4][:, :], ACT.Copy).then_inc(hhi_ready, 1)

            def glu(name, between=None):
                t0, o0 = TILE0[name], OUT0[name]
                between = between or {}

                def four(i):
                    for u in range(4):
                        take_half(name, (o0 + u) % 4, i * 4 + u, i * 4 + (t0 + u))
                        split(t0 + u + RING, i)
                        if u % 2 == 0:
                            act.wait_ge(scaled, i * 4 + (half0[name] + u + 1))
                            act.activation(sil[u // 2][:, :], fsum[(o0 + u) % 4][:, :], ACT.Silu).then_inc(sil_ready, 1)
                        else:
                            act.wait_ge(hid_ready, i * 2 + (hid0[name] + u // 2 + 1))
                            act.activation(at(hs, i * (4 * S) + (u // 2) * 2 * S, S), fsum[(o0 + u) % 4][:, :],
                                           ACT.Copy).then_inc(hhi_ready, 1)
                        if isinstance(i, int) and i * 4 + u in between:
                            between[i * 4 + u]()

                peeled = max(between, default=-1) // 4 + 1
                for i in range(peeled):
                    four(i)
                with act.Fori(peeled, FF2 // 2) as i:
                    four(i)

            def conv():
                name = "cin"
                t0, o0 = TILE0[name], OUT0[name]
                with act.Fori(0, KD // 4) as i:
                    for u in range(12):
                        take_half(name, (o0 + u) % 4, i * 12 + u, i * 12 + (t0 + u))
                        split(t0 + u + RING, i * 3)
                        if u % 3 == 2:
                            m = u // 3
                            act.wait_ge(hid_ready, i * 4 + (hid0[name] + m + 1))
                            act.activation(at(hs, i * (8 * S) + m * 2 * S, S), conv_y[m % 2], ACT.Copy).then_inc(hhi_ready, 1)

            def mla():
                root("mix_0")
                plain("dq", 3)
                plain("dkv", 2)
                used("kr", 1)
                for k in range(KQ + KKV):
                    act.wait_ge(scaled, half0["dq"] + k + 1)
                    gain = VEC["q_norm"] + k if k < KQ else VEC["kv_norm"] + k - KQ
                    split_x(hi_part(os_, k), cqf[:, k * S:(k + 1) * S], vec[:, gain:gain + 1])
                act.activation(ASQ[:, 0:(KQ + KKV) * S], cqf, ACT.Square).then_inc(sq_ready, 1)
                root("cq")
                used("uq", 5)
                used("uk", 2)
                used("uv", 2)
                act.wait_ge(out_read, OUT0["uv"] + 4)
                for n, (src, w) in enumerate(HEAD_SQ):
                    if n >= 2:
                        act.wait_ge(head_sum, n - 1)
                    act.activation(mscr[n % 2][:, 0:w], src, ACT.Square).then_inc(head_sq, 1)
                act.wait_ge(head_sum, len(HEAD_SQ) + 1)
                act.activation(std[:, 0:4 * H], ss[:, 0:4 * H], ACT.Sqrt, bias=eps[:, 0:1], scale=1.0 / QK).then_inc(head_std, 1)
                scale = QK ** -0.5
                with act.Fori(0, H // 4) as i:
                    act.wait_ge(a_pv, i * 4)

                    def turned(h):
                        act.wait_ge(a_turn, i * 4 + (h + 1))
                        act.activation(qkT[h % 2][0:QK, :], bank(h % 2, 0, 512, slice(0, QK)), ACT.Copy).then_inc(a_qkT, 1)

                    def exps(h):
                        act.wait_ge(a_max, i * 4 + (h + 1))
                        for tb, (a, z) in enumerate([(0, P), (P, 3 * P)]):
                            ins = act.activation(prob[h % 2][:, a:z], bank(2 + h % 2, a, z), ACT.Exp, scale=scale,
                                                 bias=nmx[:, 2 * h + tb:2 * h + tb + 1],
                                                 accum_out=rsum[:, 2 * h + tb:2 * h + tb + 1])
                            ins.then_inc(a_exp, 1)

                    def probs_turned(h):
                        act.wait_ge(a_pT, i * 4 + (h + 1))
                        if h >= 2:
                            act.wait_ge(a_pv, i * 4 + (h - 1))
                        act.activation(probT[h % 2], bank(4 + h % 2, 0, 384), ACT.Copy).then_inc(a_pTs, 1)

                    turned(0)
                    turned(1)
                    exps(0)
                    turned(2)
                    probs_turned(0)
                    exps(1)
                    turned(3)
                    probs_turned(1)
                    exps(2)
                    probs_turned(2)
                    exps(3)
                    probs_turned(3)
                out_hi("o_a")

            def out_hi(name):
                for k in range(KD):
                    act.wait_ge(o_turn[name], k + 1)
                    act.activation(hi_part(os_, k), bank(5 + k % 3, 0, S), ACT.Copy).then_inc(xhi_ready, 1)

            def mlstm():
                root("mix_1")
                plain("mgate", 2, p=slice(0, MH))
                plain("mqk", 8)
                act.wait_ge(m_gates, 2)
                act.activation(m_ti, m_ti, ACT.Tanh, scale=1.0 / GATE_CAP).then_inc(m_tanh, 1)
                act.activation(m_tf, m_tf, ACT.Tanh, scale=1.0 / GATE_CAP).then_inc(m_tanh, 1)
                act.wait_ge(m_tanh, 2)
                act.activation(m_nb, m_tf, ACT.Exp, scale=-GATE_CAP).then_inc(m_tanh, 1)
                act.wait_ge(m_tanh, 3)
                act.activation(m_tf, m_nb, ACT.Ln, bias=ones[0:MH, 0:1]).then_inc(m_tanh, 1)
                used("mv", 8)
                plain("mo", 8)
                act.wait_ge(scaled, half0["mo"] + 8)
                act.activation(m_o, m_o, ACT.Sigmoid).then_inc(m_sig, 1)
                act.wait_ge(m_rows, 1)
                act.activation(m_bc[:, S:2 * S], m_bc[:, S:2 * S], ACT.Exp).then_inc(m_floor, 1)
                for h in range(MH):
                    act.wait_ge(m_logw, h + 1)
                    act.activation(m_w[h % 2], m_w[h % 2], ACT.Exp).then_inc(m_exp, 1)
                    act.wait_ge(m_dend, h + 1)
                    act.activation(m_den[h % 2], bank(6, 0, S), ACT.Abs).then_inc(m_absd, 1)
                    act.wait_ge(m_hc, h + 1)
                    act.activation(m_sq[h % 2], m_h[h % 2], ACT.Square).then_inc(m_sqd, 1)
                    act.wait_ge(m_ss, h + 1)
                    act.activation(m_std, bank(7, 0, S), ACT.Sqrt, bias=eps[:, 0:1], scale=1.0 / MV).then_inc(m_stdd, 1)
                    for v in range(2):
                        act.wait_ge(m_out, 2 * h + v + 1)
                        act.activation(hi_part(os_, 2 * h + v), m_h[h % 2][:, v * S:(v + 1) * S], ACT.Copy).then_inc(xhi_ready, 1)

            def nsa_kv():
                root("kvn")
                used("kv", 8)
                for k in range(KD):
                    split_x(hi_part(os_, k), x[:, k * S:(k + 1) * S], vec[:, VEC["pre_1"] + k:VEC["pre_1"] + k + 1])
                act.wait_ge(out_read, OUT0["kv"] + 4)
                for tb in range(TB):
                    act.activation(c_sq[tb], kn_tok[:, tb * 512:(tb + 1) * 512], ACT.Square).then_inc(c_sqd, 1)
                plain("kvc", 8)
                for j, w in enumerate((w1c_k, w1c_v)):
                    act.dma_start(w1c[j].rearrange("p (c n) -> p c n", n=P), w.rearrange("(c p) n -> p c n", p=P)).then_inc(c_loaded, 16)
                act.dma_start(w2c[0], w2c_k).then_inc(c_loaded, 16)
                act.dma_start(w2c[1], w2c_v).then_inc(c_loaded, 16)

            def key_roots():
                act.wait_ge(c_sum, 2)
                act.activation(std[:, 8:8 + 16], c_ss, ACT.Sqrt, bias=eps[:, 0:1], scale=1.0 / DH).then_inc(c_std, 1)

            def compressed_hidden():
                act.wait_ge(c_bias, 1)
                for j in range(2):
                    act.activation(c_hid[j], bank(4, j * P, j * P + G * NC), ACT.Gelu_apprx_tanh, bias=c_pe[:, j:j + 1]).then_inc(c_gelu, 1)

            def compressed_squares():
                act.wait_ge(c_kc, 1)
                act.activation(c_kcsq, bank(6, 0, G * NC), ACT.Square).then_inc(c_kcsqd, 1)

            def compressed_roots():
                act.wait_ge(c_kcss, 1)
                act.activation(c_kcstd, bank(5, 64, 64 + G * NC), ACT.Sqrt, bias=eps[:, 0:1], scale=1.0 / DH).then_inc(c_kcstdd, 1)

            def nsa():
                t0 = TILE0["nq"]
                root("mid_1")
                used("ngate", 1)
                act.wait_ge(out_read, OUT0["ngate"] + 2)
                act.activation(n_gate, n_gate, ACT.Sigmoid).then_inc(n_sig, 1)
                used("nq", 4)

                def squares(g):
                    act.wait_ge(out_read, OUT0["nq"] + 2 * g + 2)
                    if g:
                        act.wait_ge(n_sum, 2)
                    for tb in range(TB):
                        act.activation(n_sq[:, tb * 512:(tb + 1) * 512], nq_tok[:, tb * D + g * 512:tb * D + (g + 1) * 512],
                                       ACT.Square).then_inc(n_sqd, 1)

                def roots(g):
                    act.wait_ge(n_sum, 2 * g + 2)
                    act.activation(std[:, 32 + 16 * g:32 + 16 * g + 16], n_ss[:, 16 * g:16 * g + 16], ACT.Sqrt, bias=eps[:, 0:1],
                                   scale=1.0 / DH).then_inc(n_std_, 1)

                def queries_turned(g):
                    act.wait_ge(n_turn, g + 1)
                    for b in range(2):
                        act.activation(n_qTa[:, (2 * g + b) * 512:(2 * g + b + 1) * 512], bank(4 + b), ACT.Copy).then_inc(n_qTd, 1)

                def compressed_exps(g):
                    act.wait_ge(n_clog, g + 1)
                    for tb, c in enumerate((NC0, NC)):
                        cl = n_cl[tb].rearrange("p (h c) -> p h c", h=H)[:, 8 * g:8 * g + 8, 0:c]
                        act.activation(cl, cl, ACT.Exp).then_inc(n_cexp, 1)

                def compressed_turned(g):
                    act.wait_ge(n_cT, g + 1)
                    for tb in range(TB):
                        act.activation(n_cpT[:, tb * S:(tb + 1) * S], bank(4 + tb, 0, S, slice(0, G * NC)), ACT.Copy).then_inc(n_cTs, 1)

                def queries(i, j):
                    if isinstance(i, int) and i == 0:
                        act.wait_ge(n_qTd, 2)
                        act.wait_ge(n_zero, 1)
                    else:
                        act.wait_ge(n_s, i * 4 + (2 * j - 2))
                    for e in range(2):
                        rows = slice(e * DH, (e + 1) * DH)
                        cols = slice(j * S, (j + 1) * S) if isinstance(i, int) and i == 0 else bass.ds(i * (2 * S) + j * S, S)
                        act.activation(n_qT[j][e][rows, :], n_qTa[rows, cols], ACT.Copy).then_inc(n_q, 1)

                def exps(i, w):
                    act.wait_ge(n_max, i * 4 + (w + 1))
                    for br in range(2):
                        for tb, (a, z) in enumerate([(0, P), (P, 3 * P)]):
                            m = 2 * tb + br
                            act.activation(n_p[w % 2][:, br * 384 + a:br * 384 + z], n_l[w % 2][:, br * 384 + a:br * 384 + z], ACT.Exp,
                                           bias=n_nmx[w][:, m:m + 1], accum_out=n_rs[w][:, m:m + 1]).then_inc(n_exp, 1)

                def probs_turned(i, w):
                    for br in range(2):
                        act.wait_ge(n_pT, i * 8 + (2 * w + br + 1))
                        if not (isinstance(i, int) and 4 * i + w < 2):
                            act.wait_ge(n_pv, i * 4 + (w - 1))
                        act.activation(n_pTs[w % 2][:, br * 384:(br + 1) * 384], bank(4 + br, 0, 384), ACT.Copy).then_inc(n_pTd, 1)

                squares(0)
                split(t0 + 4 + RING)
                roots(0)
                queries_turned(0)
                split(t0 + 5 + RING)
                queries(0, 0)
                queries(0, 1)
                compressed_exps(0)
                split(t0 + 6 + RING)
                compressed_turned(0)
                split(t0 + 7 + RING)
                squares(1)
                roots(1)
                queries_turned(1)
                compressed_exps(1)
                exps(0, 0)
                compressed_turned(1)
                exps(0, 1)

                def four(i):
                    last = isinstance(i, int) and i == HG - 1
                    for w in range(4):
                        if w % 2 == 0 and not last:
                            queries(i + 1, w // 2)
                        probs_turned(i, w)
                        if not (last and w >= 2):
                            exps(i if w < 2 else i + 1, (w + 2) % 4)

                four(0)
                with act.Fori(1, HG - 1) as i:
                    four(i)
                four(HG - 1)
                out_hi("o_n")

            for t in range(RING):
                split(t)
            act.wait_ge(x_loaded, 16 * 2)
            act.wait_ge(const_ready, 3)
            for k in range(KD):
                split_x(hi_part(xs, k), x[:, k * S:(k + 1) * S], vec[:, VEC["mix_0"] + k:VEC["mix_0"] + k + 1])
            for k in range(KD):
                act.activation(ASQ[:, k * S:(k + 1) * S], x[:, k * S:(k + 1) * S], ACT.Square).then_inc(sq_ready, 1)
            mla()
            act.wait_ge(bias_done, 1)
            act.dma_start(bias_dram, bias_row[:, :].unsqueeze(1).broadcast_to((H, COPIES, 2 * S))).then_inc(bias_out, 16)
            residual("wo_a", 1)
            root("ffn_0")
            up("up_0")
            residual("down_0", 4)
            mlstm()
            residual("wo_m", 1)
            root("ffn_1")
            up("up_1")
            residual("down_1", 4)
            root("pre_0")
            glu("glu_0")
            residual("out_0", FF2_TILES)
            root("mid_0")
            conv()
            residual("cout", 1)
            root("post_0")
            glu("glu_1")
            residual("out_1", FF2_TILES)
            nsa_kv()
            glu("glu_2", {0: key_roots, 9: compressed_hidden, 11: compressed_squares, 13: compressed_roots})
            residual("out_2", FF2_TILES)
            act.wait_ge(bias_out, 16)
            act.wait_ge(tile_done, TILE0["out_2"])
            for g in range(P // COPIES):
                act.dma_start(bias[g * COPIES:(g + 1) * COPIES, :].rearrange("p (h s) -> p h s", h=H),
                              bass.AP(tensor=bias_dram.tensor, offset=P - 1 - g * COPIES,
                                      ap=[[2 * S - 1, COPIES], [COPIES * 2 * S, H], [1, S]])).then_inc(bias_in, 16)
            nsa()
            residual("wo_n", 1)
            root("post_1")
            glu("glu_3")
            residual("out_3", FF2_TILES)

        @block.vector
        def _(dve):
            steps = Steps()

            def then(ins):
                dve.wait_ge(dve_step, steps.mark(ins))

            def hi_of(ap):
                return ap.bitcast(F32)

            def clear_sums(name):
                dve.memset(ssq[:, :], 0.0).then_inc(ssq_ready, 1)

            def norm(name):
                dve.wait_ge(std_ready, STD0[name])
                if name in TO_ROWS:
                    then(dve.reciprocal(rb[:, :], stdb[:, :]))
                if name in TO_COLUMNS:
                    col, n = (4, 2 * TB) if name == "cq" else (0, TB)
                    then(dve.reciprocal(rstd[:, col:col + n], std[:, col:col + n]))
                if name in SUMS and name != SUMS[-1]:
                    clear_sums(SUMS[SUMS.index(name) + 1])

            def rest_x(dst, src, gain, hi, count):
                dve.wait_ge(xhi_ready, count)
                dve.scalar_tensor_tensor(out=dst, in0=src, scalar=gain, in1=hi_of(hi), op0=ALU.mult, op1=ALU.subtract).then_inc(xs_ready, 1)

            def rest_all(name, dst):
                for k in range(KD):
                    g = VEC[name] + k
                    rest_x(lo_part(dst, k), x[:, k * S:(k + 1) * S], vec[:, g:g + 1], hi_part(dst, k), XS0[name] + k + 1)

            def add_halves(name, b, u, dst, i=0, per=0, a=0, z=S, p=slice(None)):
                dve.wait_ge(half_ready, i * per + (half0[name] + u + 1))
                return dve.tensor_tensor(dst, bank(b, a, z, p), half[b][p, a:z], ALU.add).then_inc(out_read, 1)

            def output(name, u, dst=None, i=0, per=0, p=slice(None)):
                b = (OUT0[name] + u) % 4
                f = fsum[b][p, :]
                add_halves(name, b, u, f, i, per, p=p)
                dve.wait_ge(out_read, i * per + (OUT0[name] + u + 1))
                dve.tensor_tensor(f if dst is None else dst, f, rb[p, :], ALU.mult).then_inc(scaled, 1)
                return f

            def plain(name, outs, dst):
                for o in range(outs):
                    output(name, o, dst(o))

            def token_major(name, outs, dst, tiles_, col=0):
                for o in range(outs):
                    d = dst(o)
                    dve.wait_ge(tile_done, TILE0[name] + tiles_(o))
                    dve.tensor_scalar(d, bank((OUT0[name] + o) % 4, 0, d.shape[-1]), rstd[:, col + o % 2:col + o % 2 + 1], None, ALU.mult)\
                       .then_inc(out_read, 1)

            def residual(name, per, scale=1.0):
                t0, o0, no = TILE0[name], OUT0[name], RES.index(name)
                with dve.Fori(0, KD // 4) as i:
                    for u in range(4):
                        b = (o0 + u) % 4
                        xo = at(x, i * (4 * S) + u * S, S)
                        dve.wait_ge(tile_done, i * (4 * per) + (t0 + (u + 1) * per))
                        dve.scalar_tensor_tensor(out=xo, in0=bank(b, 0, S), scalar=scale, in1=xo, op0=ALU.mult, op1=ALU.add)\
                           .then_inc(x_half, 1)
                        dve.wait_ge(x_half, i * 4 + (KD * no + u + 1))
                        dve.scalar_tensor_tensor(out=xo, in0=bank(b, S, 2 * S), scalar=scale, in1=xo, op0=ALU.mult, op1=ALU.add)\
                           .then_inc(out_read, 1)
                        if name in NEXT:
                            chunk = i * (8 * S) + u * 2 * S
                            norm_ = NEXT[name]
                            rest_x(at(xs, chunk + S, S), xo, at(vec, i * 4 + (VEC[norm_] + u), 1), at(xs, chunk, S),
                                   i * 4 + (XS0[norm_] + u + 1))
                            dve.wait_ge(sq_ready, i * 4 + (SQ0[name] + u + 1))
                            dve.wait_ge(ssq_ready, i * 4 + (SSQ0[norm_] + u + 1))
                            dve.tensor_tensor(ssq[:, :], ssq[:, :], sq[u][:, :], ALU.add).then_inc(ssq_ready, 1)

            def h_lo(name, src, chunk, count):
                dve.wait_ge(hhi_ready, count)
                dve.tensor_tensor(at(hs, chunk + S, S), src, hi_of(at(hs, chunk, S)), ALU.subtract).then_inc(hs_ready, 1)

            def up(name):
                h0 = hid0[name]
                with dve.Fori(0, FF1 // 4) as i:
                    for u in range(4):
                        f = output(name, u, None, i, 4)
                        dve.wait_ge(scaled, i * 4 + (half0[name] + u + 1))
                        dve.scalar_tensor_tensor(out=f, in0=f, scalar=0.0, in1=f, op0=ALU.max, op1=ALU.mult).then_inc(hid_ready, 1)
                        h_lo(name, f, i * (8 * S) + u * 2 * S, i * 4 + (h0 + u + 1))

            def glu(name, between=None):
                h0 = hid0[name]
                between = between or {}

                def four(i):
                    for u in range(4):
                        f = output(name, u, None, i, 4)
                        if u % 2:
                            dve.wait_ge(sil_ready, i * 2 + (sil0[name] + u // 2 + 1))
                            dve.wait_ge(scaled, i * 4 + (half0[name] + u + 1))
                            dve.tensor_tensor(f, f, sil[u // 2][:, :], ALU.mult).then_inc(hid_ready, 1)
                            h_lo(name, f, i * (4 * S) + (u // 2) * 2 * S, i * 2 + (h0 + u // 2 + 1))
                        if isinstance(i, int) and i * 4 + u in between:
                            between[i * 4 + u]()

                peeled = max(between, default=-1) // 4 + 1
                for i in range(peeled):
                    four(i)
                with dve.Fori(peeled, FF2 // 2) as i:
                    four(i)

            def conv():
                name, h0 = "cin", hid0["cin"]
                for j in range(2):
                    ins = dve.memset(conv_u[j][:, 0:TAPS - 1], 0.0)
                then(ins)
                with dve.Fori(0, KD // 4) as i:
                    steps.base, start, steps.n = i * 16 + steps.n, steps.n, 0
                    for m in range(4):
                        j = m % 2
                        for n, dst in enumerate((conv_b[j], conv_c[j], conv_v[j])):
                            output(name, 3 * m + n, dst, i, 12)
                        dve.wait_ge(scaled, i * 12 + (half0[name] + 3 * m + 3))
                        then(dve.tensor_tensor(conv_u[j][:, TAPS - 1:], conv_c[j], conv_v[j], ALU.mult))
                        for k in range(TAPS):
                            w = at(vec, i * 4 + (VEC["taps"] + k * KD + m), 1)
                            if k == 0:
                                then(dve.tensor_scalar(conv_y[j], conv_u[j][:, 0:S], w, None, ALU.mult))
                            else:
                                then(dve.scalar_tensor_tensor(out=conv_y[j], in0=conv_u[j][:, k:k + S], scalar=w, in1=conv_y[j],
                                                              op0=ALU.mult, op1=ALU.add))
                        dve.tensor_tensor(conv_y[j], conv_y[j], conv_b[j], ALU.mult).then_inc(hid_ready, 1)
                        h_lo(name, conv_y[j], i * (8 * S) + m * 2 * S, i * 4 + (h0 + m + 1))
                    assert steps.n == 16
                    steps.base, steps.n = 0, start + 16 * (KD // 4)

            def out_lo(name):
                for k in range(KD):
                    dve.wait_ge(xhi_ready, XS0[name] + k + 1)
                    dve.tensor_tensor(lo_part(os_, k), bank(5 + k % 3, 0, S), hi_of(hi_part(os_, k)), ALU.subtract).then_inc(xs_ready, 1)

            def mla():
                plain("dq", 3, lambda o: cqf[:, o * S:(o + 1) * S])
                plain("dkv", 2, lambda o: cqf[:, (KQ + o) * S:(KQ + o + 1) * S])
                token_major("kr", 2, lambda o: kr_tok[:, o * ROPE:(o + 1) * ROPE], lambda o: 1)
                for k in range(KQ + KKV):
                    g = VEC["q_norm"] + k if k < KQ else VEC["kv_norm"] + k - KQ
                    rest_x(lo_part(os_, k), cqf[:, k * S:(k + 1) * S], vec[:, g:g + 1], hi_part(os_, k), XS0["cq"] + k + 1)
                norm("cq")
                token_major("uq", 6, lambda o: q_tok[:, (o % 2) * H * QK + (o // 2) * 512:][:, 0:512],
                            lambda o: [2, 2, 3, 3, 5, 5][o], 4)
                token_major("uk", 4, lambda o: k_tok[:, (o % 2) * H * NOPE + (o // 2) * 512:][:, 0:512], lambda o: 1 + o // 2, 6)
                token_major("uv", 4, lambda o: v_tok[:, (o % 2) * H * VD + (o // 2) * 512:][:, 0:512], lambda o: 1 + o // 2, 6)
                dve.wait_ge(out_read, OUT0["uv"] + 4)
                dve.wait_ge(row_ready, 1)
                dve.tensor_copy(bias_row[:, :], bank(6, 0, 2 * S, slice(0, H))).then_inc(bias_done, 1)
                q3 = q_tok.rearrange("p (n d) -> p n d", d=QK)
                k3 = k_tok.rearrange("p (n d) -> p n d", d=NOPE)
                kr3 = kr_tok.rearrange("p (n d) -> p n d", d=ROPE)
                gq, gk = row[:, ROW["q_gain"]:ROW["q_gain"] + QK], row[:, ROW["k_gain"]:ROW["k_gain"] + QK]
                sizes = [(mscr[n % 2][:, 0:w], w) for n, (_, w) in enumerate(HEAD_SQ)]
                for n, (src, w) in enumerate(sizes):
                    d = [QK] * 4 + [NOPE] * 2 + [ROPE]
                    first = [0, 8, 16, 24, 32, 48, 64][n]
                    dve.wait_ge(head_sq, n + 1)
                    dve.tensor_reduce(ss[:, first:first + w // d[n]], src.rearrange("p (n d) -> p n d", d=d[n]), AX_X, ALU.add)\
                       .then_inc(head_sum, 1)
                dve.wait_ge(head_sum, len(HEAD_SQ))
                ssk = ss[:, 2 * H:4 * H].rearrange("p (t h) -> p t h", t=TB)
                ssr = ss[:, 4 * H:4 * H + TB].unsqueeze(2).to_broadcast([P, TB, H])
                dve.tensor_tensor(ssk, ssk, ssr, ALU.add).then_inc(head_sum, 1)
                then(dve.tensor_tensor(q3, q3, gq.unsqueeze(1).to_broadcast([P, TB * H, QK]), ALU.mult))
                dve.tensor_tensor(k3, k3, gk[:, 0:NOPE].unsqueeze(1).to_broadcast([P, TB * H, NOPE]), ALU.mult)
                then(dve.tensor_tensor(kr3, kr3, gk[:, NOPE:].unsqueeze(1).to_broadcast([P, TB, ROPE]), ALU.mult))
                cos = con[:, CONST["cos"]:CONST["cos"] + TB * HALF].rearrange("p (t d) -> p t d", t=TB)
                sin = con[:, CONST["sin"]:CONST["sin"] + TB * HALF].rearrange("p (t d) -> p t d", t=TB)
                q4 = q_tok.rearrange("p (t h d) -> p t h d", t=TB, h=H)
                for heads, lo_, hi_ in ((H, q4[:, :, :, NOPE:NOPE + HALF], q4[:, :, :, NOPE + HALF:QK]),
                                        (1, kr3[:, :, 0:HALF].unsqueeze(2), kr3[:, :, HALF:ROPE].unsqueeze(2))):
                    n = TB * heads * HALF
                    t = [rope_t[:, j * n:(j + 1) * n].rearrange("p (t h d) -> p t h d", t=TB, h=heads) for j in range(4)]
                    c4 = cos.unsqueeze(2).to_broadcast([P, TB, heads, HALF])
                    s4 = sin.unsqueeze(2).to_broadcast([P, TB, heads, HALF])
                    dve.tensor_tensor(t[0], lo_, c4, ALU.mult)
                    dve.tensor_tensor(t[1], hi_, s4, ALU.mult)
                    dve.tensor_tensor(t[2], hi_, c4, ALU.mult)
                    then(dve.tensor_tensor(t[3], lo_, s4, ALU.mult))
                    dve.tensor_tensor(lo_, t[0], t[1], ALU.subtract)
                    then(dve.tensor_tensor(hi_, t[2], t[3], ALU.add))
                dve.wait_ge(head_std, 1)
                then(dve.reciprocal(rstd[:, 0:4 * H], std[:, 0:4 * H]))
                rq = rstd[:, 0:2 * H].rearrange("p (t h) -> p t h", t=TB)
                rk = rstd[:, 2 * H:4 * H].rearrange("p (t h) -> p t h", t=TB)
                qs4 = q_st.rearrange("p (t h d) -> p t h d", t=TB, h=4)
                ks4 = k_st.rearrange("p (t h d) -> p t h d", t=TB, h=4)
                kt3 = k_tok.rearrange("p (t c) -> p t c", t=TB)
                qt3 = q_tok.rearrange("p (t c) -> p t c", t=TB)
                ot3 = o_tok.rearrange("p (t c) -> p t c", t=TB)
                with dve.Fori(0, H // 4) as i:
                    steps.base, start, steps.n = i * 8 + steps.n, steps.n, 0
                    for tb in range(TB):
                        r = rq[:, tb, bass.ds(i * 4, 4)].unsqueeze(2)
                        dve.tensor_tensor(qs4[:, tb], qt3[:, tb, bass.ds(i * (4 * QK), 4 * QK)].rearrange("p (h d) -> p h d", h=4),
                                          r.to_broadcast([P, 4, QK]), ALU.mult)
                        r = rk[:, tb, bass.ds(i * 4, 4)].unsqueeze(2)
                        dve.tensor_tensor(ks4[:, tb, :, 0:NOPE],
                                          kt3[:, tb, bass.ds(i * (4 * NOPE), 4 * NOPE)].rearrange("p (h d) -> p h d", h=4),
                                          r.to_broadcast([P, 4, NOPE]), ALU.mult)
                        ins = dve.tensor_tensor(ks4[:, tb, :, NOPE:QK], kr3[:, tb].unsqueeze(1).to_broadcast([P, 4, ROPE]),
                                                r.to_broadcast([P, 4, ROPE]), ALU.mult)
                    ins.then_inc(a_st, 1)

                    def maxima(h):
                        dve.wait_ge(a_s, i * 4 + (h + 1))
                        dve.tensor_reduce(mx[:, 2 * h:2 * h + 1], bank(2 + h % 2, 0, P), AX_X, ALU.max)
                        then(dve.tensor_reduce(mx[:, 2 * h + 1:2 * h + 2], bank(2 + h % 2, P, 3 * P), AX_X, ALU.max))
                        dve.tensor_scalar(nmx[:, 2 * h:2 * h + 2], mx[:, 2 * h:2 * h + 2], -(QK ** -0.5), None, ALU.mult).then_inc(a_max, 1)

                    def outputs(h):
                        dve.wait_ge(a_exp, i * 8 + 2 * (h + 1))
                        then(dve.reciprocal(rinv[:, 2 * h:2 * h + 2], rsum[:, 2 * h:2 * h + 2]))
                        dve.wait_ge(a_pv, i * 4 + (h + 1))
                        for tb in range(TB):
                            ins = dve.tensor_scalar(ot3[:, tb, bass.ds(i * (4 * VD) + h * VD, VD)], bank(6 + h % 2, tb * VD, (tb + 1) * VD),
                                                    rinv[:, 2 * h + tb:2 * h + tb + 1], None, ALU.mult)
                        ins.then_inc(a_o, 1)

                    maxima(0)
                    maxima(1)
                    maxima(2)
                    outputs(0)
                    maxima(3)
                    outputs(1)
                    outputs(2)
                    outputs(3)
                    assert steps.n == 8
                    steps.base, steps.n = 0, start + 8 * (H // 4)
                out_lo("o_a")

            def mlstm():
                for o, (dst, b) in enumerate(((m_ti, "b_i"), (m_tf, "b_f"))):
                    output("mgate", o, dst, p=slice(0, MH))
                    dve.wait_ge(scaled, half0["mgate"] + o + 1)
                    dve.tensor_scalar(dst, dst, vec[0:MH, VEC[b]:VEC[b] + 1], None, ALU.add).then_inc(m_gates, 1)
                plain("mqk", 8, lambda o: m_qk[:, o * S:(o + 1) * S])
                then(dve.memset(m_one, 1.0))
                dve.wait_ge(m_tanh, 4)
                then(dve.tensor_tensor_scan(m_nb, m_one, m_tf, 0.0, ALU.mult, ALU.add))
                then(dve.scalar_tensor_tensor(out=m_a, in0=m_ti, scalar=GATE_CAP, in1=m_nb, op0=ALU.mult, op1=ALU.add))
                then(dve.tensor_tensor_scan(m_g, m_a, m_a, 0.0, ALU.max, ALU.max))
                dve.tensor_scalar(m_bc[:, 0:S], m_g, -1.0, None, ALU.mult)
                dve.tensor_tensor(m_bc[:, S:2 * S], m_nb, m_g, ALU.subtract).then_inc(m_rows, 1)
                token_major("mv", 4, lambda o: m_v[:, (o % 2) * D + (o // 2) * 512:][:, 0:512], lambda o: 4 * (1 + o // 2))
                plain("mo", 8, lambda o: m_o[:, o * S:(o + 1) * S])
                dve.wait_ge(m_at, 1)
                then(dve.tensor_copy(m_acol, bank(7, 0, TB * MH)))
                causal = const("causal", 0, P)

                def exponents(h):
                    dve.wait_ge(m_bcd, h + 1)
                    dve.tensor_copy(m_fl[h % 2], bank(4, S, 2 * S))
                    dve.tensor_scalar(m_w[h % 2][:, 0:S], bank(4, 0, S), m_acol[:, h:h + 1], 0.0, ALU.add, ALU.min)
                    dve.tensor_scalar(m_w[h % 2][:, S:S + P], bank(4, P, S), m_acol[:, MH + h:MH + h + 1], 0.0, ALU.add, ALU.min)\
                       .then_inc(m_logw, 1)

                def weights(h):
                    w = m_w[h % 2]
                    dve.wait_ge(m_exp, h + 1)
                    dve.tensor_tensor(w[:, 0:P], w[:, 0:P], causal, ALU.mult)
                    then(dve.tensor_tensor(w[:, S:S + P], w[:, S:S + P], causal, ALU.mult))
                    dve.wait_ge(m_st, h + 1)
                    dve.scalar_tensor_tensor(out=m_pt[h % 2], in0=bank(5, 0, 384), scalar=MQK ** -0.5, in1=w, op0=ALU.mult, op1=ALU.mult)\
                       .then_inc(m_ptd, 1)

                exponents(0)
                for h in range(MH):
                    weights(h)
                    if h + 1 < MH:
                        exponents(h + 1)
                    hh = m_h[h % 2]
                    den = m_den[h % 2]
                    dve.wait_ge(m_absd, h + 1)
                    then(dve.tensor_tensor(den, den, m_fl[h % 2], ALU.max))
                    then(dve.reciprocal(den, den))
                    dve.wait_ge(m_num, h + 1)
                    dve.tensor_tensor(hh.rearrange("p (v t) -> p v t", v=2), bank(h % 2).rearrange("p (v t) -> p v t", v=2),
                                      den.unsqueeze(1).to_broadcast([P, 2, S]), ALU.mult).then_inc(m_hc, 1)
                    dve.wait_ge(m_stdd, h + 1)
                    then(dve.reciprocal(m_r, m_std))
                    for v in range(2):
                        g = VEC["head_norm"] + 2 * h + v
                        ins = dve.scalar_tensor_tensor(out=hh[:, v * S:(v + 1) * S], in0=hh[:, v * S:(v + 1) * S], scalar=vec[:, g:g + 1],
                                                       in1=m_r, op0=ALU.mult, op1=ALU.mult)
                    then(ins)
                    if h == 0:
                        dve.wait_ge(m_sig, 1)
                    for v in range(2):
                        dve.tensor_tensor(hh[:, v * S:(v + 1) * S], hh[:, v * S:(v + 1) * S],
                                          m_o[:, (2 * h + v) * S:(2 * h + v + 1) * S], ALU.mult).then_inc(m_out, 1)
                    for v in range(2):
                        k = 2 * h + v
                        dve.wait_ge(xhi_ready, XS0["o_m"] + k + 1)
                        dve.tensor_tensor(lo_part(os_, k), hh[:, v * S:(v + 1) * S], hi_of(hi_part(os_, k)), ALU.subtract).then_inc(xs_ready, 1)

            def nsa_kv():
                token_major("kv", 4, lambda o: (kn_tok if o < 2 else vtok)[:, (o % 2) * 512:(o % 2 + 1) * 512],
                            lambda o: 4 * (1 + o // 2))
                rest_all("pre_1", os_)
                for tb in range(TB):
                    dve.wait_ge(c_sqd, tb + 1)
                    dve.tensor_reduce(c_ss[:, tb * 8:(tb + 1) * 8], c_sq[tb].rearrange("p (n d) -> p n d", d=DH), AX_X, ALU.add)\
                       .then_inc(c_sum, 1)
                for j, pe_at in enumerate((VEC["pe_k"], VEC["pe_v"])):
                    then(dve.memset(c_dup[j][:, G * S:], 0.0))
                    dve.tensor_copy(c_dup[j][:, G * S:G * S + CBLOCK:2], vec[:, pe_at:pe_at + CBLOCK // 2])
                for o in range(8):
                    b = (OUT0["kvc"] + o) % 4
                    dst = c_dup[o // G][:, (o % G) * S:(o % G + 1) * S]
                    add_halves("kvc", b, o, fsum[b][:, :])
                    dve.wait_ge(out_read, OUT0["kvc"] + o + 1)
                    dve.tensor_tensor(dst[0:DH, :], fsum[b][0:DH, :], rb[0:DH, :], ALU.mult)
                    dve.tensor_tensor(dst[DH:P, 0:S - 1], fsum[b][DH:P, 1:S], rb[DH:P, 1:S], ALU.mult).then_inc(scaled, 1)

            def keys():
                dve.wait_ge(c_std, 1)
                then(dve.reciprocal(c_r, std[:, 8:8 + 16]))
                kn3 = kn_tok.rearrange("p (n d) -> p n d", d=DH)
                then(dve.tensor_tensor(kn3, kn3, c_r.unsqueeze(2).to_broadcast([P, 16, DH]), ALU.mult))
                gains = row[:, ROW["ks"]:ROW["ks"] + 2 * DH].rearrange("p (b d) -> p b d", b=2)
                then(dve.tensor_tensor(gains, gains, row[:, ROW["nq"]:ROW["nq"] + DH].unsqueeze(1).to_broadcast([P, 2, DH]), ALU.mult))
                gain = row[:, ROW["ks"]:ROW["ks"] + 2 * DH].rearrange("p (b d) -> p b d", b=2).unsqueeze(2).to_broadcast([P, 2, G, DH])
                for tb in range(TB):
                    k4 = kn_tok[:, tb * 512:(tb + 1) * 512].rearrange("p (b g d) -> p b g d", b=2, g=G)
                    ins = dve.tensor_tensor(k4, k4, gain, ALU.mult)
                ins.then_inc(c_kn, 1)

            def keys_turned():
                dve.wait_ge(c_kt, 1)
                for b in range(2):
                    dve.tensor_copy(kT[:, b * 512:(b + 1) * 512], bank(6 + b)).then_inc(c_kT, 1)

            def compression_bias():
                dve.wait_ge(c_hd, 1)
                for j in range(2):
                    ins = dve.tensor_copy(c_pe[:, j:j + 1], bank(4, j * P + G * NC, j * P + G * NC + 1))
                ins.then_inc(c_bias, 1)

            def compressed():
                dve.wait_ge(c_kcstdd, 1)
                then(dve.reciprocal(c_kcr, c_kcstd))
                g = VEC["kc_norm"]
                then(dve.tensor_tensor(vec[:, g:g + 1], vec[:, g:g + 1], vec[:, VEC["nq_norm"]:VEC["nq_norm"] + 1], ALU.mult))
                then(dve.memset(kcT[:, :], 0.0))
                for e in range(2):
                    rows = slice(e * DH, (e + 1) * DH)
                    out, keys_, rms = (t[rows, :].rearrange("p (g e c) -> p g e c", g=2, e=2)[:, :, e, :]
                                       for t in (kcT, bank(6, 0, G * NC), c_kcr))
                    ins = dve.scalar_tensor_tensor(out=out, in0=keys_, scalar=vec[rows, g:g + 1], in1=rms, op0=ALU.mult, op1=ALU.mult)
                ins.then_inc(c_end, 1)
                dve.wait_ge(c_vcd, 1)
                n = G * NC
                dve.tensor_tensor(vc[:, :].rearrange("p (g d) -> p g d", g=G),
                                  bank(7, 0, DH, slice(0, n)).unsqueeze(1).to_broadcast([n, G, DH]),
                                  const("groups", 0, G, slice(0, n)).unsqueeze(2).to_broadcast([n, G, DH]), ALU.mult).then_inc(c_end, 1)

            def nsa():
                n_r3 = n_r.rearrange("p (t h) -> p t h", t=TB)
                gate4 = n_gate.rearrange("p (t h b) -> p t h b", t=TB, b=3)
                b4 = bias[:, :].rearrange("p (h a b) -> p h a b", h=H, b=CSTRIDE)
                cl3 = [n_cl[tb].rearrange("p (h c) -> p h c", h=H) for tb in range(TB)]
                cmx3, crs3, csc3 = (t.rearrange("p (t h) -> p t h", t=TB) for t in (n_cmx, n_crs, n_csc))
                no4 = no_tok.rearrange("p (t h d) -> p t h d", t=TB, h=H)

                def evacuate(g):
                    for tb in range(TB):
                        dve.wait_ge(tile_done, TILE0["nq"] + 4 * g + 4)
                        dve.tensor_scalar(nq_tok[:, tb * D + g * 512:tb * D + (g + 1) * 512], bank((OUT0["nq"] + 2 * g + tb) % 4),
                                          rstd[:, tb:tb + 1], None, ALU.mult).then_inc(out_read, 1)

                def query_sums(g):
                    for tb in range(TB):
                        dve.wait_ge(n_sqd, 2 * g + tb + 1)
                        dve.tensor_reduce(n_ss[:, 16 * g + 8 * tb:16 * g + 8 * tb + 8],
                                          n_sq[:, tb * 512:(tb + 1) * 512].rearrange("p (n d) -> p n d", d=DH), AX_X, ALU.add).then_inc(n_sum, 1)

                def query_scales(g):
                    r = n_r3[:, :, 8 * g:8 * g + 8]
                    dve.wait_ge(n_std_, g + 1)
                    then(dve.reciprocal(r, std[:, 32 + 16 * g:32 + 16 * g + 16].rearrange("p (t h) -> p t h", t=TB)))
                    then(dve.tensor_scalar(r, r, DH ** -0.5, None, ALU.mult))

                def compressed_logits(g):
                    dve.wait_ge(n_cs, g + 1)
                    mine = slice(8 * g, 8 * g + 8)
                    for tb, c in enumerate((NC0, NC)):
                        raw_ = bank(6, tb * P, (tb + 1) * P).rearrange("p (j x) -> p j x", j=4)[:, :, 0:2 * NC]
                        ins = dve.tensor_tensor(cl3[tb][:, mine, 0:c].rearrange("p (j e) c -> p j e c", e=2),
                                                raw_.rearrange("p j (e c) -> p j e c", e=2)[:, :, :, 0:c],
                                                n_r3[:, tb, mine].rearrange("p (j e) -> p j e", e=2).unsqueeze(3).to_broadcast([P, 4, 2, c]), ALU.mult)
                    then(ins)
                    views = [(cl3[tb][:, 8 * g:8 * g + 8, 0:c], c, first) for tb, (c, first) in enumerate(((NC0, 9), (NC, 1)))]
                    for cl, c, first in views:
                        ins = dve.tensor_tensor(cl, cl, b4[:, 8 * g:8 * g + 8, first:first + c, CSTRIDE - 1], ALU.add)
                    then(ins)
                    for tb, (cl, c, _) in enumerate(views):
                        ins = dve.tensor_reduce(cmx3[:, tb, 8 * g:8 * g + 8], cl, AX_X, ALU.max)
                    then(ins)
                    for tb, (cl, c, _) in enumerate(views):
                        ins = dve.tensor_tensor(cl, cl, cmx3[:, tb, 8 * g:8 * g + 8].unsqueeze(2).to_broadcast([P, 8, c]), ALU.subtract)
                    ins.then_inc(n_clog, 1)

                def compressed_scales(g):
                    dve.wait_ge(n_cexp, 2 * g + 2)
                    mine = slice(8 * g, 8 * g + 8)
                    for tb, c in enumerate((NC0, NC)):
                        ins = dve.tensor_reduce(crs3[:, tb, mine], cl3[tb][:, mine, 0:c], AX_X, ALU.add)
                    then(ins)
                    then(dve.reciprocal(crs3[:, :, mine], crs3[:, :, mine]))
                    then(dve.tensor_tensor(csc3[:, :, mine], crs3[:, :, mine], gate4[:, :, mine, 0], ALU.mult))
                    valid = const("valid", 0, TB).unsqueeze(2).to_broadcast([P, TB, 8])
                    then(dve.tensor_tensor(csc3[:, :, mine], csc3[:, :, mine], valid, ALU.mult))

                def compressed_outputs(g):
                    dve.wait_ge(n_cpv, g + 1)
                    for tb in range(TB):
                        ins = dve.tensor_tensor(no4[:, tb, 8 * g:8 * g + 8], bank(6 + tb).rearrange("p (h d) -> p h d", d=DH),
                                                csc3[:, tb, 8 * g:8 * g + 8].unsqueeze(2).to_broadcast([P, 8, DH]), ALU.mult)
                    ins.then_inc(n_co, 1)

                def logits(i, w):
                    e, log = w % 2, n_l[w % 2].rearrange("p (b c) -> p b c", b=2)
                    dve.wait_ge(n_s, i * 4 + (w + 1))
                    if not (isinstance(i, int) and 4 * i + w < 2):
                        dve.wait_ge(n_exp, i * 16 + 4 * (w - 1))
                    scores = psum[:, 2 * e * BANK:(2 * e + 2) * BANK].rearrange("p (b c) -> p b c", b=2)
                    for tb, (a, z) in enumerate([(0, P), (P, 3 * P)]):
                        table = at(bias, i * (4 * S) + (w * S + (P if tb == 0 else 0)), z - a)
                        ins = dve.scalar_tensor_tensor(out=log[:, :, a:z], in0=scores[:, :, a:z], scalar=at(n_r, i * 4 + (tb * H + w), 1),
                                                       in1=table.unsqueeze(1).to_broadcast([P, 2, z - a]), op0=ALU.mult, op1=ALU.add)
                    ins.then_inc(n_log, 1)
                    dve.wait_ge(n_log, i * 4 + (w + 1))
                    dve.tensor_reduce(n_mx[w][:, 0:2], log[:, :, 0:P], AX_X, ALU.max)
                    then(dve.tensor_reduce(n_mx[w][:, 2:4], log[:, :, P:3 * P], AX_X, ALU.max))
                    dve.tensor_scalar(n_nmx[w], n_mx[w], -1.0, None, ALU.mult).then_inc(n_max, 1)

                def outputs(i, w):
                    dve.wait_ge(n_exp, i * 16 + 4 * (w + 1))
                    then(dve.reciprocal(n_sc[w], n_rs[w]))
                    h = i * 4 + w
                    g = gate4[:, :, h:h + 1, 1:3] if isinstance(i, int) else gate4[:, :, bass.ds(h, 1), 1:3]
                    sc = n_sc[w].rearrange("p (t o b) -> p t o b", t=TB, o=1)
                    then(dve.tensor_tensor(sc, sc, g, ALU.mult))
                    dve.wait_ge(n_pv, i * 4 + (w + 1))
                    for br in range(2):
                        for tb in range(TB):
                            o = at(no_tok, i * (4 * DH) + (tb * D + w * DH), DH)
                            col = (2 * br + tb) * P + w % 2 * DH
                            ins = dve.scalar_tensor_tensor(out=o, in0=bank(6 + w % 2, col, col + DH), scalar=n_sc[w][:, 2 * tb + br:2 * tb + br + 1],
                                                           in1=o, op0=ALU.mult, op1=ALU.add)
                        if br == 0:
                            then(ins)
                    ins.then_inc(n_od, 1)

                for j in range(2):
                    for e in range(2):
                        ins = dve.memset(n_qT[j][e][DH - e * DH:P - e * DH, :], 0.0)
                ins.then_inc(n_zero, 1)
                dve.memset(n_cl[0], 0.0)
                token_major("ngate", 2, lambda o: n_gate[:, o * 3 * H:(o + 1) * 3 * H], lambda o: 1)
                evacuate(0)
                query_sums(0)
                query_scales(0)
                dve.wait_ge(n_sig, 1)
                dve.wait_ge(bias_in, 16 * (P // COPIES))
                compressed_logits(0)
                compressed_scales(0)
                evacuate(1)
                query_sums(1)
                compressed_outputs(0)
                query_scales(1)
                compressed_logits(1)
                logits(0, 0)
                compressed_scales(1)
                logits(0, 1)
                compressed_outputs(1)
                dve.wait_ge(n_co, 2)

                def four(i):
                    first, last = (isinstance(i, int) and i == j for j in (0, HG - 1))
                    for w in range(4):
                        if not (last and w >= 2):
                            logits(i if w < 2 else i + 1, (w + 2) % 4)
                        if not (first and w == 0):
                            outputs(i if w else i - 1, (w - 1) % 4)

                four(0)
                with dve.Fori(1, HG - 1) as i:
                    start, steps.n = steps.n, 0
                    steps.base = i * 16 + (start - 16)
                    four(i)
                    assert steps.n == 16
                    steps.base, steps.n = 0, start + 16 * (HG - 2)
                four(HG - 1)
                outputs(HG - 1, 3)
                out_lo("o_n")

            dve.wait_ge(x_loaded, 16 * 2)
            rest_all("mix_0", xs)
            clear_sums("mix_0")
            for k in range(KD):
                dve.wait_ge(sq_ready, k + 1)
                dve.wait_ge(ssq_ready, k + 1)
                dve.tensor_tensor(ssq[:, :], ssq[:, :], ASQ[:, k * S:(k + 1) * S], ALU.add).then_inc(ssq_ready, 1)
            dve.wait_ge(loaded, 16 * 3)
            dve.wait_ge(const_ready, 3)
            dve.tensor_copy(chunk_u[:, :], con[0:1, CONST["chunk_u"]:CONST["chunk_u"] + P])
            then(dve.tensor_copy(chunk_v[:, :], con[0:1, CONST["chunk_v"]:CONST["chunk_v"] + P]))
            norm("mix_0")
            mla()
            residual("wo_a", 1)
            norm("ffn_0")
            up("up_0")
            residual("down_0", 4)
            norm("mix_1")
            mlstm()
            residual("wo_m", 1)
            norm("ffn_1")
            up("up_1")
            residual("down_1", 4)
            norm("pre_0")
            glu("glu_0")
            residual("out_0", FF2_TILES, 0.5)
            norm("mid_0")
            conv()
            residual("cout", 1)
            norm("post_0")
            glu("glu_1")
            residual("out_1", FF2_TILES, 0.5)
            norm("kvn")
            nsa_kv()
            glu("glu_2", {0: keys, 2: keys_turned, 9: compression_bias, 15: compressed})
            residual("out_2", FF2_TILES, 0.5)
            norm("mid_1")
            nsa()
            residual("wo_n", 1)
            norm("post_1")
            glu("glu_3")
            residual("out_3", FF2_TILES, 0.5)

        @block.tensor
        def _(pe):
            def product(out_bank, lhs, k, src, first, last, hi=0):
                s, c = lhs
                chunk = k * 2 * S
                pe.matmul(bank(out_bank), w_hi[s][:, c:c + P], src[:, chunk:chunk + 2 * S], start=first, stop=False)
                return pe.matmul(bank(out_bank, 0, S), w_lo[s][:, c:c + P], src[:, chunk:chunk + S], start=False, stop=last)

            def sums(name):
                if name == "cq":
                    pe.wait_ge(sq_ready, SQ0["cq"] + 1)
                    for tb in range(TB):
                        for k in range(KQ + KKV):
                            col, first, last = (4, 0, KQ - 1) if k < KQ else (6, KQ, KQ + KKV - 1)
                            ins = pe.matmul(bank(STAT, col + tb, col + tb + 1), ASQ[:, k * S + tb * P:k * S + (tb + 1) * P], ones[:, 0:1],
                                            start=k == first, stop=k == last)
                else:
                    pe.wait_ge(ssq_ready, SSQ0[name] + KD + 1)
                    if name == "mix_0":
                        pe.wait_ge(const_ready, 3)
                    if name in TO_ROWS:
                        ins = pe.matmul(bank(RB, 0, S), ones[:, :], ssq[:, :], start=True, stop=True)
                    if name in TO_COLUMNS:
                        for tb in range(TB):
                            ins = pe.matmul(bank(STAT, tb, tb + 1), ssq[:, tb * P:(tb + 1) * P], ones[:, 0:1], start=True, stop=True)
                ins.then_inc(stat_done, 1)

            def feature(name, outs, xs_name, src=xs, norm_=None, between=None):
                between = between or {}
                t0, o0 = TILE0[name], OUT0[name]

                def one(u, i=0, wait_x=False):
                    s, b = (t0 + u) % RING, (o0 + u) % 4
                    pe.wait_ge(lo_ready, i * 4 + (t0 + u + 1))
                    if not (isinstance(i, int) and o0 + u + 4 * i < 4):
                        pe.wait_ge(out_read, i * 4 + (o0 + u - 3))
                    for k in range(KD):
                        if wait_x:
                            pe.wait_ge(xs_ready, XS0[xs_name] + k + 1)
                        ins = product(b, (s, k * P), k, src, k == 0, k == KD - 1)
                    ins.then_inc(tile_done, 1)

                head = outs if outs % 4 else min(outs, max(1, max(between, default=0) // 4 + 1) * 4)
                for u in range(head):
                    one(u, 0, u == 0)
                    if u in between:
                        between[u]()
                    if norm_ and u == 0:
                        sums(norm_)
                if head < outs:
                    with pe.Fori(head // 4, outs // 4) as i:
                        for u in range(4):
                            one(u, i)

            def residual(name, per, chunks, src, ready):
                t0, o0 = TILE0[name], OUT0[name]
                with pe.Fori(0, KD // 4) as i:
                    for u in range(4):
                        b = (o0 + u) % 4
                        pe.wait_ge(out_read, i * 4 + (o0 + u - 3))
                        for j in range(per):
                            t = t0 + u * per + j
                            pe.wait_ge(lo_ready, i * (4 * per) + (t + 1))
                            n = min(BLK, chunks - j * BLK)
                            for k in range(n):
                                c = j * BLK + k
                                if u == 0:
                                    pe.wait_ge(*ready(c))
                                ins = product(b, (t % RING, k * P), c, src, c == 0, c == chunks - 1)
                            ins.then_inc(tile_done, 1)

            def token_major(name, groups, chunks, k0=0, xs_name=None, src=xs, norm_=None, between=None):
                t0, o0 = TILE0[name], OUT0[name]
                for n in range(groups * chunks):
                    g, c = divmod(n, chunks)
                    s, col = (t0 + n // 2) % RING, n % 2 * 512
                    pe.wait_ge(lo_ready, t0 + n // 2 + 1)
                    if c == 0:
                        pe.wait_ge(out_read, o0 + 2 * g + 1 - 3)
                    if xs_name and g == 0:
                        pe.wait_ge(xs_ready, XS0[xs_name] + k0 + c + 1)
                    for tb in range(TB):
                        x_hi, x_lo = (src[:, (k0 + c) * 2 * S + part_ * S + tb * P:][:, 0:P] for part_ in range(2))
                        out = bank((o0 + 2 * g + tb) % 4)
                        pe.matmul(out, x_hi, w_hi[s][:, col:col + 512], start=c == 0, stop=False)
                        pe.matmul(out, x_hi, w_lo[s][:, col:col + 512], start=False, stop=False)
                        ins = pe.matmul(out, x_lo, w_hi[s][:, col:col + 512], start=False, stop=c == chunks - 1)
                    if n % 2 == 1 or n == groups * chunks - 1:
                        ins.then_inc(tile_done, 1)
                    if norm_ and n == chunks // 2:
                        sums(norm_)
                    if between and n in between:
                        between[n]()

            def narrow(name, width, xs_name=None):
                t0, o0 = TILE0[name], OUT0[name]
                s = t0 % RING
                pe.wait_ge(lo_ready, t0 + 1)
                pe.wait_ge(out_read, o0 + 1 - 3)
                for tb in range(TB):
                    for k in range(KD):
                        if xs_name and tb == 0:
                            pe.wait_ge(xs_ready, XS0[xs_name] + k + 1)
                        x_hi, x_lo = (xs[:, k * 2 * S + part_ * S + tb * P:][:, 0:P] for part_ in range(2))
                        out = bank((o0 + tb) % 4, 0, width)
                        wh, wl = (w[s][:, k * P:k * P + width] for w in (w_hi, w_lo))
                        pe.matmul(out, x_hi, wh, start=k == 0, stop=False)
                        pe.matmul(out, x_hi, wl, start=False, stop=False)
                        ins = pe.matmul(out, x_lo, wh, start=False, stop=k == KD - 1)
                ins.then_inc(tile_done, 1)

            def turn_outputs(name, src, ready):
                pe.wait_ge(*ready)
                for k in range(KD):
                    if k >= 3:
                        pe.wait_ge(xs_ready, XS0[name] + k - 2)
                    for tb in range(TB):
                        ins = pe.transpose(bank(5 + k % 3, tb * P, (tb + 1) * P), src[:, tb * D + k * P:tb * D + (k + 1) * P], ident)
                    ins.then_inc(o_turn[name], 1)

            def mla():
                feature("dq", 3, "mix_0", norm_="mix_0")
                feature("dkv", 2, "mix_0")
                narrow("kr", ROPE)
                pe.wait_ge(loaded, 16 * 3)
                pe.matmul(bank(6, 0, 2 * S, slice(0, H)), relb[:, :], const("onehot", 0, 2 * S, slice(0, BUCKETS + 1)), start=True, stop=True)\
                  .then_inc(row_ready, 1)
                token_major("uq", 3, KQ, 0, "cq", os_, "cq")
                token_major("uk", 2, KKV, KQ, "cq", os_)
                token_major("uv", 2, KKV, KQ, None, os_)
                pe.wait_ge(out_read, OUT0["uv"] + 4)
                qs4 = q_st.rearrange("p (t h d) -> p t h d", t=TB, h=4)
                ks4 = k_st.rearrange("p (t h d) -> p t h d", t=TB, h=4)
                vt3 = v_tok.rearrange("p (t c) -> p t c", t=TB)
                with pe.Fori(0, H // 4) as i:
                    def turn(h):
                        for n, src in enumerate((qs4, ks4)):
                            for tb in range(TB):
                                at_ = (n * TB + tb) * P
                                ins = pe.transpose(bank(h % 2, at_, at_ + P, slice(0, QK)), src[:, tb, h, :], ident)
                        ins.then_inc(a_turn, 1)

                    def scores(h):
                        pe.wait_ge(a_qkT, i * 4 + (h + 1))
                        qk, b = qkT[h % 2][0:QK, :], 2 + h % 2
                        pe.matmul(bank(b, 0, P), qk[:, 0:P], qk[:, S:S + P], start=True, stop=False)
                        pe.matmul(bank(b, 0, P), chunk_u[:, :], chunk_v[:, :], start=False, stop=True)
                        pe.matmul(bank(b, P, 3 * P), qk[:, P:S], qk[:, S:2 * S], start=True, stop=False)
                        pe.matmul(bank(b, 2 * P, 3 * P), chunk_u[:, :], chunk_v[:, :], start=False, stop=True).then_inc(a_s, 1)

                    def turn_probs(h):
                        pe.wait_ge(a_exp, i * 8 + 2 * (h + 1))
                        for n in range(3):
                            ins = pe.transpose(bank(4 + h % 2, n * P, (n + 1) * P), prob[h % 2][:, n * P:(n + 1) * P], ident)
                        ins.then_inc(a_pT, 1)

                    def values(h):
                        pe.wait_ge(a_pTs, i * 4 + (h + 1))
                        if h < 2:
                            pe.wait_ge(a_o, i * 4)
                        else:
                            pe.wait_ge(a_o, i * 4 + (h - 1))
                        b, pT = 6 + h % 2, probT[h % 2]
                        v = [vt3[:, tb, bass.ds(i * (4 * VD) + h * VD, VD)] for tb in range(TB)]
                        pe.matmul(bank(b, 0, VD), pT[:, 0:P], v[0], start=True, stop=True)
                        pe.matmul(bank(b, VD, 2 * VD), pT[:, P:2 * P], v[0], start=True, stop=False)
                        pe.matmul(bank(b, VD, 2 * VD), pT[:, 2 * P:3 * P], v[1], start=False, stop=True).then_inc(a_pv, 1)

                    pe.wait_ge(a_st, i + 1)
                    turn(0)
                    turn(1)
                    scores(0)
                    scores(1)
                    turn_probs(0)
                    turn(2)
                    scores(2)
                    values(0)
                    turn_probs(1)
                    turn(3)
                    scores(3)
                    values(1)
                    turn_probs(2)
                    values(2)
                    turn_probs(3)
                    values(3)
                turn_outputs("o_a", o_tok, (a_o, H))

            def mlstm():
                feature("mgate", 2, "mix_1", norm_="mix_1")
                feature("mqk", 8, "mix_1")
                token_major("mv", 2, KD)
                feature("mo", 8, "mix_1")
                pe.wait_ge(m_rows, 1)
                for tb in range(TB):
                    ins = pe.transpose(bank(7, tb * MH, (tb + 1) * MH), m_a[:, tb * P:(tb + 1) * P], con[0:MH, CONST["ident"]:CONST["ident"] + MH])
                ins.then_inc(m_at, 1)
                pe.wait_ge(m_floor, 1)
                pe.wait_ge(scaled, half0["mo"] + 8)

                def spread(h):
                    if h >= 1:
                        pe.wait_ge(m_logw, h)
                    pe.matmul(bank(4), const("select", h * P, (h + 1) * P, slice(0, MH)), m_bc, start=True, stop=True).then_inc(m_bcd, 1)

                def scores(h):
                    if h >= 1:
                        pe.wait_ge(m_ptd, h)
                    q, k = (m_qk[:, (n * MH + h) * S:(n * MH + h + 1) * S] for n in range(2))
                    pe.matmul(bank(5, 0, S), k[:, 0:P], q, start=True, stop=True)
                    pe.matmul(bank(5, S, S + P), k[:, P:S], q[:, P:S], start=True, stop=True).then_inc(m_st, 1)

                def outputs(h):
                    pt = m_pt[h % 2]
                    pe.wait_ge(m_ptd, h + 1)
                    if h >= 1:
                        pe.wait_ge(m_absd, h)
                    pe.matmul(bank(6, 0, S), ones[:, :], pt[:, 0:S], start=True, stop=False)
                    pe.matmul(bank(6, P, S), ones[:, :], pt[:, S:S + P], start=False, stop=True).then_inc(m_dend, 1)
                    if h >= 2:
                        pe.wait_ge(m_hc, h - 1)
                    for v in range(2):
                        cols = h * MV + v * P
                        pe.matmul(bank(h % 2, v * S, (v + 1) * S), m_v[:, cols:cols + P], pt[:, 0:S], start=True, stop=False)
                        ins = pe.matmul(bank(h % 2, v * S + P, (v + 1) * S), m_v[:, D + cols:D + cols + P], pt[:, S:S + P],
                                        start=False, stop=True)
                    ins.then_inc(m_num, 1)

                def head_squares(h):
                    pe.wait_ge(m_sqd, h + 1)
                    if h >= 1:
                        pe.wait_ge(m_stdd, h)
                    pe.matmul(bank(7, 0, S), ones[:, :], m_sq[h % 2][:, 0:S], start=True, stop=False)
                    pe.matmul(bank(7, 0, S), ones[:, :], m_sq[h % 2][:, S:2 * S], start=False, stop=True).then_inc(m_ss, 1)

                spread(0)
                scores(0)
                for h in range(MH):
                    if h + 1 < MH:
                        spread(h + 1)
                    outputs(h)
                    if h + 1 < MH:
                        scores(h + 1)
                    head_squares(h)

            def nsa_kv():
                token_major("kv", 2, KD, 0, "kvn", xs, "kvn")
                feature("kvc", 8, "kvn")

            def keys_turned():
                pe.wait_ge(c_kn, 1)
                for b in range(4):
                    for tb in range(TB):
                        ins = pe.transpose(bank(6 + b // 2, b % 2 * S + tb * P, b % 2 * S + (tb + 1) * P),
                                           kn_tok[:, tb * 512 + b * P:tb * 512 + (b + 1) * P], ident)
                ins.then_inc(c_kt, 1)

            def compress():
                pe.wait_ge(c_loaded, 16 * 4)
                pe.wait_ge(scaled, half0["kvc"] + 8)
                for j in range(2):
                    for n in range(CBLOCK // 2):
                        w = w1c[j][:, n * P:(n + 1) * P]
                        blk = c_dup[j].rearrange("p (g s) -> p g s", g=G + 1)[:, :, 2 * n:2 * n + CSTRIDE * (NC - 1) + 1:CSTRIDE]
                        ins = pe.matmul(bank(4, j * P, j * P + (G + 1) * NC), w, blk, start=n == 0, stop=n == CBLOCK // 2 - 1)
                ins.then_inc(c_hd, 1)

            def compressed():
                pe.wait_ge(c_gelu, 1)
                pe.wait_ge(c_kT, 2)
                pe.matmul(bank(6, 0, G * NC), w2c[0], c_hid[0], start=True, stop=True).then_inc(c_kc, 1)
                pe.wait_ge(c_gelu, 2)
                pe.matmul(bank(7, 0, DH, slice(0, G * NC)), c_hid[1], w2c[1][:, 0:DH], start=True, stop=True).then_inc(c_vcd, 1)

            def compressed_sums():
                pe.wait_ge(c_kcsqd, 1)
                pe.matmul(bank(5, 64, 64 + G * NC), const("blockdiag", 0, P), c_kcsq, start=True, stop=True).then_inc(c_kcss, 1)

            def nsa():
                def turn_queries(g):
                    pe.wait_ge(out_read, OUT0["nq"] + 2 * g + 2)
                    if g:
                        pe.wait_ge(n_cTs, 2)
                    for j in range(4):
                        for tb in range(TB):
                            col = j % 2 * S + tb * P
                            ins = pe.transpose(bank(4 + j // 2, col, col + P), nq_tok[:, tb * D + (4 * g + j) * P:][:, 0:P], ident)
                    ins.then_inc(n_turn, 1)

                def compressed_scores(g):
                    pe.wait_ge(n_qTd, 2 * g + 2)
                    if g:
                        pe.wait_ge(n_co, 1)
                    for j in range(4):
                        for tb in range(TB):
                            at_ = (4 * g + j) * S + tb * P
                            ins = pe.matmul(bank(6, tb * P + j * 32, tb * P + j * 32 + 2 * NC), n_qTa[:, at_:at_ + P],
                                            kcT[:, j % 2 * 2 * NC:(j % 2 + 1) * 2 * NC], start=True, stop=True)
                    ins.then_inc(n_cs, 1)

                def compressed_turn(g):
                    pe.wait_ge(n_cexp, 2 * g + 2)
                    pe.wait_ge(n_qTd, 2 * g + 2)
                    for tb in range(TB):
                        for j in range(2):
                            cols = (2 * g + j) * G * NC
                            ins = pe.transpose(bank(4 + tb, j * P, (j + 1) * P, slice(0, G * NC)), n_cl[tb][:, cols:cols + G * NC], ident)
                    ins.then_inc(n_cT, 1)

                def compressed_values(g):
                    pe.wait_ge(n_cTs, 2 * g + 2)
                    for tb in range(TB):
                        for j in range(2):
                            ins = pe.matmul(bank(6 + tb, j * S, (j + 1) * S), n_cpT[:, tb * S + j * P:tb * S + (j + 1) * P], vc[:, :],
                                            start=True, stop=True)
                    ins.then_inc(n_cpv, 1)

                def scores(i, w):
                    gp, e = w // 2, w % 2
                    pe.wait_ge(n_q, i * 4 + 2 * (gp + 1))
                    if not (isinstance(i, int) and 4 * i + w < 2):
                        pe.wait_ge(n_log, i * 4 + (w - 1))
                    for br in range(2):
                        q, k = n_qT[gp][e], kT[:, (br * 2 + gp) * S:(br * 2 + gp + 1) * S]
                        pe.matmul(bank(2 * e + br, 0, P), q[:, 0:P], k[:, 0:P], start=True, stop=True)
                        ins = pe.matmul(bank(2 * e + br, P, 3 * P), q[:, P:S], k, start=True, stop=True)
                    ins.then_inc(n_s, 1)

                def turn_probs(i, w):
                    pe.wait_ge(n_exp, i * 16 + 4 * (w + 1))
                    first = isinstance(i, int) and 4 * i + w == 0
                    for br in range(2):
                        if first:
                            pe.wait_ge(n_cTs, 4)
                        else:
                            pe.wait_ge(n_pTd, i * 8 + (2 * w + br - 1))
                        for n in range(3):
                            col = br * 384 + n * P
                            ins = pe.transpose(bank(4 + br, n * P, (n + 1) * P), n_p[w % 2][:, col:col + P], ident)
                        ins.then_inc(n_pT, 1)

                def values(i, w):
                    pe.wait_ge(n_pTd, i * 8 + 2 * (w + 1))
                    if isinstance(i, int) and 4 * i + w < 2:
                        pe.wait_ge(n_co, 2)
                    else:
                        pe.wait_ge(n_od, i * 4 + (w - 1))
                    b = 6 + w % 2
                    for br in range(2):
                        pT = n_pTs[w % 2][:, br * 384:(br + 1) * 384]
                        v = [vtok[:, tb * 512 + br * S + w // 2 * P:][:, 0:P] for tb in range(TB)]
                        first, second = (bank(b, (2 * br + tb) * P, (2 * br + tb + 1) * P) for tb in range(TB))
                        pe.matmul(first, pT[:, 0:P], v[0], start=True, stop=True)
                        pe.matmul(second, pT[:, P:2 * P], v[0], start=True, stop=False)
                        ins = pe.matmul(second, pT[:, 2 * P:3 * P], v[1], start=False, stop=True)
                    ins.then_inc(n_pv, 1)

                narrow("ngate", 3 * H, "mid_1")
                sums("mid_1")
                pe.wait_ge(c_end, 2)
                token_major("nq", 2, KD, between={9: lambda: turn_queries(0), 11: lambda: compressed_scores(0),
                                                  13: lambda: compressed_turn(0), 15: lambda: compressed_values(0)})
                turn_queries(1)
                compressed_scores(1)
                scores(0, 0)
                scores(0, 1)
                compressed_turn(1)
                compressed_values(1)

                def four(i):
                    first, last = (isinstance(i, int) and i == j for j in (0, HG - 1))
                    for w in range(4):
                        if not (last and w >= 2):
                            scores(i if w < 2 else i + 1, (w + 2) % 4)
                        turn_probs(i, w)
                        if not (first and w == 0):
                            values(i if w else i - 1, (w - 1) % 4)

                four(0)
                with pe.Fori(1, HG - 1) as i:
                    four(i)
                four(HG - 1)
                values(HG - 1, 3)
                turn_outputs("o_n", no_tok, (n_od, H))

            def after(event, first):
                return lambda c: (event, first + c + 1)

            mla()
            residual("wo_a", 1, KD, os_, after(xs_ready, XS0["o_a"]))
            feature("up_0", FF1, "ffn_0", norm_="ffn_0")
            residual("down_0", FF1 // BLK, FF1, hs, after(hs_ready, hid0["up_0"]))
            mlstm()
            residual("wo_m", 1, KD, os_, after(xs_ready, XS0["o_m"]))
            feature("up_1", FF1, "ffn_1", norm_="ffn_1")
            residual("down_1", FF1 // BLK, FF1, hs, after(hs_ready, hid0["up_1"]))
            feature("glu_0", 2 * FF2, "pre_0", norm_="pre_0")
            residual("out_0", FF2_TILES, FF2, hs, after(hs_ready, hid0["glu_0"]))
            feature("cin", 3 * KD, "mid_0", norm_="mid_0")
            residual("cout", 1, KD, hs, after(hs_ready, hid0["cin"]))
            feature("glu_1", 2 * FF2, "post_0", norm_="post_0")
            residual("out_1", FF2_TILES, FF2, hs, after(hs_ready, hid0["glu_1"]))
            nsa_kv()
            feature("glu_2", 2 * FF2, "pre_1", os_, between={1: keys_turned, 8: compress, 11: compressed, 13: compressed_sums})
            residual("out_2", FF2_TILES, FF2, hs, after(hs_ready, hid0["glu_2"]))
            nsa()
            residual("wo_n", 1, KD, os_, after(xs_ready, XS0["o_n"]))
            feature("glu_3", 2 * FF2, "post_1", norm_="post_1")
            residual("out_3", FF2_TILES, FF2, hs, after(hs_ready, hid0["glu_3"]))


def feature_tiles(w):
    k, m = w.shape[0] // P, w.shape[1] // P
    per = -(-k // BLK)
    out = np.zeros((m, P, per * BLK, P), np.float32)
    out[:, :, :k] = w.reshape(k, P, m, P).transpose(2, 1, 0, 3)
    return out.reshape(m, P, per, TILE).transpose(0, 2, 1, 3).reshape(m * per, P, TILE)


def token_tiles(w):
    k, g = w.shape[0] // P, w.shape[1] // 512
    out = np.zeros((-(-k * g // 2) * 2, P, 512), np.float32)
    out[:k * g] = w.reshape(k, P, g, 512).transpose(2, 0, 1, 3).reshape(k * g, P, 512)
    return out.reshape(-1, 2, P, 512).transpose(0, 2, 1, 3).reshape(-1, P, TILE)


def narrow_tile(w):
    out = np.zeros((P, KD, P), np.float32)
    out[:, :, :w.shape[1]] = w.reshape(KD, P, -1).transpose(1, 0, 2)
    return out.reshape(1, P, TILE)


def interleave(*ws):
    k = ws[0].shape[0]
    return np.stack([w.reshape(k, -1, P) for w in ws], axis=2).reshape(k, -1)


_OUT = ((D, S), "float32")


def kernel(**inputs):
    import concourse.bacc as bacc
    from concourse.bass_utils import run_bass_kernel_spmd

    a = {n: np.asarray(v) for n, v in inputs.items()}
    heads = np.array([g * HG + hg for hg in range(HG) for g in range(G)])
    w_ukv = a["mla_w_ukv"][0].reshape(KV_RANK, H, NOPE + VD)
    w_dkv = a["mla_w_dkv"][0]
    m_in, w_if = a["mlstm_w_in"][0], a["mlstm_w_if"][0]
    mqk = 2 * MH * MQK
    kv = a["w_kv_2"].reshape(D, 3, 2, G, DH)
    wq = a["attn_w_q_2"][0]
    glu, out, mlp1, mlp2 = {}, {}, a["ffn_w1"], a["ffn_w2"]
    for n, (which, layer) in enumerate((("ffn1", 0), ("ffn2", 0), ("ffn1", 1), ("ffn2", 1))):
        w = a[f"{which}_w_in_2"][layer]
        glu[n] = feature_tiles(interleave(w[:, :FF2 * P], w[:, FF2 * P:]))
        out[n] = feature_tiles(a[f"{which}_w_out_2"][layer])
    w_cin = a["conv_w_in_2"][0]
    stream = [
        feature_tiles(a["mla_w_dq"][0]), feature_tiles(w_dkv[:, :KV_RANK]), narrow_tile(w_dkv[:, KV_RANK:]),
        token_tiles(a["mla_w_uq"][0]), token_tiles(w_ukv[:, :, :NOPE].reshape(KV_RANK, -1)),
        token_tiles(w_ukv[:, :, NOPE:].reshape(KV_RANK, -1)), feature_tiles(a["mla_w_o"][0]),
        feature_tiles(mlp1[0]), feature_tiles(mlp2[0]),
        narrow_tile(w_if[:, :MH]), narrow_tile(w_if[:, MH:]), feature_tiles(m_in[:, :mqk]),
        token_tiles(m_in[:, mqk:mqk + MH * MV]), feature_tiles(m_in[:, mqk + MH * MV:]), feature_tiles(a["mlstm_w_o"][0]),
        feature_tiles(mlp1[1]), feature_tiles(mlp2[1]),
        glu[0], out[0], feature_tiles(interleave(w_cin[:, :D], w_cin[:, D:2 * D], w_cin[:, 2 * D:])),
        feature_tiles(a["conv_w_out_2"][0]), glu[1], out[1],
        token_tiles(kv[:, 1:, :, :, :].transpose(0, 2, 1, 3, 4).reshape(D, -1)),
        feature_tiles(np.stack([kv[:, 0], kv[:, 0]], axis=3).reshape(D, -1)), glu[2], out[2],
        narrow_tile(wq[:, H * DH:].reshape(D, H, 3)[:, heads].reshape(D, -1)),
        token_tiles(wq[:, :H * DH].reshape(D, H, DH)[:, heads].reshape(D, -1)),
        feature_tiles(a["attn_w_o_2"][0].reshape(H, DH, D)[heads].reshape(D, D)), glu[3], out[3],
    ]
    tiles = np.concatenate(stream)
    assert tiles.shape[0] == N_TILES

    vecs = np.zeros((P, N_VEC), np.float32)

    def put(name, v):
        v = v.reshape(-1, min(P, v.shape[-1])).T
        vecs[:v.shape[0], VEC[name]:VEC[name] + v.shape[1]] = v

    for name, v in (("mix_0", a["norm_mix"][0]), ("ffn_0", a["norm_ffn"][0]), ("mix_1", a["norm_mix"][1]), ("ffn_1", a["norm_ffn"][1]),
                    ("pre_0", a["ffn1_norm_2"][0]), ("mid_0", a["mix_norm_2"][0]), ("post_0", a["ffn2_norm_2"][0]),
                    ("kvn", a["kv_norm_2"]), ("pre_1", a["ffn1_norm_2"][1]), ("mid_1", a["mix_norm_2"][1]),
                    ("post_1", a["ffn2_norm_2"][1]), ("q_norm", a["mla_q_norm"][0]), ("kv_norm", a["mla_kv_norm"][0]),
                    ("head_norm", a["mlstm_head_norm"][0]), ("taps", a["conv_w_2"][0].reshape(-1)),
                    ("kc_norm", np.concatenate([a["k_norm_2"][0]] * 2)),
                    ("nq_norm", np.concatenate([a["attn_q_norm_2"][0]] * 2)), ("b_i", a["mlstm_b_if"][0][:MH]),
                    ("b_f", a["mlstm_b_if"][0][MH:]), ("pe_k", a["cmp_pe_k_2"].reshape(-1)), ("pe_v", a["cmp_pe_v_2"].reshape(-1))):
        put(name, v)
    rows = np.concatenate([a["mla_q_gain"][0], a["mla_k_gain"][0], a["attn_q_norm_2"][0], a["k_norm_2"][1], a["k_norm_2"][2]])
    w2 = [np.concatenate([a[n]] * 2, axis=1) for n in ("cmp_w2_k_2", "cmp_w2_v_2")]
    arrays = {
        "x_in": np.ascontiguousarray(a["x"][0].T), "tiles": tiles, "vecs": vecs, "rows": rows, "consts": constants(),
        "rel_bias": np.ascontiguousarray(a["rel_bias_2"][:, heads]), "w1c_k": a["cmp_w1_k_2"], "w1c_v": a["cmp_w1_v_2"],
        "w2c_k": w2[0], "w2c_v": w2[1],
    }
    nc = bacc.Bacc("TRN2", target_bir_lowering=False, num_devices=1)
    args = [nc.dram_tensor(n, v.shape, mybir.dt.from_np(v.dtype), kind="ExternalInput").ap() for n, v in arrays.items()]
    y = nc.dram_tensor("y_out", _OUT[0], F32, kind="ExternalOutput").ap()
    build(nc, *args, y)
    r = run_bass_kernel_spmd(nc, [arrays], core_ids=[0])
    return np.ascontiguousarray(r.results[0]["y_out"].T)[None]
```

```python
from contextlib import ExitStack

import numpy as np

import concourse.bass as bass
from concourse import mybir

F32 = mybir.dt.float32
F32R = mybir.dt.float32r
ACT = mybir.ActivationFunctionType
ALU = mybir.AluOpType
AX_X = mybir.AxisListType.X

P = 128
S = 256
TB = S // P
D = 1024
KD = D // P
BLK = 8
TILE = BLK * P
RING = 4
BANK = 512
EPS = 1e-6
NEG = -1e30

Q_RANK, KV_RANK = 384, 256
H, NOPE, ROPE, VD = 16, 64, 32, 64
QK = NOPE + ROPE
HALF = ROPE // 2
KQ, KKV = Q_RANK // P, KV_RANK // P

MH, MQK, MV = 4, 128, 256
GATE_CAP = 15.0

FF1 = 4096 // P
FF2 = 2816 // P
FF2_TILES = -(-FF2 // BLK)
TAPS = 3

G, HG, DH = 4, 4, 64
NC, CSTRIDE, CBLOCK = 15, 16, 32
NC0 = 7
BUCKETS = 32

STAGES = [
    ("dq", 3, 3), ("dkv", 2, 2), ("kr", 1, 1), ("uk", 2, 4), ("uq", 5, 6), ("uv", 2, 4), ("wo_a", 8, 8),
    ("up_0", 32, 32), ("down_0", 32, 8),
    ("mgate", 2, 2), ("mqk", 8, 8), ("mv", 8, 4), ("mo", 8, 4), ("wo_m", 8, 8),
    ("up_1", 32, 32), ("down_1", 32, 8),
    ("glu_0", 44, 44), ("out_0", 24, 8), ("cin", 24, 24), ("cout", 8, 8), ("glu_1", 44, 44), ("out_1", 24, 8),
    ("kv", 8, 4), ("kvc", 8, 8), ("glu_2", 44, 44), ("out_2", 24, 8),
    ("ngate", 1, 1), ("nq", 8, 4), ("wo_n", 8, 8), ("glu_3", 44, 44), ("out_3", 24, 8),
]
TILE0, OUT0 = {}, {}
N_TILES = N_OUTS = 0
for _name, _tiles, _outs in STAGES:
    TILE0[_name], OUT0[_name] = N_TILES, N_OUTS
    N_TILES, N_OUTS = N_TILES + _tiles, N_OUTS + _outs

VEC = {}
N_VEC = 0
for _name, _n in [("mix_0", 8), ("ffn_0", 8), ("mix_1", 8), ("ffn_1", 8), ("pre_0", 8), ("mid_0", 8), ("post_0", 8),
                  ("kvn", 8), ("pre_1", 8), ("mid_1", 8), ("post_1", 8), ("q_norm", KQ), ("kv_norm", KKV),
                  ("head_norm", 8), ("taps", TAPS * KD), ("kc_norm", 1), ("nq_norm", 1), ("b_i", 1), ("b_f", 1),
                  ("pe_k", 16), ("pe_v", 16)]:
    VEC[_name] = N_VEC
    N_VEC += _n
ROW = {"q_gain": 0, "k_gain": QK, "nq": 2 * QK, "ks": 2 * QK + DH, "kw": 2 * QK + 2 * DH}
N_ROW = 2 * QK + 3 * DH
COPIES = 16
CONST = {}
N_CONST = 0
for _name, _n in [("ident", P), ("blockdiag", P), ("causal", P), ("select", MH * P), ("onehot", 2 * S), ("cos", TB * ROPE),
                  ("sin", TB * ROPE), ("valid", TB), ("groups", G)]:
    CONST[_name] = N_CONST
    N_CONST += _n


def constants():
    c = np.zeros((P, N_CONST), np.float32)

    def put(name, a):
        c[:a.shape[0], CONST[name]:CONST[name] + a.shape[1]] = a

    put("ident", np.eye(P))
    put("blockdiag", np.kron(np.eye(2), np.ones((DH, DH))))
    put("causal", np.triu(np.ones((P, P))))
    put("select", np.kron(np.eye(MH), np.ones((1, P))))
    rel = S - 1 - np.arange(2 * S)
    n = np.maximum(rel, 0)
    exact, most = BUCKETS // 2, 4096
    nf = np.maximum(n, 1).astype(np.float32)
    large = exact + (np.log(nf / np.float32(exact)) / np.float32(np.log(most / exact))
                     * np.float32(BUCKETS - exact)).astype(np.int32)
    bucket = np.where(n < exact, n, np.minimum(large, BUCKETS - 1))
    hot = np.zeros((BUCKETS + 1, 2 * S))
    hot[bucket, np.arange(2 * S)] = rel >= 0
    hot[BUCKETS] = np.where(rel < 0, NEG, 0.0)
    put("onehot", hot)
    freq = np.float32(10000.0) ** (-np.arange(HALF, dtype=np.float32) / np.float32(HALF))
    ang = (np.arange(S, dtype=np.float32)[:, None] * freq[None, :]).astype(np.float32)
    for name, f in (("cos", np.concatenate([np.cos(ang)] * 2, axis=1)), ("sin", np.concatenate([-np.sin(ang), np.sin(ang)], axis=1))):
        put(name, f.reshape(TB, P, ROPE).transpose(1, 0, 2).reshape(P, TB * ROPE))
    put("valid", (np.arange(S) >= CBLOCK - 1).astype(np.float32).reshape(TB, P).T)
    put("groups", np.kron(np.eye(G), np.ones((NC, 1))))
    at = CONST["onehot"]
    for tb in range(TB):
        c[QK + tb, at + tb * P:at + tb * P + 64] = 1.0
        c[QK + tb, at + S + tb * P + 64:at + S + (tb + 1) * P] = NEG
    return c


def build(nc, x_in, tiles, vecs, rows, consts, rel_bias, w1c_k, w1c_v, w2c_k, w2c_v, y_out):
    ctx = ExitStack()
    with ctx:
        def sb(name, shape, dt=F32):
            return ctx.enter_context(nc.sbuf_tensor(name, shape, dt))

        def sem(name):
            return ctx.enter_context(nc.semaphore(name))

        raw = [sb(f"raw{s}", [P, TILE]) for s in range(RING)]
        w_hi = [sb(f"w_hi{s}", [P, TILE], F32R) for s in range(RING)]
        w_lo = [sb(f"w_lo{s}", [P, TILE], F32R) for s in range(RING)]
        x = sb("x", [P, KD * S])
        with nc.sbuf_tensor("w1c_all", [P, 2 * 16 * P], F32) as w1c_all:
            pass
        xs = sb("xs", [P, KD * 2 * S], F32R)
        half = [sb(f"half{s}", [P, S]) for s in range(4)]
        fsum = [sb(f"fsum{s}", [P, S]) for s in range(4)]
        sq = [sb(f"sq{s}", [P, S]) for s in range(4)]
        sil = [sb(f"sil{s}", [P, S]) for s in range(2)]
        vec = sb("vec", [P, N_VEC])
        row = sb("row", [P, N_ROW])
        con = sb("con", [P, N_CONST])
        ones = sb("ones", [P, P])
        eps = sb("eps", [P, 1])
        std = sb("std", [P, 64])
        rstd = sb("rstd", [P, 64])
        ssq = sb("ssq", [P, S])
        stdb = sb("stdb", [P, S])
        rb = sb("rb", [P, S])
        with nc.sbuf_tensor("os", [P, KD * 2 * S], F32R) as os_:
            pass
        bias = sb("bias", [P, H * S])
        relb = sb("relb", [BUCKETS + 1, H])
        bias_row = sb("bias_row", [H, 2 * S])
        kT = sb("kT", [P, 4 * S])
        vtok = sb("vtok", [P, TB * 2 * G * DH])
        kcT = sb("kcT", [P, G * NC])
        vc = sb("vc", [G * NC, G * DH])
        with nc.sbuf_tensor("hs", [P, FF1 * 2 * S], F32R) as hs:
            pass
        arena = sb("arena", [P, FF1 * 2 * S])

        def part(at, n):
            return arena[:, at:at + n]

        psum = ctx.enter_context(nc.psum_tensor("psum", [P, 8 * BANK], F32))

        def bank(b, a=0, z=BANK, p=slice(None)):
            return psum[p, b * BANK + a:b * BANK + z]

        def const(name, a, z, p=slice(None)):
            at = CONST[name]
            return con[p, at + a:at + z]

        ident = const("ident", 0, P)
        STAT, RB = 4, 5

        tile_loaded = [sem(f"tile_loaded{s}") for s in range(RING)]
        hi_ready, lo_ready = sem("hi_ready"), sem("lo_ready")
        tile_done = sem("tile_done")
        out_read = sem("out_read")
        half_ready = sem("half_ready")
        x_loaded, loaded = sem("x_loaded"), sem("loaded")
        scaled = sem("scaled")
        const_ready = sem("const_ready")
        ssq_ready = sem("ssq_ready")
        stat_done, std_ready = sem("stat_done"), sem("std_ready")
        sq_ready = sem("sq_ready")
        xhi_ready, xs_ready = sem("xhi_ready"), sem("xs_ready")
        hid_ready, hhi_ready, hs_ready = sem("hid_ready"), sem("hhi_ready"), sem("hs_ready")
        sil_ready = sem("sil_ready")
        x_half = sem("x_half")
        dve_step = sem("dve_step")
        stored = sem("stored")
        row_ready = sem("row_ready")
        bias_done, bias_out, bias_in = sem("bias_done"), sem("bias_out"), sem("bias_in")
        head_sq, head_sum, head_std = sem("head_sq"), sem("head_sum"), sem("head_std")
        head_k, a_mask, a_rope = sem("head_k"), sem("a_mask"), sem("a_rope")
        a_keys, pool_step = sem("a_keys"), sem("pool_step")
        a_st, a_turn, a_qkT, a_s, a_max, a_exp = (sem(f"a_{n}") for n in ("st", "turn", "qkT", "s", "max", "exp"))
        a_pT, a_pTs, a_pv, a_o = (sem(f"a_{n}") for n in ("pT", "pTs", "pv", "o"))
        o_turn = {n: sem(f"turn_{n}") for n in ("o_a", "o_m", "o_n")}
        m_gates, m_tanh, m_rows, m_at, m_cols, m_floor, m_bcd, m_st, m_logw, m_exp, m_ptd = (
            sem(f"m_{n}") for n in ("gates", "tanh", "rows", "at", "cols", "floor", "bcd", "st", "logw", "exp", "ptd"))
        m_one_, m_num, m_hd, m_sqd, m_stdd, m_gated = (sem(f"m_{n}") for n in ("one", "num", "hd", "sqd", "stdd", "gated"))
        c_loaded, c_sqd, c_sum, c_std, c_bias, c_gelu, c_kc, c_kcsqd, c_kcss, c_kcstdd = (
            sem(f"c_{n}") for n in ("loaded", "sqd", "sum", "std", "bias", "gelu", "kc", "kcsqd", "kcss", "kcstdd"))
        c_kn, c_kt, c_kT, c_hd, c_vcd, c_end = (sem(f"c_{n}") for n in ("kn", "kt", "kT", "hd", "vcd", "end"))
        n_gturn, n_sqd, n_sum, n_std_, n_turn, n_qTd, n_cs, n_clog, n_cexp, n_cT, n_cTs, n_cpv, n_co = (
            sem(f"n_{n}") for n in ("gturn", "sqd", "sum", "std", "turn", "qTd", "cs", "clog", "cexp", "cT", "cTs", "cpv", "co"))
        n_gs, n_pg = sem("n_gs"), sem("n_pg")
        n_zero = sem("n_zero")
        n_q, n_s, n_log, n_max, n_exp, n_pT, n_pTd, n_pv, n_od = (
            sem(f"n_{n}") for n in ("q", "s", "log", "max", "exp", "pT", "pTd", "pv", "od"))

        half0, hid0, sil0, n_half, n_hid, n_sil = {}, {}, {}, 0, 0, 0
        for name, _, outs in STAGES:
            half0[name], hid0[name], sil0[name] = n_half, n_hid, n_sil
            kind = name.split("_")[0]
            if kind in ("dq", "dkv", "kr", "ngate", "up", "mgate", "mqk", "glu", "cin", "kvc"):
                n_half += outs
            n_hid += {"up": outs, "glu": outs // 2, "cin": outs // 3}.get(kind, 0)
            n_sil += {"glu": outs // 2}.get(kind, 0)
        RES = [n for n, _, _ in STAGES if n.split("_")[0] in ("wo", "down", "out", "cout")]

        class Steps:

            def __init__(self):
                self.base, self.n = 0, 0

            def mark(self, ins):
                ins.then_inc(dve_step, 1)
                self.n += 1
                return self.base + self.n

        def at(t, start, n):
            return t[:, start:start + n] if isinstance(start, int) else t[:, bass.ds(start, n)]

        cqf = part(0, (KQ + KKV) * S)
        q_tok = part(2048, TB * H * QK)
        k_tok = part(2048 + 3072, TB * H * NOPE)
        v_tok = part(2048 + 5120, TB * H * VD)
        o_tok = part(0, TB * H * VD)
        kr_tok = part(9216, TB * ROPE)
        ss = part(9280, 4 * H + 2)
        rope_t = [part(9408 + P * j, P) for j in range(2)]
        mscr = [part(9664 + 1024 * j, 1024) for j in range(3)]
        HEAD_SQ = [(k_tok[:, tb * 1024:(tb + 1) * 1024], NOPE, 2 * H + tb * H) for tb in range(TB)] + [(kr_tok, ROPE, 4 * H)]
        HEAD_SQ += [(q_tok[:, tb * 1536 + j * 768:tb * 1536 + (j + 1) * 768], QK, tb * H + j * 8) for j in range(2) for tb in range(TB)]
        prob = [part(9664 + 384 * j, 384) for j in range(2)]
        probT = [part(9664 + 768 + 384 * j, 384) for j in range(2)]
        q_st = [part(12736 + 768 * j, TB * 2 * QK) for j in range(2)]
        k_st = [part(12736 + 768 * j + 384, TB * 2 * QK) for j in range(2)]
        qkT = [part(14272 + 512 * j, 512) for j in range(2)]
        mx, nmx, rsum, rinv = ([part(15296 + 8 * j + 2 * u, TB) for u in range(4)] for j in range(4))

        turn_bank, score_bank = ([(OUT0["uv"] + j + k) % 4 for k in range(2)] for j in (0, 2))
        gq, gk = row[:, ROW["q_gain"]:ROW["q_gain"] + QK], row[:, ROW["k_gain"]:ROW["k_gain"] + QK]
        kr3 = kr_tok.rearrange("p (t h d) -> p t h d", t=TB, h=1)
        cos, sin = (con[:, CONST[n]:CONST[n] + TB * ROPE].rearrange("p (t d) -> p t d", t=TB) for n in ("cos", "sin"))

        def rotate(engine, then, v, heads):
            a, b = (t[:, 0:TB * heads * ROPE].rearrange("p (t h d) -> p t h d", t=TB, h=heads) for t in rope_t)
            c4, s4 = (t.unsqueeze(2).to_broadcast([P, TB, heads, ROPE]) for t in (cos, sin))
            engine.tensor_tensor(a, v, c4, ALU.mult)
            engine.tensor_tensor(b[:, :, :, 0:HALF], v[:, :, :, HALF:], s4[:, :, :, 0:HALF], ALU.mult)
            then(engine.tensor_tensor(b[:, :, :, HALF:], v[:, :, :, 0:HALF], s4[:, :, :, HALF:], ALU.mult))
            return engine.tensor_tensor(v, a, b, ALU.add)

        ASQ = part(2048, KD * S)

        def ahead(step, i, u, n):
            if not (isinstance(i, int) and 4 * i + u + n >= H):
                step(i + 1 if u + n >= 4 else i, (u + n) % 4)

        def heads_loop(engine, *steps_):
            def four(i):
                for u in range(4):
                    for step in steps_:
                        step(i, u)

            four(0)
            with engine.Fori(1, H // 4 - 1) as i:
                four(i)
            four(H // 4 - 1)

        conv_b = [part(KD * 512 + j * S, S) for j in range(2)]
        conv_c = [part(KD * 512 + (2 + j) * S, S) for j in range(2)]
        conv_v = [part(KD * 512 + (4 + j) * S, S) for j in range(2)]
        conv_y = [part(KD * 512 + (6 + j) * S, S) for j in range(2)]
        conv_u = [part(KD * 512 + 8 * S + j * 2 * S, S + TAPS - 1) for j in range(2)]

        m_qk = part(0, 2 * MH * S)
        m_v = part(2048, TB * MH * (MV + 1))
        m_o = part(4128, TB * D)
        m_row = [arena[0:MH, 6208 + j * S:6208 + (j + 1) * S] for j in range(8)]
        m_ti, m_tf, m_nb, m_a, m_g, m_one = m_row[:6]
        m_ng, m_nm = m_row[6:]
        m_col = part(8256, 2 * TB * MH)
        m_w = [part(8320 + 384 * h, 384) for h in range(MH)]
        m_h = part(9856, TB * D)
        m_sq = part(11904, MV)
        m_nd, m_dn = ([part(12160 + 8 * j + TB * h, TB) for h in range(MH)] for j in range(2))
        m_ss, m_sr, m_r = (part(12176 + 8 * j, TB * MH) for j in range(3))

        w1c = [w1c_all[:, 16 * P * j:16 * P * (j + 1)] for j in range(2)]
        c_at = FF2 * 2 * S
        w2c = [part(c_at + P * j, P) for j in range(2)]
        c_dup = [part(c_at + 256 + (G + 1) * S * j, (G + 1) * S) for j in range(2)]
        kn_tok = part(c_at + 2816, TB * 2 * G * DH)
        c_sq = [part(c_at + 3840 + 512 * j, 512) for j in range(2)]
        c_ss = part(c_at + 4864, 16)
        c_r = part(c_at + 4880, 16)
        c_pe = part(c_at + 4896, 2)
        c_hid, c_kcsq, c_kcstd, c_kcr = ([part(c_at + 3840 + 64 * j, G * NC) for j in range(2)],
                                         *(part(c_at + 3840 + 64 * j, G * NC) for j in (2, 3, 4)))

        nq_tok = part(0, TB * D)
        no_tok = part(2048, TB * D)
        n_gate = part(4096, TB * 3 * H)
        n_sq = part(4224, TB * 512)
        n_r = part(6272, TB * H)
        n_ss = part(6304, TB * H)
        n_qTa = part(6336, 2 * D)
        n_qT = [[part(14720 + S * (2 * j + e), S) for e in range(2)] for j in range(2)]
        n_l = [part(8896 + 768 * j, 768) for j in range(2)]
        n_p = [part(10432 + 768 * j, 768) for j in range(2)]
        n_pTs = [part(11968 + 768 * j, 768) for j in range(2)]
        n_mx, n_nmx, n_rs, n_sc = ([part(13504 + 16 * j + 4 * w, 4) for w in range(4)] for j in range(4))
        n_cl = [part(13568 + H * NC * tb, H * NC) for tb in range(TB)]
        n_cmx, n_crs, n_csc = (part(14048 + TB * H * j, TB * H) for j in range(3))
        n_cpT = arena[0:G * NC, 14144:14144 + 2 * S]

        NORMS = ["mix_0", "cq", "ffn_0", "mix_1", "ffn_1", "pre_0", "mid_0", "post_0", "kvn", "mid_1", "post_1"]
        NEXT = dict(zip(RES, NORMS[2:]))
        TO_ROWS = [n for n in NORMS if n not in ("cq", "mid_1")]
        TO_COLUMNS = ["mix_0", "cq", "mix_1", "kvn", "mid_1"]
        SUMS = [n for n in NORMS if n != "cq"]
        STAT0 = {n: j + 1 for j, n in enumerate(NORMS)}
        SSQ0 = {n: (KD + 1) * j for j, n in enumerate(SUMS)}
        STD0, n_std = {}, 0
        for name in NORMS:
            n_std += (name in TO_ROWS) + (name in TO_COLUMNS) + (name == "cq")
            STD0[name] = n_std
        XS0, n_xs = {}, 0
        for name in ["mix_0", "cq", "o_a", "ffn_0", "mix_1", "o_m", "ffn_1", "pre_0", "mid_0", "post_0", "kvn", "pre_1", "mid_1",
                     "o_n", "post_1"]:
            XS0[name] = n_xs
            n_xs += KQ + KKV if name == "cq" else KD
        SQ0 = {"mix_0": 0, "cq": KD} | {name: KD + 1 + KD * j for j, name in enumerate(RES)}

        def hi_part(t, k):
            return t[:, k * 2 * S:k * 2 * S + S]

        def lo_part(t, k):
            return t[:, k * 2 * S + S:(k + 1) * 2 * S]

        bias_dram = nc.dram_tensor("bias_dram", (H, COPIES, 2 * S), F32, kind="Internal").ap()
        block = ctx.enter_context(nc.Block())

        @block.sync
        def _(sp):
            sp.dma_start(raw[0][:, :], tiles[0]).then_inc(tile_loaded[0], 16)
            sp.dma_start(vec[:, :], vecs).then_inc(x_loaded, 16)
            sp.dma_start(x[:, :].rearrange("p (k t) -> p k t", k=KD), x_in.rearrange("(k p) t -> p k t", p=P)).then_inc(x_loaded, 16)
            for s in range(1, RING):
                sp.dma_start(raw[s][:, :], tiles[s]).then_inc(tile_loaded[s], 16)
            sp.dma_start(con[:, :], consts).then_inc(loaded, 16)
            sp.dma_start(row[:, :], rows.partition_broadcast(P)).then_inc(loaded, 16)
            sp.dma_start(relb[0:BUCKETS, :], rel_bias).then_inc(loaded, 16)
            with sp.Fori(1, N_TILES // RING) as i:
                for s in range(RING):
                    sp.wait_ge(lo_ready, i * RING + (s + 1 - RING))
                    sp.dma_start(raw[s][:, :], tiles[bass.ds(i * RING + s, 1)].rearrange("o p n -> p (o n)")).then_inc(tile_loaded[s], 16)
            for t in range(N_TILES // RING * RING, N_TILES):
                s = t % RING
                sp.wait_ge(lo_ready, t + 1 - RING)
                sp.dma_start(raw[s][:, :], tiles[t]).then_inc(tile_loaded[s], 16)
            for k in range(KD):
                sp.wait_ge(out_read, OUT0["out_3"] + k + 1)
                sp.dma_start(y_out[k * P:(k + 1) * P, :], x[:, k * S:(k + 1) * S]).then_inc(stored, 16)
            sp.wait_ge(stored, 16 * KD)
            sp.wait_ge(bias_out, 16)

        @block.gpsimd
        def _(pool):
            pool.memset(ones[:, :], 1.0).then_inc(const_ready, 1)
            pool.memset(eps[:, :], EPS).then_inc(const_ready, 1)
            pool.wait_ge(const_ready, 2)
            pool.memset(relb[BUCKETS:BUCKETS + 1, :], 1.0).then_inc(const_ready, 1)
            pool.wait_ge(const_ready, 3)

            def take_lo(s, t):
                pool.wait_ge(hi_ready, t + 1)
                pool.tensor_tensor(w_lo[s][:, :], raw[s][:, :], w_hi[s][:, :].bitcast(F32), ALU.subtract).then_inc(lo_ready, 1)

            def stage(h, first):
                def cols(t, size):
                    return t.rearrange("p (t c) -> p t c", t=TB)[:, :, h * size:(h + 2) * size].rearrange("p t (h d) -> p t h d", h=2)

                def then(ins):
                    then.n += 1
                    ins.then_inc(pool_step, 1)
                    pool.wait_ge(pool_step, then.n)

                then.n = first
                qs, ks = (t[h // 2 % 2].rearrange("p (t h d) -> p t h d", t=TB, h=2) for t in (q_st, k_st))
                rk = cols(rstd[:, 2 * H:4 * H], 1)
                gains = gq.unsqueeze(1).unsqueeze(1).to_broadcast([P, TB, 2, QK])
                pool.tensor_tensor(ks[:, :, :, 0:NOPE], cols(k_tok, NOPE), rk.to_broadcast([P, TB, 2, NOPE]), ALU.mult)
                pool.tensor_tensor(ks[:, :, :, NOPE:QK], kr3.to_broadcast([P, TB, 2, ROPE]), rk.to_broadcast([P, TB, 2, ROPE]), ALU.mult)
                then(pool.tensor_tensor(qs, cols(q_tok, QK), gains, ALU.mult))
                rotate(pool, then, qs[:, :, :, NOPE:QK], 2).then_inc(a_st, 1)

            before = (TILE0["wo_a"] + RING - 1) // RING * RING
            for t in range(before):
                take_lo(t % RING, t)
                if t == TILE0["wo_a"] - 1:
                    pool.wait_ge(a_keys, 1)
                    for h in (0, 2):
                        stage(h, h)
            pool.wait_ge(out_read, OUT0["uq"] + 6)
            for h in range(4, H, 2):
                pool.wait_ge(a_turn, h - 2)
                stage(h, h)
            for t in range(before, before + RING):
                take_lo(t % RING, t)

            def tiles_between(first, last):
                with pool.Fori(first // RING, last // RING) as i:
                    for s in range(RING):
                        take_lo(s, i * RING + s)
                for t in range(last // RING * RING, last):
                    take_lo(t % RING, t)

            tiles_between(before + RING, TILE0["wo_n"] + RING)
            with pool.Fori(0, HG) as i:
                for w in range(4):
                    pool.wait_ge(n_gs, i * 4 + (w + 1))
                    for tb, (a, z) in enumerate([(0, P), (P, 3 * P)]):
                        probs = n_p[w % 2].rearrange("p (b c) -> p b c", b=2)[:, :, a:z]
                        ins = pool.tensor_tensor(probs, probs, n_sc[w][:, 2 * tb:2 * tb + 2].unsqueeze(2).to_broadcast([P, 2, z - a]), ALU.mult)
                    ins.then_inc(n_pg, 1)
            rest = (TILE0["wo_n"] + 2 * RING - 1) // RING * RING
            for t in range(TILE0["wo_n"] + RING, rest):
                take_lo(t % RING, t)
            tiles_between(rest, N_TILES)

        @block.scalar
        def _(act):
            def split(t, q=0):
                if isinstance(q, int) and t + RING * q >= N_TILES:
                    return
                s = t % RING
                act.wait_ge(tile_loaded[s], (q + (t // RING + 1)) * 16)
                if t >= RING:
                    act.wait_ge(tile_done, q * RING + (t + 1 - RING))
                act.activation(w_hi[s][:, :], raw[s][:, :], ACT.Copy).then_inc(hi_ready, 1)

            def take_half(name, b, o, t, q=0, p=slice(None)):
                act.wait_ge(tile_done, t + 1)
                if not (isinstance(o, int) and OUT0[name] + o < 4):
                    act.wait_ge(out_read, o + (OUT0[name] - 3))
                act.activation(half[b][p, :], bank(b, S, 2 * S, p), ACT.Copy).then_inc(half_ready, 1)

            def root(name):
                act.wait_ge(stat_done, STAT0[name])
                if name in TO_ROWS:
                    act.activation(stdb[:, :], bank(RB, 0, S), ACT.Sqrt, bias=eps[:, 0:1], scale=1.0 / D).then_inc(std_ready, 1)
                if name in TO_COLUMNS:
                    for col, size in [(4, Q_RANK), (6, KV_RANK)] if name == "cq" else [(0, D)]:
                        act.activation(std[:, col:col + TB], bank(STAT, col, col + TB), ACT.Sqrt, bias=eps[:, 0:1],
                                       scale=1.0 / size).then_inc(std_ready, 1)

            def split_x(dst, src, gain):
                act.activation(dst, src, ACT.Copy, scale=gain).then_inc(xhi_ready, 1)

            def plain(name, outs, p=slice(None), first=0):
                for o in range(first, outs):
                    t = TILE0[name] + o
                    take_half(name, (OUT0[name] + o) % 4, o, t, p=p)
                    split(t + RING)

            def used(name, tiles_):
                for t in range(TILE0[name], TILE0[name] + tiles_):
                    split(t + RING)

            def residual(name, per, outs=KD):
                t0, o0 = TILE0[name], OUT0[name]
                last = name == RES[-1]
                gain = 0 if last else VEC[NEXT[name]]

                def four(i):
                    for u in range(4):
                        for j in range(per):
                            split(t0 + u * per + j + RING, i * per)
                        if not last:
                            act.wait_ge(out_read, i * 4 + (o0 + u + 1))
                            split_x(at(xs, i * (8 * S) + u * 2 * S, S), at(x, i * (4 * S) + u * S, S), at(vec, i * 4 + (gain + u), 1))
                            act.activation(sq[u][:, :], at(x, i * (4 * S) + u * S, S), ACT.Square).then_inc(sq_ready, 1)
                if last:
                    for i in range(outs // 4):
                        four(i)
                else:
                    with act.Fori(0, outs // 4) as i:
                        four(i)

            def up(name):
                t0, o0 = TILE0[name], OUT0[name]
                with act.Fori(0, FF1 // 4) as i:
                    for u in range(4):
                        take_half(name, (o0 + u) % 4, i * 4 + u, i * 4 + (t0 + u))
                        split(t0 + u + RING, i)
                        act.wait_ge(hid_ready, i * 4 + (hid0[name] + u + 1))
                        act.activation(at(hs, i * (8 * S) + u * 2 * S, S), fsum[(o0 + u) % 4][:, :], ACT.Copy).then_inc(hhi_ready, 1)

            def glu(name, between=None):
                t0, o0 = TILE0[name], OUT0[name]
                between = between or {}

                def four(i):
                    for u in range(4):
                        take_half(name, (o0 + u) % 4, i * 4 + u, i * 4 + (t0 + u))
                        split(t0 + u + RING, i)
                        if u % 2 == 0:
                            act.wait_ge(scaled, i * 4 + (half0[name] + u + 1))
                            act.activation(sil[u // 2][:, :], fsum[(o0 + u) % 4][:, :], ACT.Silu).then_inc(sil_ready, 1)
                        else:
                            act.wait_ge(hid_ready, i * 2 + (hid0[name] + u // 2 + 1))
                            act.activation(at(hs, i * (4 * S) + (u // 2) * 2 * S, S), fsum[(o0 + u) % 4][:, :],
                                           ACT.Copy).then_inc(hhi_ready, 1)
                        if isinstance(i, int) and i * 4 + u in between:
                            between[i * 4 + u]()

                peeled = max(between, default=-1) // 4 + 1
                for i in range(peeled):
                    four(i)
                with act.Fori(peeled, FF2 // 2) as i:
                    four(i)

            def conv():
                name = "cin"
                t0, o0 = TILE0[name], OUT0[name]
                with act.Fori(0, KD // 4) as i:
                    for u in range(12):
                        take_half(name, (o0 + u) % 4, i * 12 + u, i * 12 + (t0 + u))
                        split(t0 + u + RING, i * 3)
                        if u % 3 == 2:
                            m = u // 3
                            act.wait_ge(hid_ready, i * 4 + (hid0[name] + m + 1))
                            act.activation(at(hs, i * (8 * S) + m * 2 * S, S), conv_y[m % 2], ACT.Copy).then_inc(hhi_ready, 1)

            def mla():
                root("mix_0")
                plain("dq", 3)
                plain("dkv", 2)
                for k in range(KQ + KKV):
                    act.wait_ge(scaled, half0["dq"] + k + 1)
                    gain = VEC["q_norm"] + k if k < KQ else VEC["kv_norm"] + k - KQ
                    split_x(hi_part(os_, k), cqf[:, k * S:(k + 1) * S], vec[:, gain:gain + 1])
                act.activation(ASQ[:, 0:(KQ + KKV) * S], cqf, ACT.Square).then_inc(sq_ready, 1)
                plain("kr", 1, slice(0, ROPE))
                root("cq")
                used("uk", 2)
                tq, tv = TILE0["uq"] + RING, TILE0["uv"] + RING
                def squares(n):
                    src = HEAD_SQ[n][0]
                    if n >= 3:
                        act.wait_ge(head_sum, n - 2)
                    act.activation(mscr[n % 3][:, 0:src.shape[-1]], src, ACT.Square).then_inc(head_sq, 1)

                split(tq)
                act.wait_ge(out_read, OUT0["uk"] + 4)
                for n in range(3):
                    squares(n)
                split(tq + 1)
                act.wait_ge(head_k, 1)
                act.activation(std[:, 2 * H:4 * H], ss[:, 2 * H:4 * H], ACT.Sqrt, bias=eps[:, 0:1], scale=1.0 / QK).then_inc(head_std, 1)
                split(tq + 2)
                act.wait_ge(out_read, OUT0["uq"] + 4)
                for n in (3, 4):
                    squares(n)
                split(tq + 3)
                split(tq + 4)
                act.wait_ge(out_read, OUT0["uq"] + 6)
                for n in (5, 6):
                    squares(n)
                split(tv)
                split(tv + 1)

                def turned(i, u):
                    act.wait_ge(a_turn, i * 4 + (u + 1))
                    act.activation(qkT[u % 2][0:QK, :], bank(turn_bank[u % 2], 0, 512, slice(0, QK)), ACT.Copy).then_inc(a_qkT, 1)

                def exps(i, u):
                    act.wait_ge(a_max, i * 4 + (u + 1))
                    for tb, (a, z) in enumerate([(0, P), (P, 3 * P)]):
                        act.activation(prob[u % 2][:, a:z], bank(score_bank[u % 2], a, z), ACT.Exp, scale=at(rstd, i * 4 + (tb * H + u), 1),
                                       bias=nmx[u][:, tb:tb + 1], accum_out=rsum[u][:, tb:tb + 1]).then_inc(a_exp, 1)

                def probs_turned(i, u):
                    act.wait_ge(a_pT, i * 4 + (u + 1))
                    if not (isinstance(i, int) and 4 * i + u < 2):
                        act.wait_ge(a_pv, i * 4 + (u - 1))
                    act.activation(probT[u % 2], bank(4 + u % 2, 0, 384), ACT.Copy).then_inc(a_pTs, 1)

                turned(0, 0)
                turned(0, 1)
                act.wait_ge(head_sum, 7)
                act.activation(std[:, 0:2 * H], ss[:, 0:2 * H], ACT.Sqrt, bias=eps[:, 0:1], scale=1.0 / QK).then_inc(head_std, 1)
                turned(0, 2)
                exps(0, 0)
                exps(0, 1)
                probs_turned(0, 0)
                heads_loop(act, lambda i, u: ahead(turned, i, u, 3), lambda i, u: ahead(probs_turned, i, u, 1),
                           lambda i, u: ahead(exps, i, u, 2))
                out_hi("o_a")

            def out_hi(name, chunks=range(KD), gain=None):
                for k in chunks:
                    act.wait_ge(o_turn[name], k + 1)
                    act.activation(hi_part(os_, k), bank(5 + k % 3, 0, S), ACT.Copy,
                                   scale=1.0 if gain is None else vec[:, gain + k:gain + k + 1]).then_inc(xhi_ready, 1)

            def mlstm():
                root("mix_1")
                plain("mgate", 2, p=slice(0, MH))
                plain("mqk", 2)
                act.wait_ge(m_gates, 2)
                act.activation(m_ti, m_ti, ACT.Tanh, scale=1.0 / GATE_CAP).then_inc(m_tanh, 1)
                act.activation(m_tf, m_tf, ACT.Tanh, scale=1.0 / GATE_CAP).then_inc(m_tanh, 1)
                act.wait_ge(m_tanh, 2)
                act.activation(m_nb, m_tf, ACT.Exp, scale=-GATE_CAP).then_inc(m_tanh, 1)
                act.wait_ge(m_tanh, 3)
                act.activation(m_tf, m_nb, ACT.Ln, bias=ones[0:MH, 0:1]).then_inc(m_tanh, 1)
                plain("mqk", 8, first=2)

                def floors():
                    act.wait_ge(m_cols, 1)
                    act.activation(m_col[:, TB * MH:], m_col[:, TB * MH:], ACT.Exp).then_inc(m_floor, 1)

                def exps(h):
                    act.wait_ge(m_logw, h + 1)
                    act.activation(m_w[h], m_w[h], ACT.Exp).then_inc(m_exp, 1)

                def squares(h):
                    act.wait_ge(m_hd, h + 1)
                    for tb in range(TB):
                        n = len(squares.done)
                        if n:
                            act.wait_ge(m_sqd, n)
                        act.activation(m_sq, m_h[:, tb * D + h * MV:tb * D + (h + 1) * MV], ACT.Square,
                                       accum_out=m_ss[:, tb * MH + h:tb * MH + h + 1]).then_inc(m_sqd, 1)
                        squares.done.append((h, tb))

                squares.done = []

                def gates(g):
                    for tb in range(TB):
                        o = OUT0["mo"] + 2 * g + tb
                        act.wait_ge(tile_done, TILE0["mo"] + 4 * g + 4)
                        act.wait_ge(out_read, o)
                        act.activation(m_o[:, tb * D + g * 512:tb * D + (g + 1) * 512], bank(o % 4), ACT.Sigmoid,
                                       scale=rstd[:, tb:tb + 1]).then_inc(out_read, 1)

                def roots():
                    act.wait_ge(m_sqd, TB * MH)
                    act.activation(m_sr, m_ss, ACT.Sqrt, bias=eps[:, 0:1], scale=1.0 / MV).then_inc(m_stdd, 1)

                between = {("mv", 2): [floors, lambda: exps(0)], ("mv", 3): [lambda: exps(1)], ("mv", 4): [lambda: exps(2)],
                           ("mv", 5): [lambda: exps(3)], ("mo", 1): [lambda: squares(0)],
                           ("mo", 2): [lambda: squares(1), lambda: squares(2)], ("mo", 3): [lambda: squares(3), roots],
                           ("mo", 4): [lambda: gates(0)], ("mo", 5): [lambda: out_hi("o_m", range(3), VEC["head_norm"])],
                           ("mo", 6): [lambda: out_hi("o_m", [3], VEC["head_norm"])]}
                for name in ("mv", "mo"):
                    for j in range(8):
                        if (name, j) == ("mo", 7):
                            gates(1)
                        split(TILE0[name] + j + RING)
                        for step in between.get((name, j), []):
                            step()
                out_hi("o_m", range(4, KD), VEC["head_norm"])

            def nsa_kv():
                root("kvn")
                used("kv", 8)
                for k in range(KD):
                    split_x(hi_part(os_, k), x[:, k * S:(k + 1) * S], vec[:, VEC["pre_1"] + k:VEC["pre_1"] + k + 1])
                act.wait_ge(out_read, OUT0["kv"] + 4)
                for tb in range(TB):
                    act.activation(c_sq[tb], kn_tok[:, tb * 512:(tb + 1) * 512], ACT.Square).then_inc(c_sqd, 1)
                plain("kvc", 8)
                for j, w in enumerate((w1c_k, w1c_v)):
                    act.dma_start(w1c[j].rearrange("p (c n) -> p c n", n=P), w.rearrange("(c p) n -> p c n", p=P)).then_inc(c_loaded, 16)
                act.dma_start(w2c[0], w2c_k).then_inc(c_loaded, 16)
                act.dma_start(w2c[1], w2c_v).then_inc(c_loaded, 16)

            def key_roots():
                act.wait_ge(c_sum, 2)
                act.activation(std[:, 8:8 + 16], c_ss, ACT.Sqrt, bias=eps[:, 0:1], scale=1.0 / DH).then_inc(c_std, 1)

            def compressed_hidden():
                act.wait_ge(c_bias, 1)
                for j in range(2):
                    act.activation(c_hid[j], bank(4, j * P, j * P + G * NC), ACT.Gelu_apprx_tanh, bias=c_pe[:, j:j + 1]).then_inc(c_gelu, 1)

            def compressed_squares():
                act.wait_ge(c_kc, 1)
                act.activation(c_kcsq, bank(6, 0, G * NC), ACT.Square).then_inc(c_kcsqd, 1)

            def compressed_roots():
                act.wait_ge(c_kcss, 1)
                act.activation(c_kcstd, bank(5, 64, 64 + G * NC), ACT.Sqrt, bias=eps[:, 0:1], scale=1.0 / DH).then_inc(c_kcstdd, 1)

            def nsa():
                t0 = TILE0["nq"]
                root("mid_1")
                plain("ngate", 1, slice(0, 3 * H))
                split(t0 + RING)
                act.wait_ge(n_zero, 1)
                act.wait_ge(n_gturn, 1)
                for tb in range(TB):
                    ins = act.activation(n_gate[:, tb * 3 * H:(tb + 1) * 3 * H], bank(7, tb * 3 * H, (tb + 1) * 3 * H), ACT.Sigmoid,
                                         scale=rstd[:, tb:tb + 1])
                ins.then_inc(scaled, 1)
                for t in range(t0 + 1, t0 + 4):
                    split(t + RING)

                def squares(g):
                    act.wait_ge(out_read, OUT0["nq"] + 2 * g + 2)
                    if g:
                        act.wait_ge(n_sum, 2)
                    for tb in range(TB):
                        act.activation(n_sq[:, tb * 512:(tb + 1) * 512], nq_tok[:, tb * D + g * 512:tb * D + (g + 1) * 512],
                                       ACT.Square).then_inc(n_sqd, 1)

                def roots(g):
                    act.wait_ge(n_sum, 2 * g + 2)
                    act.activation(std[:, 32 + 16 * g:32 + 16 * g + 16], n_ss[:, 16 * g:16 * g + 16], ACT.Sqrt, bias=eps[:, 0:1],
                                   scale=1.0 / DH).then_inc(n_std_, 1)

                def queries_turned(g):
                    act.wait_ge(n_turn, g + 1)
                    for b in range(2):
                        act.activation(n_qTa[:, (2 * g + b) * 512:(2 * g + b + 1) * 512], bank(4 + b), ACT.Copy).then_inc(n_qTd, 1)

                def compressed_exps(g):
                    act.wait_ge(n_clog, g + 1)
                    for tb, c in enumerate((NC0, NC)):
                        cl = n_cl[tb].rearrange("p (h c) -> p h c", h=H)[:, 8 * g:8 * g + 8, 0:c]
                        act.activation(cl, cl, ACT.Exp).then_inc(n_cexp, 1)

                def compressed_turned(g):
                    act.wait_ge(n_cT, g + 1)
                    for tb in range(TB):
                        act.activation(n_cpT[:, tb * S:(tb + 1) * S], bank(4 + tb, 0, S, slice(0, G * NC)), ACT.Copy).then_inc(n_cTs, 1)

                def queries(i, j):
                    if isinstance(i, int) and i == 0:
                        act.wait_ge(n_qTd, 2)
                        act.wait_ge(n_zero, 1)
                    else:
                        act.wait_ge(n_s, i * 4 + (2 * j - 2))
                    for e in range(2):
                        rows = slice(e * DH, (e + 1) * DH)
                        cols = slice(j * S, (j + 1) * S) if isinstance(i, int) and i == 0 else bass.ds(i * (2 * S) + j * S, S)
                        act.activation(n_qT[j][e][rows, :], n_qTa[rows, cols], ACT.Copy).then_inc(n_q, 1)

                def exps(i, w):
                    act.wait_ge(n_max, i * 4 + (w + 1))
                    for br in range(2):
                        for tb, (a, z) in enumerate([(0, P), (P, 3 * P)]):
                            m = 2 * tb + br
                            act.activation(n_p[w % 2][:, br * 384 + a:br * 384 + z], n_l[w % 2][:, br * 384 + a:br * 384 + z], ACT.Exp,
                                           bias=n_nmx[w][:, m:m + 1], accum_out=n_rs[w][:, m:m + 1]).then_inc(n_exp, 1)

                def probs_turned(i, w):
                    for br in range(2):
                        act.wait_ge(n_pT, i * 8 + (2 * w + br + 1))
                        if not (isinstance(i, int) and 4 * i + w < 2):
                            act.wait_ge(n_pv, i * 4 + (w - 1))
                        act.activation(n_pTs[w % 2][:, br * 384:(br + 1) * 384], bank(4 + br, 0, 384), ACT.Copy).then_inc(n_pTd, 1)

                squares(0)
                split(t0 + 4 + RING)
                roots(0)
                queries_turned(0)
                split(t0 + 5 + RING)
                queries(0, 0)
                queries(0, 1)
                compressed_exps(0)
                split(t0 + 6 + RING)
                compressed_turned(0)
                split(t0 + 7 + RING)
                squares(1)
                queries_turned(1)
                roots(1)
                exps(0, 0)
                compressed_exps(1)
                compressed_turned(1)
                exps(0, 1)

                def four(i):
                    last = isinstance(i, int) and i == HG - 1
                    for w in range(4):
                        if w % 2 == 0 and not last:
                            queries(i + 1, w // 2)
                        probs_turned(i, w)
                        if not (last and w >= 2):
                            exps(i if w < 2 else i + 1, (w + 2) % 4)

                four(0)
                with act.Fori(1, HG - 1) as i:
                    four(i)
                four(HG - 1)
                out_hi("o_n")

            split(0)
            act.wait_ge(x_loaded, 16 * 2)
            act.wait_ge(const_ready, 3)
            for k in range(KD):
                split_x(hi_part(xs, k), x[:, k * S:(k + 1) * S], vec[:, VEC["mix_0"] + k:VEC["mix_0"] + k + 1])
                if k == KD // 2:
                    split(1)
            split(2)
            for k in range(KD):
                if k == KD // 2:
                    split(3)
                act.activation(ASQ[:, k * S:(k + 1) * S], x[:, k * S:(k + 1) * S], ACT.Square).then_inc(sq_ready, 1)
            mla()
            act.wait_ge(bias_done, 1)
            act.dma_start(bias_dram, bias_row[:, :].unsqueeze(1).broadcast_to((H, COPIES, 2 * S))).then_inc(bias_out, 16)
            residual("wo_a", 1)
            root("ffn_0")
            up("up_0")
            residual("down_0", 4)
            mlstm()
            residual("wo_m", 1)
            root("ffn_1")
            up("up_1")
            residual("down_1", 4)
            root("pre_0")
            glu("glu_0")
            residual("out_0", FF2_TILES)
            root("mid_0")
            conv()
            residual("cout", 1)
            root("post_0")
            glu("glu_1")
            residual("out_1", FF2_TILES)
            nsa_kv()
            glu("glu_2", {0: key_roots, 9: compressed_hidden, 11: compressed_squares, 13: compressed_roots})
            residual("out_2", FF2_TILES)
            act.wait_ge(bias_out, 16)
            act.wait_ge(tile_done, TILE0["out_2"])
            for g in range(P // COPIES):
                act.dma_start(bias[g * COPIES:(g + 1) * COPIES, :].rearrange("p (h s) -> p h s", h=H),
                              bass.AP(tensor=bias_dram.tensor, offset=P - 1 - g * COPIES,
                                      ap=[[2 * S - 1, COPIES], [COPIES * 2 * S, H], [1, S]])).then_inc(bias_in, 16)
            nsa()
            residual("wo_n", 1)
            root("post_1")
            glu("glu_3")
            residual("out_3", FF2_TILES)

        @block.vector
        def _(dve):
            steps = Steps()

            def then(ins):
                dve.wait_ge(dve_step, steps.mark(ins))

            def hi_of(ap):
                return ap.bitcast(F32)

            def clear_sums(name):
                dve.memset(ssq[:, :], 0.0).then_inc(ssq_ready, 1)

            def norm(name):
                dve.wait_ge(std_ready, STD0[name])
                if name in TO_ROWS:
                    then(dve.reciprocal(rb[:, :], stdb[:, :]))
                if name in TO_COLUMNS:
                    col, n = (4, 2 * TB) if name == "cq" else (0, TB)
                    then(dve.reciprocal(rstd[:, col:col + n], std[:, col:col + n]))
                if name in SUMS and name != SUMS[-1]:
                    clear_sums(SUMS[SUMS.index(name) + 1])

            def rest_x(dst, src, gain, hi, count):
                dve.wait_ge(xhi_ready, count)
                dve.scalar_tensor_tensor(out=dst, in0=src, scalar=gain, in1=hi_of(hi), op0=ALU.mult, op1=ALU.subtract).then_inc(xs_ready, 1)

            def rest_all(name, dst):
                for k in range(KD):
                    g = VEC[name] + k
                    rest_x(lo_part(dst, k), x[:, k * S:(k + 1) * S], vec[:, g:g + 1], hi_part(dst, k), XS0[name] + k + 1)

            def add_halves(name, b, u, dst, i=0, per=0, a=0, z=S, p=slice(None)):
                dve.wait_ge(half_ready, i * per + (half0[name] + u + 1))
                return dve.tensor_tensor(dst, bank(b, a, z, p), half[b][p, a:z], ALU.add).then_inc(out_read, 1)

            def output(name, u, dst=None, i=0, per=0, p=slice(None)):
                b = (OUT0[name] + u) % 4
                f = fsum[b][p, :]
                add_halves(name, b, u, f, i, per, p=p)
                dve.wait_ge(out_read, i * per + (OUT0[name] + u + 1))
                dve.tensor_tensor(f if dst is None else dst, f, rb[p, :], ALU.mult).then_inc(scaled, 1)
                return f

            def plain(name, outs, dst):
                for o in range(outs):
                    output(name, o, dst(o))

            def token_major(name, outs, dst, tiles_, col=0):
                for o in range(outs):
                    d = dst(o)
                    dve.wait_ge(tile_done, TILE0[name] + tiles_(o))
                    dve.tensor_scalar(d, bank((OUT0[name] + o) % 4, 0, d.shape[-1]), rstd[:, col + o % 2:col + o % 2 + 1], None, ALU.mult)\
                       .then_inc(out_read, 1)

            def residual(name, per, scale=1.0):
                t0, o0, no = TILE0[name], OUT0[name], RES.index(name)
                with dve.Fori(0, KD // 4) as i:
                    for u in range(4):
                        b = (o0 + u) % 4
                        xo = at(x, i * (4 * S) + u * S, S)
                        dve.wait_ge(tile_done, i * (4 * per) + (t0 + (u + 1) * per))
                        dve.scalar_tensor_tensor(out=xo, in0=bank(b, 0, S), scalar=scale, in1=xo, op0=ALU.mult, op1=ALU.add)\
                           .then_inc(x_half, 1)
                        dve.wait_ge(x_half, i * 4 + (KD * no + u + 1))
                        dve.scalar_tensor_tensor(out=xo, in0=bank(b, S, 2 * S), scalar=scale, in1=xo, op0=ALU.mult, op1=ALU.add)\
                           .then_inc(out_read, 1)
                        if name in NEXT:
                            chunk = i * (8 * S) + u * 2 * S
                            norm_ = NEXT[name]
                            rest_x(at(xs, chunk + S, S), xo, at(vec, i * 4 + (VEC[norm_] + u), 1), at(xs, chunk, S),
                                   i * 4 + (XS0[norm_] + u + 1))
                            dve.wait_ge(sq_ready, i * 4 + (SQ0[name] + u + 1))
                            dve.wait_ge(ssq_ready, i * 4 + (SSQ0[norm_] + u + 1))
                            dve.tensor_tensor(ssq[:, :], ssq[:, :], sq[u][:, :], ALU.add).then_inc(ssq_ready, 1)

            def h_lo(name, src, chunk, count):
                dve.wait_ge(hhi_ready, count)
                dve.tensor_tensor(at(hs, chunk + S, S), src, hi_of(at(hs, chunk, S)), ALU.subtract).then_inc(hs_ready, 1)

            def up(name):
                h0 = hid0[name]
                with dve.Fori(0, FF1 // 4) as i:
                    for u in range(4):
                        f = output(name, u, None, i, 4)
                        dve.wait_ge(scaled, i * 4 + (half0[name] + u + 1))
                        dve.scalar_tensor_tensor(out=f, in0=f, scalar=0.0, in1=f, op0=ALU.max, op1=ALU.mult).then_inc(hid_ready, 1)
                        h_lo(name, f, i * (8 * S) + u * 2 * S, i * 4 + (h0 + u + 1))

            def glu(name, between=None):
                h0 = hid0[name]
                between = between or {}

                def four(i):
                    for u in range(4):
                        f = output(name, u, None, i, 4)
                        if u % 2:
                            dve.wait_ge(sil_ready, i * 2 + (sil0[name] + u // 2 + 1))
                            dve.wait_ge(scaled, i * 4 + (half0[name] + u + 1))
                            dve.tensor_tensor(f, f, sil[u // 2][:, :], ALU.mult).then_inc(hid_ready, 1)
                            h_lo(name, f, i * (4 * S) + (u // 2) * 2 * S, i * 2 + (h0 + u // 2 + 1))
                        if isinstance(i, int) and i * 4 + u in between:
                            between[i * 4 + u]()

                peeled = max(between, default=-1) // 4 + 1
                for i in range(peeled):
                    four(i)
                with dve.Fori(peeled, FF2 // 2) as i:
                    four(i)

            def conv():
                name, h0 = "cin", hid0["cin"]
                for j in range(2):
                    ins = dve.memset(conv_u[j][:, 0:TAPS - 1], 0.0)
                then(ins)
                with dve.Fori(0, KD // 4) as i:
                    steps.base, start, steps.n = i * 16 + steps.n, steps.n, 0
                    for m in range(4):
                        j = m % 2
                        output(name, 3 * m, conv_c[j], i, 12)
                        output(name, 3 * m + 1, conv_v[j], i, 12)
                        dve.wait_ge(scaled, i * 12 + (half0[name] + 3 * m + 2))
                        then(dve.tensor_tensor(conv_u[j][:, TAPS - 1:], conv_c[j], conv_v[j], ALU.mult))
                        for k in range(TAPS):
                            w = at(vec, i * 4 + (VEC["taps"] + k * KD + m), 1)
                            if k == 0:
                                then(dve.tensor_scalar(conv_y[j], conv_u[j][:, 0:S], w, None, ALU.mult))
                            else:
                                then(dve.scalar_tensor_tensor(out=conv_y[j], in0=conv_u[j][:, k:k + S], scalar=w, in1=conv_y[j],
                                                              op0=ALU.mult, op1=ALU.add))
                        output(name, 3 * m + 2, conv_b[j], i, 12)
                        dve.wait_ge(scaled, i * 12 + (half0[name] + 3 * m + 3))
                        dve.tensor_tensor(conv_y[j], conv_y[j], conv_b[j], ALU.mult).then_inc(hid_ready, 1)
                        h_lo(name, conv_y[j], i * (8 * S) + m * 2 * S, i * 4 + (h0 + m + 1))
                    assert steps.n == 16
                    steps.base, steps.n = 0, start + 16 * (KD // 4)

            def out_lo(name, chunks=range(KD), gain=None):
                for k in chunks:
                    dve.wait_ge(xhi_ready, XS0[name] + k + 1)
                    dve.scalar_tensor_tensor(out=lo_part(os_, k), in0=bank(5 + k % 3, 0, S),
                                             scalar=1.0 if gain is None else vec[:, gain + k:gain + k + 1],
                                             in1=hi_of(hi_part(os_, k)), op0=ALU.mult, op1=ALU.subtract).then_inc(xs_ready, 1)

            def mla():
                plain("dq", 3, lambda o: cqf[:, o * S:(o + 1) * S])
                plain("dkv", 2, lambda o: cqf[:, (KQ + o) * S:(KQ + o + 1) * S])
                for k in range(KQ + KKV):
                    g = VEC["q_norm"] + k if k < KQ else VEC["kv_norm"] + k - KQ
                    rest_x(lo_part(os_, k), cqf[:, k * S:(k + 1) * S], vec[:, g:g + 1], hi_part(os_, k), XS0["cq"] + k + 1)
                b = OUT0["kr"] % 4
                add_halves("kr", b, 0, fsum[b][0:ROPE, :], p=slice(0, ROPE))
                norm("cq")
                dve.wait_ge(row_ready, 1)
                dve.tensor_copy(bias_row[:, :], bank(6, 0, 2 * S, slice(0, H))).then_inc(bias_done, 1)
                dve.wait_ge(loaded, 16 * 3)
                at_ = CONST["onehot"]
                for j in range(2):
                    dve.tensor_copy(qkT[j][QK:QK + TB, :], con[QK:QK + TB, at_:at_ + 2 * S]).then_inc(a_mask, 1)
                def head_sums(n):
                    src, d, first = HEAD_SQ[n]
                    w = src.shape[-1]
                    dve.wait_ge(head_sq, n + 1)
                    dve.tensor_reduce(ss[:, first:first + w // d], mscr[n % 3][:, 0:w].rearrange("p (n d) -> p n d", d=d), AX_X, ALU.add)\
                       .then_inc(head_sum, 1)

                def up_kv(name, dst, g):
                    for tb in range(TB):
                        last = {"uk": 1 + g, "uv": 1 + g, "uq": (2, 3, 5)[g]}[name]
                        dve.wait_ge(tile_done, TILE0[name] + last)
                        n = dst.shape[-1] // TB
                        col = (4 if name == "uq" else 6) + tb
                        dve.tensor_scalar(dst[:, tb * n + g * 512:tb * n + (g + 1) * 512], bank((OUT0[name] + 2 * g + tb) % 4),
                                          rstd[:, col:col + 1], None, ALU.mult).then_inc(out_read, 1)

                dve.wait_ge(a_rope, 1)
                for tb in range(TB):
                    ins = dve.tensor_scalar(kr_tok[:, tb * ROPE:(tb + 1) * ROPE], bank(7, tb * ROPE, (tb + 1) * ROPE), rstd[:, tb:tb + 1],
                                            None, ALU.mult)
                ins.then_inc(scaled, 1)
                up_kv("uk", k_tok, 0)
                up_kv("uk", k_tok, 1)
                then(dve.tensor_tensor(gq[:, 0:NOPE], gq[:, 0:NOPE], gk[:, 0:NOPE], ALU.mult))
                up_kv("uq", q_tok, 0)
                for n in range(3):
                    head_sums(n)
                dve.wait_ge(head_sum, 3)
                ssk = ss[:, 2 * H:4 * H].rearrange("p (t h) -> p t h", t=TB)
                ssr = ss[:, 4 * H:4 * H + TB].unsqueeze(2).to_broadcast([P, TB, H])
                dve.tensor_tensor(ssk, ssk, ssr, ALU.add).then_inc(head_k, 1)
                then(dve.tensor_tensor(kr3, kr3, gk[:, NOPE:].unsqueeze(1).unsqueeze(1).to_broadcast([P, TB, 1, ROPE]), ALU.mult))
                rotate(dve, then, kr3, 1)
                up_kv("uq", q_tok, 1)
                dve.wait_ge(head_std, 1)
                dve.reciprocal(rstd[:, 2 * H:4 * H], std[:, 2 * H:4 * H]).then_inc(a_keys, 1)
                up_kv("uq", q_tok, 2)
                head_sums(3)
                head_sums(4)
                up_kv("uv", v_tok, 0)
                up_kv("uv", v_tok, 1)
                head_sums(5)
                head_sums(6)
                dve.wait_ge(head_std, 2)
                dve.wait_ge(out_read, OUT0["uv"] + 4)
                then(dve.reciprocal(rstd[:, 0:2 * H], std[:, 0:2 * H]))
                then(dve.tensor_scalar(rstd[:, 0:2 * H], rstd[:, 0:2 * H], QK ** -0.5, None, ALU.mult))

                def maxima(i, u):
                    b = score_bank[u % 2]
                    dve.wait_ge(a_s, i * 4 + (u + 1))
                    dve.tensor_reduce(mx[u][:, 0:1], bank(b, 0, P), AX_X, ALU.max)
                    then(dve.tensor_reduce(mx[u][:, 1:2], bank(b, P, 3 * P), AX_X, ALU.max))
                    h = i * 4 + u
                    r = rstd[:, 0:2 * H].rearrange("p (t h) -> p t h", t=TB)
                    r = r[:, :, h:h + 1] if isinstance(i, int) else r[:, :, bass.ds(h, 1)]
                    dve.scalar_tensor_tensor(out=nmx[u].unsqueeze(2), in0=mx[u].unsqueeze(2), scalar=-1.0, in1=r, op0=ALU.mult, op1=ALU.mult)\
                       .then_inc(a_max, 1)

                def outputs(i, u):
                    dve.wait_ge(a_exp, i * 8 + 2 * (u + 1))
                    then(dve.reciprocal(rinv[u], rsum[u]))
                    dve.wait_ge(a_pv, i * 4 + (u + 1))
                    for tb in range(TB):
                        col = tb * P + u % 2 * VD
                        ins = dve.tensor_scalar(at(o_tok, i * (4 * VD) + (tb * H * VD + u * VD), VD), bank(6 + u % 2, col, col + VD),
                                                rinv[u][:, tb:tb + 1], None, ALU.mult)
                    ins.then_inc(a_o, 1)

                maxima(0, 0)
                maxima(0, 1)
                per = 8

                def begin(i, u):
                    if u == 0 and not isinstance(i, int):
                        steps.base, begin.n, steps.n = i * per + (steps.n - per), steps.n, 0

                def end(i, u):
                    if u == 3 and not isinstance(i, int):
                        assert steps.n == per
                        steps.base, steps.n = 0, begin.n + per * (H // 4 - 2)

                heads_loop(dve, begin, lambda i, u: ahead(maxima, i, u, 2), outputs, end)
                out_lo("o_a")

            def mlstm():
                for o, (dst, b) in enumerate(((m_ti, "b_i"), (m_tf, "b_f"))):
                    output("mgate", o, dst, p=slice(0, MH))
                    dve.wait_ge(scaled, half0["mgate"] + o + 1)
                    dve.tensor_scalar(dst, dst, vec[0:MH, VEC[b]:VEC[b] + 1], None, ALU.add).then_inc(m_gates, 1)
                dve.memset(m_v.rearrange("p (n c) -> p n c", c=MV + 1)[:, :, MV:], 1.0).then_inc(m_one_, 1)
                plain("mqk", 8, lambda o: m_qk[:, o * S:(o + 1) * S])
                then(dve.memset(m_one, 1.0))
                dve.wait_ge(m_tanh, 4)
                then(dve.tensor_tensor_scan(m_nb, m_one, m_tf, 0.0, ALU.mult, ALU.add))
                then(dve.scalar_tensor_tensor(out=m_a, in0=m_ti, scalar=GATE_CAP, in1=m_nb, op0=ALU.mult, op1=ALU.add))
                then(dve.tensor_tensor_scan(m_g, m_a, m_a, 0.0, ALU.max, ALU.max))
                dve.tensor_scalar(m_ng, m_g, -1.0, None, ALU.mult)
                dve.tensor_tensor(m_nm, m_nb, m_g, ALU.subtract).then_inc(m_rows, 1)
                causal = const("causal", 0, P)

                def columns():
                    dve.wait_ge(m_at, 1)
                    dve.tensor_copy(m_col, bank(7, 0, 2 * TB * MH)).then_inc(m_cols, 1)
                    dve.wait_ge(m_cols, 1)

                def exponents(h):
                    b = 4 + h % 2
                    dve.wait_ge(m_bcd, h + 1)
                    dve.tensor_scalar(m_w[h][:, 0:S], bank(b, 0, S), m_col[:, h:h + 1], 0.0, ALU.add, ALU.min)
                    dve.tensor_scalar(m_w[h][:, S:S + P], bank(b, P, S), m_col[:, MH + h:MH + h + 1], 0.0, ALU.add, ALU.min)\
                       .then_inc(m_logw, 1)

                def weights(h):
                    w = m_w[h]
                    dve.wait_ge(m_exp, h + 1)
                    dve.tensor_tensor(w[:, 0:P], w[:, 0:P], causal, ALU.mult)
                    then(dve.tensor_tensor(w[:, S:S + P], w[:, S:S + P], causal, ALU.mult))
                    dve.wait_ge(m_st, h + 1)
                    dve.scalar_tensor_tensor(out=w, in0=bank(6 + h % 2, 0, 384), scalar=MQK ** -0.5, in1=w, op0=ALU.mult, op1=ALU.mult)\
                       .then_inc(m_ptd, 1)

                def values(g):
                    v4 = m_v.rearrange("p (t h c) -> p t h c", t=TB, h=MH)
                    for tb in range(TB):
                        dve.wait_ge(tile_done, TILE0["mv"] + 4 * g + 4)
                        dve.tensor_scalar(v4[:, tb, 2 * g:2 * g + 2, 0:MV], bank((OUT0["mv"] + 2 * g + tb) % 4).rearrange("p (h c) -> p h c", h=2),
                                          rstd[:, tb:tb + 1], None, ALU.mult).then_inc(out_read, 1)

                def head(h):
                    b = 4 + 2 * (h % 2)
                    den = psum[:, b * BANK + MV:(b + 1) * BANK + MV + 1:BANK]
                    floor = m_col[:, TB * MH + h::MH]
                    dve.wait_ge(m_num, h + 1)
                    then(dve.tensor_scalar(m_nd[h], den, -1.0, None, ALU.mult))
                    then(dve.tensor_tensor(m_dn[h], den, m_nd[h], ALU.max))
                    if h == 0:
                        dve.wait_ge(m_floor, 1)
                    then(dve.tensor_tensor(m_dn[h], m_dn[h], floor, ALU.max))
                    then(dve.reciprocal(m_dn[h], m_dn[h]))
                    for tb in range(TB):
                        ins = dve.tensor_scalar(m_h[:, tb * D + h * MV:tb * D + (h + 1) * MV], bank(b + tb, 0, MV), m_dn[h][:, tb:tb + 1],
                                                None, ALU.mult)
                    ins.then_inc(m_hd, 1)

                def gate(g):
                    for tb in range(TB):
                        dve.wait_ge(out_read, OUT0["mo"] + 2 * g + tb + 1)
                        for h in (2 * g, 2 * g + 1):
                            out = m_h[:, tb * D + h * MV:tb * D + (h + 1) * MV]
                            ins = dve.scalar_tensor_tensor(out=out, in0=out, scalar=m_r[:, tb * MH + h:tb * MH + h + 1],
                                                           in1=m_o[:, tb * D + h * MV:tb * D + (h + 1) * MV], op0=ALU.mult, op1=ALU.mult)
                    ins.then_inc(m_gated, 1)

                columns()
                exponents(0)
                exponents(1)
                weights(0)
                exponents(2)
                weights(1)
                values(0)
                exponents(3)
                weights(2)
                weights(3)
                values(1)
                for h in range(MH):
                    head(h)
                dve.wait_ge(m_stdd, 1)
                then(dve.reciprocal(m_r, m_sr))
                gate(0)
                out_lo("o_m", range(4), VEC["head_norm"])
                gate(1)
                out_lo("o_m", range(4, KD), VEC["head_norm"])

            def nsa_kv():
                token_major("kv", 4, lambda o: (kn_tok if o < 2 else vtok)[:, (o % 2) * 512:(o % 2 + 1) * 512],
                            lambda o: 4 * (1 + o // 2))
                rest_all("pre_1", os_)
                for tb in range(TB):
                    dve.wait_ge(c_sqd, tb + 1)
                    dve.tensor_reduce(c_ss[:, tb * 8:(tb + 1) * 8], c_sq[tb].rearrange("p (n d) -> p n d", d=DH), AX_X, ALU.add)\
                       .then_inc(c_sum, 1)
                for j, pe_at in enumerate((VEC["pe_k"], VEC["pe_v"])):
                    then(dve.memset(c_dup[j][:, G * S:], 0.0))
                    dve.tensor_copy(c_dup[j][:, G * S:G * S + CBLOCK:2], vec[:, pe_at:pe_at + CBLOCK // 2])
                for o in range(8):
                    b = (OUT0["kvc"] + o) % 4
                    dst = c_dup[o // G][:, (o % G) * S:(o % G + 1) * S]
                    add_halves("kvc", b, o, fsum[b][:, :])
                    dve.wait_ge(out_read, OUT0["kvc"] + o + 1)
                    dve.tensor_tensor(dst[0:DH, :], fsum[b][0:DH, :], rb[0:DH, :], ALU.mult)
                    dve.tensor_tensor(dst[DH:P, 0:S - 1], fsum[b][DH:P, 1:S], rb[DH:P, 1:S], ALU.mult).then_inc(scaled, 1)

            def keys():
                dve.wait_ge(c_std, 1)
                then(dve.reciprocal(c_r, std[:, 8:8 + 16]))
                kn3 = kn_tok.rearrange("p (n d) -> p n d", d=DH)
                then(dve.tensor_tensor(kn3, kn3, c_r.unsqueeze(2).to_broadcast([P, 16, DH]), ALU.mult))
                gains = row[:, ROW["ks"]:ROW["ks"] + 2 * DH].rearrange("p (b d) -> p b d", b=2)
                then(dve.tensor_tensor(gains, gains, row[:, ROW["nq"]:ROW["nq"] + DH].unsqueeze(1).to_broadcast([P, 2, DH]), ALU.mult))
                gain = row[:, ROW["ks"]:ROW["ks"] + 2 * DH].rearrange("p (b d) -> p b d", b=2).unsqueeze(2).to_broadcast([P, 2, G, DH])
                for tb in range(TB):
                    k4 = kn_tok[:, tb * 512:(tb + 1) * 512].rearrange("p (b g d) -> p b g d", b=2, g=G)
                    ins = dve.tensor_tensor(k4, k4, gain, ALU.mult)
                ins.then_inc(c_kn, 1)

            def keys_turned():
                dve.wait_ge(c_kt, 1)
                for b in range(2):
                    dve.tensor_copy(kT[:, b * 512:(b + 1) * 512], bank(6 + b)).then_inc(c_kT, 1)

            def compression_bias():
                dve.wait_ge(c_hd, 1)
                for j in range(2):
                    ins = dve.tensor_copy(c_pe[:, j:j + 1], bank(4, j * P + G * NC, j * P + G * NC + 1))
                ins.then_inc(c_bias, 1)

            def compressed():
                dve.wait_ge(c_kcstdd, 1)
                then(dve.reciprocal(c_kcr, c_kcstd))
                g = VEC["kc_norm"]
                then(dve.tensor_tensor(vec[:, g:g + 1], vec[:, g:g + 1], vec[:, VEC["nq_norm"]:VEC["nq_norm"] + 1], ALU.mult))
                then(dve.memset(kcT[:, :], 0.0))
                for e in range(2):
                    rows = slice(e * DH, (e + 1) * DH)
                    out, keys_, rms = (t[rows, :].rearrange("p (g e c) -> p g e c", g=2, e=2)[:, :, e, :]
                                       for t in (kcT, bank(6, 0, G * NC), c_kcr))
                    ins = dve.scalar_tensor_tensor(out=out, in0=keys_, scalar=vec[rows, g:g + 1], in1=rms, op0=ALU.mult, op1=ALU.mult)
                ins.then_inc(c_end, 1)
                dve.wait_ge(c_vcd, 1)
                n = G * NC
                dve.tensor_tensor(vc[:, :].rearrange("p (g d) -> p g d", g=G),
                                  bank(7, 0, DH, slice(0, n)).unsqueeze(1).to_broadcast([n, G, DH]),
                                  const("groups", 0, G, slice(0, n)).unsqueeze(2).to_broadcast([n, G, DH]), ALU.mult).then_inc(c_end, 1)

            def nsa():
                n_r3 = n_r.rearrange("p (t h) -> p t h", t=TB)
                gate4 = n_gate.rearrange("p (t h b) -> p t h b", t=TB, b=3)
                b4 = bias[:, :].rearrange("p (h a b) -> p h a b", h=H, b=CSTRIDE)
                cl3 = [n_cl[tb].rearrange("p (h c) -> p h c", h=H) for tb in range(TB)]
                cmx3, crs3, csc3 = (t.rearrange("p (t h) -> p t h", t=TB) for t in (n_cmx, n_crs, n_csc))
                no4 = no_tok.rearrange("p (t h d) -> p t h d", t=TB, h=H)

                def evacuate(g):
                    for tb in range(TB):
                        dve.wait_ge(tile_done, TILE0["nq"] + 4 * g + 4)
                        dve.tensor_scalar(nq_tok[:, tb * D + g * 512:tb * D + (g + 1) * 512], bank((OUT0["nq"] + 2 * g + tb) % 4),
                                          rstd[:, tb:tb + 1], None, ALU.mult).then_inc(out_read, 1)

                def query_sums(g):
                    for tb in range(TB):
                        dve.wait_ge(n_sqd, 2 * g + tb + 1)
                        dve.tensor_reduce(n_ss[:, 16 * g + 8 * tb:16 * g + 8 * tb + 8],
                                          n_sq[:, tb * 512:(tb + 1) * 512].rearrange("p (n d) -> p n d", d=DH), AX_X, ALU.add).then_inc(n_sum, 1)

                def query_scales(g):
                    r = n_r3[:, :, 8 * g:8 * g + 8]
                    dve.wait_ge(n_std_, g + 1)
                    then(dve.reciprocal(r, std[:, 32 + 16 * g:32 + 16 * g + 16].rearrange("p (t h) -> p t h", t=TB)))
                    then(dve.tensor_scalar(r, r, DH ** -0.5, None, ALU.mult))

                def compressed_logits(g):
                    dve.wait_ge(n_cs, g + 1)
                    mine = slice(8 * g, 8 * g + 8)
                    for tb, c in enumerate((NC0, NC)):
                        raw_ = bank(6, tb * P, (tb + 1) * P).rearrange("p (j x) -> p j x", j=4)[:, :, 0:2 * NC]
                        ins = dve.tensor_tensor(cl3[tb][:, mine, 0:c].rearrange("p (j e) c -> p j e c", e=2),
                                                raw_.rearrange("p j (e c) -> p j e c", e=2)[:, :, :, 0:c],
                                                n_r3[:, tb, mine].rearrange("p (j e) -> p j e", e=2).unsqueeze(3).to_broadcast([P, 4, 2, c]), ALU.mult)
                    then(ins)
                    views = [(cl3[tb][:, 8 * g:8 * g + 8, 0:c], c, first) for tb, (c, first) in enumerate(((NC0, 9), (NC, 1)))]
                    for cl, c, first in views:
                        ins = dve.tensor_tensor(cl, cl, b4[:, 8 * g:8 * g + 8, first:first + c, CSTRIDE - 1], ALU.add)
                    then(ins)
                    for tb, (cl, c, _) in enumerate(views):
                        ins = dve.tensor_reduce(cmx3[:, tb, 8 * g:8 * g + 8], cl, AX_X, ALU.max)
                    then(ins)
                    for tb, (cl, c, _) in enumerate(views):
                        ins = dve.tensor_tensor(cl, cl, cmx3[:, tb, 8 * g:8 * g + 8].unsqueeze(2).to_broadcast([P, 8, c]), ALU.subtract)
                    ins.then_inc(n_clog, 1)

                def compressed_scales(g):
                    dve.wait_ge(n_cexp, 2 * g + 2)
                    mine = slice(8 * g, 8 * g + 8)
                    for tb, c in enumerate((NC0, NC)):
                        ins = dve.tensor_reduce(crs3[:, tb, mine], cl3[tb][:, mine, 0:c], AX_X, ALU.add)
                    then(ins)
                    then(dve.reciprocal(crs3[:, :, mine], crs3[:, :, mine]))
                    then(dve.tensor_tensor(csc3[:, :, mine], crs3[:, :, mine], gate4[:, :, mine, 0], ALU.mult))
                    valid = const("valid", 0, TB).unsqueeze(2).to_broadcast([P, TB, 8])
                    then(dve.tensor_tensor(csc3[:, :, mine], csc3[:, :, mine], valid, ALU.mult))

                def compressed_outputs(g):
                    dve.wait_ge(n_cpv, g + 1)
                    for tb in range(TB):
                        ins = dve.tensor_tensor(no4[:, tb, 8 * g:8 * g + 8], bank(6 + tb).rearrange("p (h d) -> p h d", d=DH),
                                                csc3[:, tb, 8 * g:8 * g + 8].unsqueeze(2).to_broadcast([P, 8, DH]), ALU.mult)
                    ins.then_inc(n_co, 1)

                def logits(i, w):
                    e, log = w % 2, n_l[w % 2].rearrange("p (b c) -> p b c", b=2)
                    dve.wait_ge(n_s, i * 4 + (w + 1))
                    if not (isinstance(i, int) and 4 * i + w < 2):
                        dve.wait_ge(n_exp, i * 16 + 4 * (w - 1))
                    scores = psum[:, 2 * e * BANK:(2 * e + 2) * BANK].rearrange("p (b c) -> p b c", b=2)
                    for tb, (a, z) in enumerate([(0, P), (P, 3 * P)]):
                        table = at(bias, i * (4 * S) + (w * S + (P if tb == 0 else 0)), z - a)
                        ins = dve.scalar_tensor_tensor(out=log[:, :, a:z], in0=scores[:, :, a:z], scalar=at(n_r, i * 4 + (tb * H + w), 1),
                                                       in1=table.unsqueeze(1).to_broadcast([P, 2, z - a]), op0=ALU.mult, op1=ALU.add)
                    ins.then_inc(n_log, 1)

                def maxima(i, w):
                    log = n_l[w % 2].rearrange("p (b c) -> p b c", b=2)
                    dve.wait_ge(n_log, i * 4 + (w + 1))
                    dve.tensor_reduce(n_mx[w][:, 0:2], log[:, :, 0:P], AX_X, ALU.max)
                    then(dve.tensor_reduce(n_mx[w][:, 2:4], log[:, :, P:3 * P], AX_X, ALU.max))
                    dve.tensor_scalar(n_nmx[w], n_mx[w], -1.0, None, ALU.mult).then_inc(n_max, 1)

                def scales(i, w):
                    dve.wait_ge(n_exp, i * 16 + 4 * (w + 1))
                    then(dve.reciprocal(n_sc[w], n_rs[w]))
                    h = i * 4 + w
                    g = gate4[:, :, h:h + 1, 1:3] if isinstance(i, int) else gate4[:, :, bass.ds(h, 1), 1:3]
                    sc = n_sc[w].rearrange("p (t o b) -> p t o b", t=TB, o=1)
                    dve.tensor_tensor(sc, sc, g, ALU.mult).then_inc(n_gs, 1)

                def outputs(i, w):
                    dve.wait_ge(n_pv, i * 4 + (w + 1))
                    first, b = i * (4 * DH) + w * DH, 6 + w % 2
                    o = no_tok.rearrange("p (t c) -> p t c", t=TB)
                    o = o[:, :, first:first + DH] if isinstance(i, int) else o[:, :, bass.ds(first, DH)]
                    pv = bank(b, 0, TB * P).rearrange("p (t c) -> p t c", t=TB)[:, :, w % 2 * DH:(w % 2 + 1) * DH]
                    dve.tensor_tensor(o, pv, o, ALU.add).then_inc(n_od, 1)

                b = OUT0["ngate"] % 4
                add_halves("ngate", b, 0, fsum[b][0:3 * H, :], p=slice(0, 3 * H))
                for j in range(2):
                    for e in range(2):
                        ins = dve.memset(n_qT[j][e][DH - e * DH:P - e * DH, :], 0.0)
                ins.then_inc(n_zero, 1)
                dve.memset(n_cl[0], 0.0)
                evacuate(0)
                query_sums(0)
                query_scales(0)
                dve.wait_ge(scaled, half0["ngate"] + 1)
                dve.wait_ge(bias_in, 16 * (P // COPIES))
                compressed_logits(0)
                compressed_scales(0)
                evacuate(1)
                query_sums(1)
                compressed_outputs(0)
                logits(0, 0)
                maxima(0, 0)
                query_scales(1)
                compressed_logits(1)
                logits(0, 1)
                maxima(0, 1)
                compressed_scales(1)
                scales(0, 0)
                compressed_outputs(1)
                dve.wait_ge(n_co, 2)

                def four(i):
                    first, last = (isinstance(i, int) and i == j for j in (0, HG - 1))
                    for w in range(4):
                        two_on = (i if w < 2 else i + 1, (w + 2) % 4)
                        if not (last and w >= 2):
                            logits(*two_on)
                        if not (last and w == 3):
                            scales(i if w < 3 else i + 1, (w + 1) % 4)
                        if not (last and w >= 2):
                            maxima(*two_on)
                        if not (first and w == 0):
                            outputs(i if w else i - 1, (w - 1) % 4)

                four(0)
                with dve.Fori(1, HG - 1) as i:
                    start, steps.n = steps.n, 0
                    steps.base = i * 8 + (start - 8)
                    four(i)
                    assert steps.n == 8
                    steps.base, steps.n = 0, start + 8 * (HG - 2)
                four(HG - 1)
                outputs(HG - 1, 3)
                out_lo("o_n")

            dve.wait_ge(x_loaded, 16 * 2)
            rest_all("mix_0", xs)
            clear_sums("mix_0")
            for k in range(KD):
                dve.wait_ge(sq_ready, k + 1)
                dve.wait_ge(ssq_ready, k + 1)
                dve.tensor_tensor(ssq[:, :], ssq[:, :], ASQ[:, k * S:(k + 1) * S], ALU.add).then_inc(ssq_ready, 1)
            dve.wait_ge(loaded, 16 * 3)
            dve.wait_ge(const_ready, 3)
            norm("mix_0")
            mla()
            residual("wo_a", 1)
            norm("ffn_0")
            up("up_0")
            residual("down_0", 4)
            norm("mix_1")
            mlstm()
            residual("wo_m", 1)
            norm("ffn_1")
            up("up_1")
            residual("down_1", 4)
            norm("pre_0")
            glu("glu_0")
            residual("out_0", FF2_TILES, 0.5)
            norm("mid_0")
            conv()
            residual("cout", 1)
            norm("post_0")
            glu("glu_1")
            residual("out_1", FF2_TILES, 0.5)
            norm("kvn")
            nsa_kv()
            glu("glu_2", {0: keys, 4: keys_turned, 9: compression_bias, 15: compressed})
            residual("out_2", FF2_TILES, 0.5)
            norm("mid_1")
            nsa()
            residual("wo_n", 1)
            norm("post_1")
            glu("glu_3")
            residual("out_3", FF2_TILES, 0.5)

        @block.tensor
        def _(pe):
            def product(out_bank, lhs, k, src, first, last, hi=0):
                s, c = lhs
                chunk = k * 2 * S
                pe.matmul(bank(out_bank), w_hi[s][:, c:c + P], src[:, chunk:chunk + 2 * S], start=first, stop=False)
                return pe.matmul(bank(out_bank, 0, S), w_lo[s][:, c:c + P], src[:, chunk:chunk + S], start=False, stop=last)

            def sums(name):
                if name == "cq":
                    pe.wait_ge(sq_ready, SQ0["cq"] + 1)
                    for tb in range(TB):
                        for k in range(KQ + KKV):
                            col, first, last = (4, 0, KQ - 1) if k < KQ else (6, KQ, KQ + KKV - 1)
                            ins = pe.matmul(bank(STAT, col + tb, col + tb + 1), ASQ[:, k * S + tb * P:k * S + (tb + 1) * P], ones[:, 0:1],
                                            start=k == first, stop=k == last)
                else:
                    pe.wait_ge(ssq_ready, SSQ0[name] + KD + 1)
                    if name == "mix_0":
                        pe.wait_ge(const_ready, 3)
                    if name in TO_ROWS:
                        ins = pe.matmul(bank(RB, 0, S), ones[:, :], ssq[:, :], start=True, stop=True)
                    if name in TO_COLUMNS:
                        for tb in range(TB):
                            ins = pe.matmul(bank(STAT, tb, tb + 1), ssq[:, tb * P:(tb + 1) * P], ones[:, 0:1], start=True, stop=True)
                ins.then_inc(stat_done, 1)

            def feature(name, outs, xs_name, src=xs, norm_=None, between=None, norm_at=0):
                between = between or {}
                t0, o0 = TILE0[name], OUT0[name]

                def one(u, i=0, wait_x=False):
                    s, b = (t0 + u) % RING, (o0 + u) % 4
                    pe.wait_ge(lo_ready, i * 4 + (t0 + u + 1))
                    if not (isinstance(i, int) and o0 + u + 4 * i < 4):
                        pe.wait_ge(out_read, i * 4 + (o0 + u - 3))
                    for k in range(KD):
                        if wait_x:
                            pe.wait_ge(xs_ready, XS0[xs_name] + k + 1)
                        ins = product(b, (s, k * P), k, src, k == 0, k == KD - 1)
                    ins.then_inc(tile_done, 1)

                head = outs if outs < 16 else outs % 8 or 8
                while head <= max(between, default=0):
                    head += 8
                for u in range(head):
                    one(u, 0, u == 0)
                    if u in between:
                        between[u]()
                    if norm_ and u == norm_at:
                        sums(norm_)
                if head < outs:
                    with pe.Fori(0, (outs - head) // 8) as i:
                        for u in range(8):
                            one(head + u, i * 2)

            def residual(name, per, chunks, src, ready):
                t0, o0 = TILE0[name], OUT0[name]
                with pe.Fori(0, KD // 4) as i:
                    for u in range(4):
                        b = (o0 + u) % 4
                        pe.wait_ge(out_read, i * 4 + (o0 + u - 3))
                        for j in range(per):
                            t = t0 + u * per + j
                            pe.wait_ge(lo_ready, i * (4 * per) + (t + 1))
                            n = min(BLK, chunks - j * BLK)
                            for k in range(n):
                                c = j * BLK + k
                                if u == 0:
                                    pe.wait_ge(*ready(c))
                                ins = product(b, (t % RING, k * P), c, src, c == 0, c == chunks - 1)
                            ins.then_inc(tile_done, 1)

            def residual_one(name, src, ready, between=None):
                between = between or {}
                t0, o0 = TILE0[name], OUT0[name]

                def chunk(o, c):
                    if c == 0:
                        pe.wait_ge(out_read, o0 + o - 3)
                        pe.wait_ge(lo_ready, t0 + o + 1)
                    ins = product((o0 + o) % 4, ((t0 + o) % RING, c * P), c, src, c == 0, c == KD - 1)
                    if c == KD - 1:
                        ins.then_inc(tile_done, 1)

                for c in range(KD):
                    pe.wait_ge(*ready(c))
                    chunk(0, c)
                    if c in between:
                        between[c]()
                for o in range(1, KD):
                    for c in range(KD):
                        chunk(o, c)

            def token_major(name, groups, chunks, k0=0, xs_name=None, src=xs, norm_=None, between=None):
                t0, o0 = TILE0[name], OUT0[name]
                for n in range(groups * chunks):
                    g, c = divmod(n, chunks)
                    s, col = (t0 + n // 2) % RING, n % 2 * 512
                    pe.wait_ge(lo_ready, t0 + n // 2 + 1)
                    if c == 0:
                        pe.wait_ge(out_read, o0 + 2 * g + 1 - 3)
                    if xs_name and g == 0:
                        pe.wait_ge(xs_ready, XS0[xs_name] + k0 + c + 1)
                    for tb in range(TB):
                        x_hi, x_lo = (src[:, (k0 + c) * 2 * S + part_ * S + tb * P:][:, 0:P] for part_ in range(2))
                        out = bank((o0 + 2 * g + tb) % 4)
                        pe.matmul(out, x_hi, w_hi[s][:, col:col + 512], start=c == 0, stop=False)
                        pe.matmul(out, x_hi, w_lo[s][:, col:col + 512], start=False, stop=False)
                        ins = pe.matmul(out, x_lo, w_hi[s][:, col:col + 512], start=False, stop=c == chunks - 1)
                    if n % 2 == 1 or n == groups * chunks - 1:
                        ins.then_inc(tile_done, 1)
                    if norm_ and n == chunks // 2:
                        sums(norm_)
                    if between and n in between:
                        between[n]()

            def turn_narrow(name, width):
                pe.wait_ge(out_read, OUT0[name] + 1)
                f = fsum[OUT0[name] % 4][0:width, :]
                for tb in range(TB):
                    ins = pe.transpose(bank(7, tb * width, (tb + 1) * width), f[:, tb * P:(tb + 1) * P], const("ident", 0, width, slice(0, width)))
                return ins

            def turn_outputs(name, src, ready, chunks=range(KD)):
                pe.wait_ge(*ready)
                for k in chunks:
                    if k >= 3:
                        pe.wait_ge(xs_ready, XS0[name] + k - 2)
                    for tb in range(TB):
                        ins = pe.transpose(bank(5 + k % 3, tb * P, (tb + 1) * P), src[:, tb * D + k * P:tb * D + (k + 1) * P], ident)
                    ins.then_inc(o_turn[name], 1)

            def mla():
                feature("dq", 3, "mix_0", norm_="mix_0", norm_at=1)
                feature("dkv", 2, "mix_0")
                feature("kr", 1, "mix_0")
                pe.wait_ge(loaded, 16 * 3)
                pe.matmul(bank(6, 0, 2 * S, slice(0, H)), relb[:, :], const("onehot", 0, 2 * S, slice(0, BUCKETS + 1)), start=True, stop=True)\
                  .then_inc(row_ready, 1)
                token_major("uk", 2, KKV, KQ, "cq", os_, "cq", {0: lambda: turn_narrow("kr", ROPE).then_inc(a_rope, 1)})
                token_major("uq", 3, KQ, 0, "cq", os_)
                token_major("uv", 2, KKV, KQ, None, os_)

                def turn(i, u):
                    if u % 2 == 0:
                        pe.wait_ge(a_st, i * 2 + (u // 2 + 1))
                    if not (isinstance(i, int) and 4 * i + u < 2):
                        pe.wait_ge(a_qkT, i * 4 + (u - 1))
                    for n, src in enumerate((q_st, k_st)):
                        src = src[u // 2].rearrange("p (t h d) -> p t h d", t=TB, h=2)
                        for tb in range(TB):
                            at_ = (n * TB + tb) * P
                            ins = pe.transpose(bank(turn_bank[u % 2], at_, at_ + P, slice(0, QK)), src[:, tb, u % 2, :], ident)
                    ins.then_inc(a_turn, 1)

                def scores(i, u):
                    pe.wait_ge(a_qkT, i * 4 + (u + 1))
                    if not (isinstance(i, int) and 4 * i + u < 2):
                        pe.wait_ge(a_exp, i * 8 + 2 * (u - 1))
                    qk, b = qkT[u % 2][0:QK + TB, :], score_bank[u % 2]
                    pe.matmul(bank(b, 0, P), qk[:, 0:P], qk[:, S:S + P], start=True, stop=True)
                    pe.matmul(bank(b, P, 3 * P), qk[:, P:S], qk[:, S:2 * S], start=True, stop=True).then_inc(a_s, 1)

                def turn_probs(i, u):
                    pe.wait_ge(a_exp, i * 8 + 2 * (u + 1))
                    if not (isinstance(i, int) and 4 * i + u < 2):
                        pe.wait_ge(a_pTs, i * 4 + (u - 1))
                    for n in range(3):
                        ins = pe.transpose(bank(4 + u % 2, n * P, (n + 1) * P), prob[u % 2][:, n * P:(n + 1) * P], ident)
                    ins.then_inc(a_pT, 1)

                def values(i, u):
                    pe.wait_ge(a_pTs, i * 4 + (u + 1))
                    if not (isinstance(i, int) and 4 * i + u < 2):
                        pe.wait_ge(a_o, i * 4 + (u - 1))
                    b, pT = 6 + u % 2, probT[u % 2]
                    v = [at(v_tok, i * (4 * VD) + (tb * H * VD + u // 2 * P), P) for tb in range(TB)]
                    pe.matmul(bank(b, 0, P), pT[:, 0:P], v[0], start=True, stop=True)
                    pe.matmul(bank(b, P, 2 * P), pT[:, P:2 * P], v[0], start=True, stop=False)
                    pe.matmul(bank(b, P, 2 * P), pT[:, 2 * P:3 * P], v[1], start=False, stop=True).then_inc(a_pv, 1)

                pe.wait_ge(out_read, OUT0["uv"] + 2)
                turn(0, 0)
                turn(0, 1)
                pe.wait_ge(out_read, OUT0["uv"] + 4)
                pe.wait_ge(a_mask, 2)
                scores(0, 0)
                turn(0, 2)
                scores(0, 1)
                turn_probs(0, 0)
                heads_loop(pe, lambda i, u: ahead(turn, i, u, 3), lambda i, u: ahead(scores, i, u, 2), values,
                           lambda i, u: ahead(turn_probs, i, u, 1))
                turn_outputs("o_a", o_tok, (a_o, H), range(3))

            def mlstm():
                def turn_rows():
                    pe.wait_ge(m_rows, 1)
                    for n, src in enumerate((m_a, m_nm)):
                        for tb in range(TB):
                            col = (n * TB + tb) * MH
                            ins = pe.transpose(bank(7, col, col + MH), src[:, tb * P:(tb + 1) * P], con[0:MH, CONST["ident"]:CONST["ident"] + MH])
                    ins.then_inc(m_at, 1)

                def scores(h):
                    if h >= 2:
                        pe.wait_ge(m_logw, h - 1)
                    pe.matmul(bank(4 + h % 2, 0, S), const("select", h * P, (h + 1) * P, slice(0, MH)), m_ng, start=True, stop=True)\
                      .then_inc(m_bcd, 1)
                    if h == 1:
                        pe.wait_ge(m_cols, 1)
                    if h >= 2:
                        pe.wait_ge(m_ptd, h - 1)
                    q, k = (m_qk[:, (n * MH + h) * S:(n * MH + h + 1) * S] for n in range(2))
                    pe.matmul(bank(6 + h % 2, 0, S), k[:, 0:P], q, start=True, stop=True)
                    pe.matmul(bank(6 + h % 2, S, S + P), k[:, P:S], q[:, P:S], start=True, stop=True).then_inc(m_st, 1)

                def numerators(h):
                    if h == 0:
                        pe.wait_ge(m_one_, 1)
                        pe.wait_ge(m_ptd, MH)
                    else:
                        pe.wait_ge(m_hd, max(h - 1, 1))
                    pe.wait_ge(out_read, OUT0["mv"] + (2 if h < 2 else 4))
                    b, w = 4 + 2 * (h % 2), m_w[h]
                    v = [m_v[:, (tb * MH + h) * (MV + 1):(tb * MH + h + 1) * (MV + 1)] for tb in range(TB)]
                    pe.matmul(bank(b, 0, MV + 1), w[:, 0:P], v[0], start=True, stop=True)
                    pe.matmul(bank(b + 1, 0, MV + 1), w[:, P:2 * P], v[0], start=True, stop=False)
                    pe.matmul(bank(b + 1, 0, MV + 1), w[:, 2 * P:3 * P], v[1], start=False, stop=True).then_inc(m_num, 1)

                feature("mgate", 2, "mix_1", norm_="mix_1")
                feature("mqk", 8, "mix_1")
                token_major("mv", 2, KD, between={2: turn_rows, 3: lambda: scores(0), 5: lambda: scores(1), 7: lambda: scores(2),
                                                  9: lambda: scores(3)})
                token_major("mo", 2, KD, between={1: lambda: numerators(0), 2: lambda: numerators(1), 4: lambda: numerators(2),
                                                  5: lambda: numerators(3), 13: lambda: turn_outputs("o_m", m_h, (m_gated, 1), range(3)),
                                                  14: lambda: turn_outputs("o_m", m_h, (m_gated, 1), [3])})

            def nsa_kv():
                token_major("kv", 2, KD, 0, "kvn", xs, "kvn")
                feature("kvc", 8, "kvn")

            def keys_turned():
                pe.wait_ge(c_kn, 1)
                for b in range(4):
                    for tb in range(TB):
                        ins = pe.transpose(bank(6 + b // 2, b % 2 * S + tb * P, b % 2 * S + (tb + 1) * P),
                                           kn_tok[:, tb * 512 + b * P:tb * 512 + (b + 1) * P], ident)
                ins.then_inc(c_kt, 1)

            def compress():
                pe.wait_ge(c_loaded, 16 * 4)
                pe.wait_ge(scaled, half0["kvc"] + 8)
                for j in range(2):
                    for n in range(CBLOCK // 2):
                        w = w1c[j][:, n * P:(n + 1) * P]
                        blk = c_dup[j].rearrange("p (g s) -> p g s", g=G + 1)[:, :, 2 * n:2 * n + CSTRIDE * (NC - 1) + 1:CSTRIDE]
                        ins = pe.matmul(bank(4, j * P, j * P + (G + 1) * NC), w, blk, start=n == 0, stop=n == CBLOCK // 2 - 1)
                ins.then_inc(c_hd, 1)

            def compressed():
                pe.wait_ge(c_gelu, 1)
                pe.wait_ge(c_kT, 2)
                pe.matmul(bank(6, 0, G * NC), w2c[0], c_hid[0], start=True, stop=True).then_inc(c_kc, 1)
                pe.wait_ge(c_gelu, 2)
                pe.matmul(bank(7, 0, DH, slice(0, G * NC)), c_hid[1], w2c[1][:, 0:DH], start=True, stop=True).then_inc(c_vcd, 1)

            def compressed_sums():
                pe.wait_ge(c_kcsqd, 1)
                pe.matmul(bank(5, 64, 64 + G * NC), const("blockdiag", 0, P), c_kcsq, start=True, stop=True).then_inc(c_kcss, 1)

            def nsa():
                def turn_queries(g):
                    pe.wait_ge(out_read, OUT0["nq"] + 2 * g + 2)
                    if g:
                        pe.wait_ge(n_cTs, 2)
                    for j in range(4):
                        for tb in range(TB):
                            col = j % 2 * S + tb * P
                            ins = pe.transpose(bank(4 + j // 2, col, col + P), nq_tok[:, tb * D + (4 * g + j) * P:][:, 0:P], ident)
                    ins.then_inc(n_turn, 1)

                def compressed_scores(g):
                    pe.wait_ge(n_qTd, 2 * g + 2)
                    if g:
                        pe.wait_ge(n_co, 1)
                    for j in range(4):
                        for tb in range(TB):
                            at_ = (4 * g + j) * S + tb * P
                            ins = pe.matmul(bank(6, tb * P + j * 32, tb * P + j * 32 + 2 * NC), n_qTa[:, at_:at_ + P],
                                            kcT[:, j % 2 * 2 * NC:(j % 2 + 1) * 2 * NC], start=True, stop=True)
                    ins.then_inc(n_cs, 1)

                def compressed_turn(g):
                    pe.wait_ge(n_cexp, 2 * g + 2)
                    pe.wait_ge(n_qTd, 2 * g + 2)
                    for tb in range(TB):
                        for j in range(2):
                            cols = (2 * g + j) * G * NC
                            ins = pe.transpose(bank(4 + tb, j * P, (j + 1) * P, slice(0, G * NC)), n_cl[tb][:, cols:cols + G * NC], ident)
                    ins.then_inc(n_cT, 1)

                def compressed_values(g):
                    pe.wait_ge(n_cTs, 2 * g + 2)
                    for tb in range(TB):
                        for j in range(2):
                            ins = pe.matmul(bank(6 + tb, j * S, (j + 1) * S), n_cpT[:, tb * S + j * P:tb * S + (j + 1) * P], vc[:, :],
                                            start=True, stop=True)
                    ins.then_inc(n_cpv, 1)

                def scores(i, w):
                    gp, e = w // 2, w % 2
                    pe.wait_ge(n_q, i * 4 + 2 * (gp + 1))
                    if not (isinstance(i, int) and 4 * i + w < 2):
                        pe.wait_ge(n_log, i * 4 + (w - 1))
                    for br in range(2):
                        q, k = n_qT[gp][e], kT[:, (br * 2 + gp) * S:(br * 2 + gp + 1) * S]
                        pe.matmul(bank(2 * e + br, 0, P), q[:, 0:P], k[:, 0:P], start=True, stop=True)
                        ins = pe.matmul(bank(2 * e + br, P, 3 * P), q[:, P:S], k, start=True, stop=True)
                    ins.then_inc(n_s, 1)

                def turn_probs(i, w):
                    pe.wait_ge(n_pg, i * 4 + (w + 1))
                    first = isinstance(i, int) and 4 * i + w == 0
                    for br in range(2):
                        if first:
                            pe.wait_ge(n_cTs, 4)
                        else:
                            pe.wait_ge(n_pTd, i * 8 + (2 * w + br - 1))
                        for n in range(3):
                            col = br * 384 + n * P
                            ins = pe.transpose(bank(4 + br, n * P, (n + 1) * P), n_p[w % 2][:, col:col + P], ident)
                        ins.then_inc(n_pT, 1)

                def values(i, w):
                    pe.wait_ge(n_pTd, i * 8 + 2 * (w + 1))
                    if isinstance(i, int) and 4 * i + w < 2:
                        pe.wait_ge(n_co, 2)
                    else:
                        pe.wait_ge(n_od, i * 4 + (w - 1))
                    b = 6 + w % 2
                    for blocks in (((0, 0, 0),), ((1, 1, 0), (1, 2, 1))):
                        steps_ = [(br, *block) for br in range(2) for block in blocks]
                        for n, (br, tb, at_, sb) in enumerate(steps_):
                            ins = pe.matmul(bank(b, tb * P, (tb + 1) * P), n_pTs[w % 2][:, br * 384 + at_ * P:br * 384 + (at_ + 1) * P],
                                            vtok[:, sb * 512 + br * S + w // 2 * P:][:, 0:P], start=n == 0, stop=n == len(steps_) - 1)
                    ins.then_inc(n_pv, 1)

                feature("ngate", 1, "mid_1", norm_="mid_1")
                pe.wait_ge(c_end, 2)
                token_major("nq", 2, KD, between={3: lambda: turn_narrow("ngate", 3 * H).then_inc(n_gturn, 1),
                                                  9: lambda: turn_queries(0), 11: lambda: compressed_scores(0),
                                                  13: lambda: compressed_turn(0), 15: lambda: compressed_values(0)})
                turn_queries(1)
                pe.wait_ge(out_read, OUT0["nq"] + 4)
                scores(0, 0)
                scores(0, 1)
                compressed_scores(1)
                compressed_turn(1)
                scores(0, 2)
                compressed_values(1)

                def four(i):
                    first, last = (isinstance(i, int) and i == j for j in (0, HG - 1))
                    for w in range(4):
                        if not (last and w >= 1):
                            scores(i if w < 1 else i + 1, (w + 3) % 4)
                        if not (first and w == 0):
                            values(i if w else i - 1, (w - 1) % 4)
                        turn_probs(i, w)

                four(0)
                with pe.Fori(1, HG - 1) as i:
                    four(i)
                four(HG - 1)
                values(HG - 1, 3)
                turn_outputs("o_n", no_tok, (n_od, H), range(3))

            def turn_others(name, src, ready):
                return {c: lambda c=c: turn_outputs(name, src, ready, [c + 3]) for c in range(KD - 3)}

            def after(event, first):
                return lambda c: (event, first + c + 1)

            mla()
            residual_one("wo_a", os_, after(xs_ready, XS0["o_a"]), turn_others("o_a", o_tok, (a_o, H)))
            feature("up_0", FF1, "ffn_0", norm_="ffn_0")
            residual("down_0", FF1 // BLK, FF1, hs, after(hs_ready, hid0["up_0"]))
            mlstm()
            residual_one("wo_m", os_, after(xs_ready, XS0["o_m"]),
                         {3: lambda: turn_outputs("o_m", m_h, (m_gated, 2), [4, 5, 6]),
                          4: lambda: turn_outputs("o_m", m_h, (m_gated, 2), [7])})
            feature("up_1", FF1, "ffn_1", norm_="ffn_1")
            residual("down_1", FF1 // BLK, FF1, hs, after(hs_ready, hid0["up_1"]))
            feature("glu_0", 2 * FF2, "pre_0", norm_="pre_0")
            residual("out_0", FF2_TILES, FF2, hs, after(hs_ready, hid0["glu_0"]))
            feature("cin", 3 * KD, "mid_0", norm_="mid_0")
            residual_one("cout", hs, after(hs_ready, hid0["cin"]))
            feature("glu_1", 2 * FF2, "post_0", norm_="post_0")
            residual("out_1", FF2_TILES, FF2, hs, after(hs_ready, hid0["glu_1"]))
            nsa_kv()
            feature("glu_2", 2 * FF2, "pre_1", os_, between={3: keys_turned, 8: compress, 11: compressed, 13: compressed_sums})
            residual("out_2", FF2_TILES, FF2, hs, after(hs_ready, hid0["glu_2"]))
            nsa()
            residual_one("wo_n", os_, after(xs_ready, XS0["o_n"]), turn_others("o_n", no_tok, (n_od, H)))
            feature("glu_3", 2 * FF2, "post_1", norm_="post_1")
            residual("out_3", FF2_TILES, FF2, hs, after(hs_ready, hid0["glu_3"]))


def feature_tiles(w):
    k, m = w.shape[0] // P, w.shape[1] // P
    per = -(-k // BLK)
    out = np.zeros((m, P, per * BLK, P), np.float32)
    out[:, :, :k] = w.reshape(k, P, m, P).transpose(2, 1, 0, 3)
    return out.reshape(m, P, per, TILE).transpose(0, 2, 1, 3).reshape(m * per, P, TILE)


def token_tiles(w):
    k, g = w.shape[0] // P, w.shape[1] // 512
    out = np.zeros((-(-k * g // 2) * 2, P, 512), np.float32)
    out[:k * g] = w.reshape(k, P, g, 512).transpose(2, 0, 1, 3).reshape(k * g, P, 512)
    return out.reshape(-1, 2, P, 512).transpose(0, 2, 1, 3).reshape(-1, P, TILE)


def narrow_tile(w):
    out = np.zeros((P, KD, P), np.float32)
    out[:, :, :w.shape[1]] = w.reshape(KD, P, -1).transpose(1, 0, 2)
    return out.reshape(1, P, TILE)


def interleave(*ws):
    k = ws[0].shape[0]
    return np.stack([w.reshape(k, -1, P) for w in ws], axis=2).reshape(k, -1)


_OUT = ((D, S), "float32")


def kernel(**inputs):
    import concourse.bacc as bacc
    from concourse.bass_utils import run_bass_kernel_spmd

    a = {n: np.asarray(v) for n, v in inputs.items()}
    heads = np.array([g * HG + hg for hg in range(HG) for g in range(G)])
    w_ukv = a["mla_w_ukv"][0].reshape(KV_RANK, H, NOPE + VD)
    w_dkv = a["mla_w_dkv"][0]
    m_in, w_if = a["mlstm_w_in"][0], a["mlstm_w_if"][0]
    mqk = 2 * MH * MQK
    kv = a["w_kv_2"].reshape(D, 3, 2, G, DH)
    wq = a["attn_w_q_2"][0]
    glu, out, mlp1, mlp2 = {}, {}, a["ffn_w1"], a["ffn_w2"]
    for n, (which, layer) in enumerate((("ffn1", 0), ("ffn2", 0), ("ffn1", 1), ("ffn2", 1))):
        w = a[f"{which}_w_in_2"][layer]
        glu[n] = feature_tiles(interleave(w[:, :FF2 * P], w[:, FF2 * P:]))
        out[n] = feature_tiles(a[f"{which}_w_out_2"][layer])
    w_cin = a["conv_w_in_2"][0]
    stream = [
        feature_tiles(a["mla_w_dq"][0]), feature_tiles(w_dkv[:, :KV_RANK]), narrow_tile(w_dkv[:, KV_RANK:]),
        token_tiles(w_ukv[:, :, :NOPE].reshape(KV_RANK, -1)), token_tiles(a["mla_w_uq"][0]),
        token_tiles(w_ukv[:, :, NOPE:].reshape(KV_RANK, -1)), feature_tiles(a["mla_w_o"][0]),
        feature_tiles(mlp1[0]), feature_tiles(mlp2[0]),
        narrow_tile(w_if[:, :MH]), narrow_tile(w_if[:, MH:]), feature_tiles(m_in[:, :mqk]),
        token_tiles(m_in[:, mqk:mqk + MH * MV]), token_tiles(m_in[:, mqk + MH * MV:]), feature_tiles(a["mlstm_w_o"][0]),
        feature_tiles(mlp1[1]), feature_tiles(mlp2[1]),
        glu[0], out[0], feature_tiles(interleave(w_cin[:, D:2 * D], w_cin[:, 2 * D:], w_cin[:, :D])),
        feature_tiles(a["conv_w_out_2"][0]), glu[1], out[1],
        token_tiles(kv[:, 1:, :, :, :].transpose(0, 2, 1, 3, 4).reshape(D, -1)),
        feature_tiles(np.stack([kv[:, 0], kv[:, 0]], axis=3).reshape(D, -1)), glu[2], out[2],
        narrow_tile(wq[:, H * DH:].reshape(D, H, 3)[:, heads].reshape(D, -1)),
        token_tiles(wq[:, :H * DH].reshape(D, H, DH)[:, heads].reshape(D, -1)),
        feature_tiles(a["attn_w_o_2"][0].reshape(H, DH, D)[heads].reshape(D, D)), glu[3], out[3],
    ]
    tiles = np.concatenate(stream)
    assert tiles.shape[0] == N_TILES

    vecs = np.zeros((P, N_VEC), np.float32)

    def put(name, v):
        v = v.reshape(-1, min(P, v.shape[-1])).T
        vecs[:v.shape[0], VEC[name]:VEC[name] + v.shape[1]] = v

    for name, v in (("mix_0", a["norm_mix"][0]), ("ffn_0", a["norm_ffn"][0]), ("mix_1", a["norm_mix"][1]), ("ffn_1", a["norm_ffn"][1]),
                    ("pre_0", a["ffn1_norm_2"][0]), ("mid_0", a["mix_norm_2"][0]), ("post_0", a["ffn2_norm_2"][0]),
                    ("kvn", a["kv_norm_2"]), ("pre_1", a["ffn1_norm_2"][1]), ("mid_1", a["mix_norm_2"][1]),
                    ("post_1", a["ffn2_norm_2"][1]), ("q_norm", a["mla_q_norm"][0]), ("kv_norm", a["mla_kv_norm"][0]),
                    ("head_norm", a["mlstm_head_norm"][0]), ("taps", a["conv_w_2"][0].reshape(-1)),
                    ("kc_norm", np.concatenate([a["k_norm_2"][0]] * 2)),
                    ("nq_norm", np.concatenate([a["attn_q_norm_2"][0]] * 2)), ("b_i", a["mlstm_b_if"][0][:MH]),
                    ("b_f", a["mlstm_b_if"][0][MH:]), ("pe_k", a["cmp_pe_k_2"].reshape(-1)), ("pe_v", a["cmp_pe_v_2"].reshape(-1))):
        put(name, v)
    rows = np.concatenate([a["mla_q_gain"][0], a["mla_k_gain"][0], a["attn_q_norm_2"][0], a["k_norm_2"][1], a["k_norm_2"][2]])
    w2 = [np.concatenate([a[n]] * 2, axis=1) for n in ("cmp_w2_k_2", "cmp_w2_v_2")]
    arrays = {
        "x_in": np.ascontiguousarray(a["x"][0].T), "tiles": tiles, "vecs": vecs, "rows": rows, "consts": constants(),
        "rel_bias": np.ascontiguousarray(a["rel_bias_2"][:, heads]), "w1c_k": a["cmp_w1_k_2"], "w1c_v": a["cmp_w1_v_2"],
        "w2c_k": w2[0], "w2c_v": w2[1],
    }
    nc = bacc.Bacc("TRN2", target_bir_lowering=False, num_devices=1)
    args = [nc.dram_tensor(n, v.shape, mybir.dt.from_np(v.dtype), kind="ExternalInput").ap() for n, v in arrays.items()]
    y = nc.dram_tensor("y_out", _OUT[0], F32, kind="ExternalOutput").ap()
    build(nc, *args, y)
    r = run_bass_kernel_spmd(nc, [arrays], core_ids=[0])
    return np.ascontiguousarray(r.results[0]["y_out"].T)[None]
```
